# Optimizing a Trainium2 kernel written in Bass

```python
import math
import jax
import jax.numpy as jnp
from jax import lax
import numpy as np

D_MODEL = 1024
BATCH = 1
SEQ = 512
DEPTH = 2
DEC_BATCH = 8
DEC_SEQ = 4
PAST_LEN = 256
PAGE_SIZE = 128

N_A_LAYERS = DEPTH // 2
N_B_LAYERS = DEPTH - N_A_LAYERS
RET_HEADS = 6
RET_DK = 128
RET_DV = 128
RET_W = RET_HEADS * RET_DV
RET_CHUNK = 128
ROPE_BASE = 10000.0
FOX_HEADS = 12
FOX_HD = 64
FOX_W = FOX_HEADS * FOX_HD
FOX_QBLOCK = 128
FORGET_BIAS = 3.0
MEM_LEN = 256
MEM_HEADS = 4
MEM_HD = 64
MEM_W = MEM_HEADS * MEM_HD
MIX_W = RET_W + MEM_W
IN_A_W = 4 * RET_W + MEM_W
IN_B_W = FOX_W + MEM_W
KV_SHARED_W = 2 * FOX_W + FOX_HEADS
N_GROUPS = 4
EXPERTS_PER_GROUP = 8
TOP_K_IN_GROUP = 2
D_EXPERT = 256
DEEPNORM_ALPHA = (2 * DEPTH) ** 0.25
DEEPNORM_BETA = (8 * DEPTH) ** -0.25
LN_EPS = 1e-5
HEAD_NORM_EPS = 1e-6

kernel_name = 'yoco_retention_fox_hmoe_step'

F32 = jnp.float32

def layer_norm(x, g, b):
    xf = x.astype(F32)
    mu = jnp.mean(xf, axis=-1, keepdims=True)
    var = jnp.mean(jnp.square(xf - mu), axis=-1, keepdims=True)
    return ((xf - mu) * lax.rsqrt(var + LN_EPS) * g.astype(F32) + b.astype(F32)).astype(x.dtype)

def head_norm(r):
    mu = jnp.mean(r, axis=-1, keepdims=True)
    var = jnp.mean(jnp.square(r - mu), axis=-1, keepdims=True)
    return (r - mu) * lax.rsqrt(var + HEAD_NORM_EPS)

def rotary(x, pos):
    half = x.shape[-1] // 2
    inv_freq = ROPE_BASE ** (-jnp.arange(half, dtype=F32) / half)
    ang = pos.astype(F32)[:, None] * inv_freq[None, :]
    cos = jnp.cos(ang)[None, :, None, :]
    sin = jnp.sin(ang)[None, :, None, :]
    xf = x.astype(F32)
    x1, x2 = xf[..., :half], xf[..., half:]
    return jnp.concatenate([x1 * cos - x2 * sin, x1 * sin + x2 * cos], axis=-1).astype(x.dtype)

def retention(q, k, v, s0, log_gamma):
    B, L, H, DK = q.shape
    DV = v.shape[-1]
    C = math.gcd(L, RET_CHUNK)
    n = L // C
    qc = q.astype(F32).reshape(B, n, C, H, DK)
    kc = k.astype(F32).reshape(B, n, C, H, DK)
    vc = v.astype(F32).reshape(B, n, C, H, DV)
    i = jnp.arange(C, dtype=F32)
    diff = i[:, None] - i[None, :]
    intra_decay = jnp.where(diff >= 0, jnp.exp(log_gamma[:, None, None] * jnp.maximum(diff, 0.0)[None]), 0.0)
    scores = jnp.einsum('bnihd,bnjhd->bnhij', qc, kc) * intra_decay
    intra = jnp.einsum('bnhij,bnjhe->bnihe', scores, vc)
    k_decay = jnp.exp(log_gamma[None, :] * (C - 1 - i)[:, None])
    kv = jnp.einsum('bnjhd,bnjhe->nbhde', kc * k_decay[None, None, :, :, None], vc)
    chunk_decay = jnp.exp(log_gamma * C)[None, :, None, None]

    def step(s, kv_n):
        return chunk_decay * s + kv_n, s

    s_final, s_prev = lax.scan(step, s0.astype(F32), kv)
    q_decay = jnp.exp(log_gamma[None, :] * (i + 1.0)[:, None])
    cross = jnp.einsum('bnihd,nbhde->bnihe', qc * q_decay[None, None, :, :, None], s_prev)
    return (intra + cross).reshape(B, L, H, DV), s_final

def forgetting_attention(q, k, v, c_q, c_k, q_pos, k_pos):
    B, Lq, H, hd = q.shape
    QB = math.gcd(Lq, FOX_QBLOCK)
    nb = Lq // QB
    scale = hd ** -0.5
    qb = q.reshape(B, nb, QB, H, hd).swapaxes(0, 1)
    cqb = c_q.reshape(B, nb, QB, H).swapaxes(0, 1)
    pqb = q_pos.reshape(nb, QB)
    ck = jnp.transpose(c_k, (0, 2, 1))

    def block(args):
        qi, ci, pi = args
        logits = jnp.einsum('bqhd,bkhd->bhqk', qi, k).astype(F32) * scale
        logits = logits + jnp.transpose(ci, (0, 2, 1))[..., None] - ck[:, :, None, :]
        logits = jnp.where(k_pos[None, :] <= pi[:, None], logits, -jnp.inf)
        p = jax.nn.softmax(logits, axis=-1).astype(v.dtype)
        return jnp.einsum('bhqk,bkhd->bqhd', p, v)

    out = lax.map(block, (qb, cqb, pqb))
    return out.swapaxes(0, 1).reshape(B, Lq, H, hd)

def memory_attention(q, mk, mv):
    logits = jnp.einsum('blhd,bmhd->bhlm', q, mk).astype(F32) * (q.shape[-1] ** -0.5)
    p = jax.nn.softmax(logits, axis=-1).astype(mv.dtype)
    return jnp.einsum('bhlm,bmhd->blhd', p, mv)

def hierarchical_moe(x, w_group, b_group, w_route, b_route, w_up, w_down):
    B, L, D = x.shape
    t = x.reshape(B * L, D)
    g_logits = (t @ w_group).astype(F32) + b_group.astype(F32)
    g_idx = jnp.argmax(g_logits, axis=-1)
    g_w = jnp.take_along_axis(jax.nn.softmax(g_logits, axis=-1), g_idx[:, None], axis=-1)
    e_logits = jnp.einsum('td,gde->tge', t, w_route).astype(F32) + b_route.astype(F32)
    e_sel = jnp.take_along_axis(e_logits, g_idx[:, None, None], axis=1)[:, 0]
    top_v, top_i = lax.top_k(e_sel, TOP_K_IN_GROUP)
    top_w = jax.nn.softmax(top_v, axis=-1) * g_w
    e_w = jnp.sum(jax.nn.one_hot(top_i, EXPERTS_PER_GROUP, dtype=F32) * top_w[..., None], axis=1)
    comb = (jax.nn.one_hot(g_idx, N_GROUPS, dtype=F32)[:, :, None] * e_w[:, None, :]).astype(x.dtype)
    out = jnp.zeros_like(t)
    for g in range(N_GROUPS):
        up = jnp.einsum('td,edf->tef', t, w_up[g])
        gate, val = jnp.split(up, 2, axis=-1)
        hid = jax.nn.silu(gate) * val * comb[:, g, :, None]
        out = out + jnp.einsum('tef,efd->td', hid, w_down[g])
    return out.reshape(B, L, D)

def gather_pages(cache, page_table):
    g = cache[page_table]
    return g.reshape((page_table.shape[0], page_table.shape[1] * cache.shape[1]) + cache.shape[2:])

def trunk(x, ret_s0, mem_k, mem_v, past_k, past_v, past_logf,
          w_in_a, w_in_b, w_kv_shared, b_forget, w_o,
          ln1_g, ln1_b, ln2_g, ln2_b, w_group, b_group, w_route, b_route, w_up, w_down):
    B, L, _ = x.shape
    P = past_k.shape[1]
    pos = P + jnp.arange(L)
    log_gamma = jnp.log(1.0 - 2.0 ** (-5.0 - jnp.arange(RET_HEADS, dtype=F32)))
    new_ret = []
    for l in range(DEPTH):
        if l < N_A_LAYERS:
            h = x @ w_in_a[l]
            q, k, v, g, mq = jnp.split(h, [RET_W, 2 * RET_W, 3 * RET_W, 4 * RET_W], axis=-1)
            q = rotary(q.reshape(B, L, RET_HEADS, RET_DK), pos)
            k = rotary(k.reshape(B, L, RET_HEADS, RET_DK), pos) * (RET_DK ** -0.5)
            r, s_new = retention(q, k, v.reshape(B, L, RET_HEADS, RET_DV), ret_s0[l], log_gamma)
            new_ret.append(s_new.astype(x.dtype))
            tok = head_norm(r).astype(x.dtype).reshape(B, L, RET_W) * jax.nn.silu(g)
        else:
            if l == N_A_LAYERS:
                kvf = x @ w_kv_shared
                k_new, v_new, f_logit = jnp.split(kvf, [FOX_W, 2 * FOX_W], axis=-1)
                k_new = k_new.reshape(B, L, FOX_HEADS, FOX_HD)
                v_new = v_new.reshape(B, L, FOX_HEADS, FOX_HD)
                logf_new = jax.nn.log_sigmoid(f_logit.astype(F32) + b_forget.astype(F32))
                k_all = jnp.concatenate([past_k, k_new.astype(past_k.dtype)], axis=1)
                v_all = jnp.concatenate([past_v, v_new.astype(past_v.dtype)], axis=1)
                c_all = jnp.cumsum(jnp.concatenate([past_logf.astype(F32), logf_new], axis=1), axis=1)
                c_q = c_all[:, P:]
                k_pos = jnp.arange(P + L)
            h = x @ w_in_b[l - N_A_LAYERS]
            fq, mq = jnp.split(h, [FOX_W], axis=-1)
            tok = forgetting_attention(fq.reshape(B, L, FOX_HEADS, FOX_HD), k_all, v_all,
                                       c_q, c_all, pos, k_pos).reshape(B, L, FOX_W).astype(x.dtype)
        mem_out = memory_attention(mq.reshape(B, L, MEM_HEADS, MEM_HD), mem_k[l], mem_v[l]).reshape(B, L, MEM_W)
        mixed = jnp.concatenate([tok, mem_out.astype(x.dtype)], axis=-1) @ w_o[l]
        x = layer_norm(DEEPNORM_ALPHA * x + mixed, ln1_g[l], ln1_b[l])
        ffn = hierarchical_moe(x, w_group[l], b_group[l], w_route[l], b_route[l], w_up[l], w_down[l])
        x = layer_norm(DEEPNORM_ALPHA * x + ffn, ln2_g[l], ln2_b[l])
    return x, jnp.stack(new_ret), k_new, v_new, logf_new.astype(x.dtype)

def setup_inputs(seed: int = 0) -> dict:
    key = jax.random.key(seed)
    ks = jax.random.split(key, 32)
    n_pages = PAST_LEN // PAGE_SIZE
    n_used = DEC_BATCH * n_pages
    n_phys = n_used + max(1, n_used // 4)

    def nrm(k, shape, s):
        return jax.random.normal(k, shape, F32) * s

    s_d = D_MODEL ** -0.5
    x_prompt = nrm(ks[0], (BATCH, SEQ, D_MODEL), 1.0)
    x_sample = nrm(ks[1], (DEC_BATCH, DEC_SEQ, D_MODEL), 1.0)
    mem_prompt = nrm(ks[2], (BATCH, MEM_LEN, D_MODEL), 1.0)
    state_ret = nrm(ks[3], (N_A_LAYERS, DEC_BATCH, RET_HEADS, RET_DK, RET_DV), 0.1)
    cache_fox_k = nrm(ks[4], (n_phys, PAGE_SIZE, FOX_HEADS, FOX_HD), 1.0)
    cache_fox_v = nrm(ks[5], (n_phys, PAGE_SIZE, FOX_HEADS, FOX_HD), DEEPNORM_BETA)
    cache_fox_logf = jax.nn.log_sigmoid(FORGET_BIAS + nrm(ks[6], (n_phys, PAGE_SIZE, FOX_HEADS), 1.0))
    cache_mem_k = nrm(ks[7], (DEPTH, DEC_BATCH, MEM_LEN, MEM_HEADS, MEM_HD), 1.0)
    cache_mem_v = nrm(ks[8], (DEPTH, DEC_BATCH, MEM_LEN, MEM_HEADS, MEM_HD), DEEPNORM_BETA)
    page_table = jax.random.permutation(ks[9], n_phys)[:n_used].reshape(DEC_BATCH, n_pages).astype(jnp.int32)
    w_in_a = nrm(ks[10], (N_A_LAYERS, D_MODEL, IN_A_W), s_d).at[:, :, 2 * RET_W:3 * RET_W].multiply(DEEPNORM_BETA)
    w_in_b = nrm(ks[11], (N_B_LAYERS, D_MODEL, IN_B_W), s_d)
    w_kv_shared = nrm(ks[12], (D_MODEL, KV_SHARED_W), s_d).at[:, FOX_W:2 * FOX_W].multiply(DEEPNORM_BETA)
    b_forget = FORGET_BIAS + nrm(ks[13], (FOX_HEADS,), 0.1)
    w_o = nrm(ks[14], (DEPTH, MIX_W, D_MODEL), MIX_W ** -0.5 * DEEPNORM_BETA)
    w_mem_kv = nrm(ks[15], (DEPTH, D_MODEL, 2 * MEM_W), s_d).at[:, :, MEM_W:].multiply(DEEPNORM_BETA)
    ln1_g = 1.0 + nrm(ks[16], (DEPTH, D_MODEL), 0.01)
    ln1_b = nrm(ks[17], (DEPTH, D_MODEL), 0.01)
    ln2_g = 1.0 + nrm(ks[18], (DEPTH, D_MODEL), 0.01)
    ln2_b = nrm(ks[19], (DEPTH, D_MODEL), 0.01)
    w_group = nrm(ks[20], (DEPTH, D_MODEL, N_GROUPS), s_d)
    b_group = nrm(ks[21], (DEPTH, N_GROUPS), 0.01)
    w_route = nrm(ks[22], (DEPTH, N_GROUPS, D_MODEL, EXPERTS_PER_GROUP), s_d)
    b_route = nrm(ks[23], (DEPTH, N_GROUPS, EXPERTS_PER_GROUP), 0.01)
    w_up = nrm(ks[24], (DEPTH, N_GROUPS, EXPERTS_PER_GROUP, D_MODEL, 2 * D_EXPERT), s_d)
    w_down = nrm(ks[25], (DEPTH, N_GROUPS, EXPERTS_PER_GROUP, D_EXPERT, D_MODEL), D_EXPERT ** -0.5 * DEEPNORM_BETA)
    return {'x_prompt': x_prompt, 'x_sample': x_sample, 'mem_prompt': mem_prompt,
            'state_ret': state_ret, 'cache_fox_k': cache_fox_k, 'cache_fox_v': cache_fox_v,
            'cache_fox_logf': cache_fox_logf, 'cache_mem_k': cache_mem_k, 'cache_mem_v': cache_mem_v,
            'page_table': page_table, 'w_in_a': w_in_a, 'w_in_b': w_in_b, 'w_kv_shared': w_kv_shared,
            'b_forget': b_forget, 'w_o': w_o, 'w_mem_kv': w_mem_kv, 'ln1_g': ln1_g, 'ln1_b': ln1_b,
            'ln2_g': ln2_g, 'ln2_b': ln2_b, 'w_group': w_group, 'b_group': b_group,
            'w_route': w_route, 'b_route': b_route, 'w_up': w_up, 'w_down': w_down}

def reference(x_prompt, x_sample, mem_prompt, state_ret, cache_fox_k, cache_fox_v, cache_fox_logf,
              cache_mem_k, cache_mem_v, page_table, w_in_a, w_in_b, w_kv_shared, b_forget, w_o,
              w_mem_kv, ln1_g, ln1_b, ln2_g, ln2_b, w_group, b_group, w_route, b_route, w_up, w_down):
    bp = x_prompt.shape[0]
    dt = x_prompt.dtype
    mem_kv = jnp.einsum('bmd,ldf->lbmf', mem_prompt, w_mem_kv).reshape(DEPTH, bp, MEM_LEN, 2, MEM_HEADS, MEM_HD)
    mem_k_prompt = mem_kv[:, :, :, 0]
    mem_v_prompt = mem_kv[:, :, :, 1]
    y_prompt, ret_state_prompt, fox_k_prompt, fox_v_prompt, fox_logf_prompt = trunk(
        x_prompt, jnp.zeros((N_A_LAYERS, bp, RET_HEADS, RET_DK, RET_DV), dt), mem_k_prompt, mem_v_prompt,
        jnp.zeros((bp, 0, FOX_HEADS, FOX_HD), dt), jnp.zeros((bp, 0, FOX_HEADS, FOX_HD), dt),
        jnp.zeros((bp, 0, FOX_HEADS), dt),
        w_in_a, w_in_b, w_kv_shared, b_forget, w_o, ln1_g, ln1_b, ln2_g, ln2_b,
        w_group, b_group, w_route, b_route, w_up, w_down)
    past_k = gather_pages(cache_fox_k, page_table)
    past_v = gather_pages(cache_fox_v, page_table)
    past_logf = gather_pages(cache_fox_logf, page_table)
    y_sample, ret_state_sample, fox_k_sample, fox_v_sample, fox_logf_sample = trunk(
        x_sample, state_ret, cache_mem_k, cache_mem_v, past_k, past_v, past_logf,
        w_in_a, w_in_b, w_kv_shared, b_forget, w_o, ln1_g, ln1_b, ln2_g, ln2_b,
        w_group, b_group, w_route, b_route, w_up, w_down)
    return (y_prompt, y_sample, ret_state_prompt, ret_state_sample,
            fox_k_prompt, fox_v_prompt, fox_logf_prompt,
            fox_k_sample, fox_v_sample, fox_logf_sample,
            mem_k_prompt, mem_v_prompt)


_drawn_inputs = setup_inputs


def setup_inputs(seed=0):
    import zlib

    import numpy as np

    out = dict(_drawn_inputs(seed))
    spreads = {}
    factors = {'cache_fox_logf': 7.729,
     'cache_mem_k': 4.653,
     'cache_mem_v': 3.05,
     'ln1_g': 3.068,
     'ln1_b': 3.06,
     'ln2_g': 3.394,
     'ln2_b': 3.65,
     'b_group': 8.0,
     'b_route': 6.964}
    for name, (base, spread) in spreads.items():
        noise = np.random.default_rng([zlib.crc32(name.encode()), seed]).standard_normal(out[name].shape)
        drawn = base * np.exp(spread * noise) if base else spread * noise
        out[name] = jnp.asarray(drawn.astype(out[name].dtype))
    for name, factor in factors.items():
        out[name] = (out[name] * factor).astype(out[name].dtype)
    return out
```

```python
from contextlib import ExitStack

import numpy as np

import concourse.bass as bass
from concourse import mybir

F32 = mybir.dt.float32
I32 = mybir.dt.int32
U32 = mybir.dt.uint32
ALU = mybir.AluOpType
ACT = mybir.ActivationFunctionType
AX = mybir.AxisListType

P = 128
D = 1024
KD = D // P
SEQ, DB, DS = 512, 8, 4
NS = DB * DS
NT = SEQ // P + 1
ST = NT - 1
ROWS = [P] * ST + [NS]
TOK = SEQ + NS
LAYERS = 2
RH, RD = 6, 128
RW = RH * RD
FH, FD = 12, 64
FW = FH * FD
MH, MD, ML = 4, 64, 256
MW = MH * MD
PG, PAGE = 2, 128
NG, EG = 4, 8
NE = NG * EG
DE = 256
ALPHA = float(np.float32((2 * LAYERS) ** 0.25))
LN_EPS, HN_EPS = 1e-5, 1e-6
SLOTS = 64
PAIRS = NE // 2
MORE = 16
STEPS = [SLOTS + P * k for k in range(4)]
NEG = -1.0e30

CONST = {}
CW = 0
for _name, _w in (("ident", P), ("tri", P), ("strict", P), ("ones", P), ("iota", P), 
                  ("decay", RH * P), ("qdecay", RH * P), ("kdecay", RH), ("decay_s", RH * NS), ("qdecay_s", RH * NS),
                  ("kdecay_s", RH * DB), ("causal", P), ("causal_s", NS), ("tri_s", NS), ("batch_s", 60),
                  ("token", NT), ("valid", NT), ("steps", 4)):
    CONST[_name] = (CW, CW + _w)
    CW += _w


def shape_constants():
    f = np.float32
    c = np.zeros((P, CW), f)

    def put(name, a):
        lo, hi = CONST[name]
        a = np.asarray(a, f)
        c[:a.shape[0], lo:hi] = a.reshape(a.shape[0], hi - lo)

    i = np.arange(P)
    t = np.arange(NS)
    lg = np.log(f(1.0) - f(2.0) ** (f(-5.0) - np.arange(RH, dtype=f))).astype(f)

    def power(h, n):
        return np.exp((lg[h] * np.asarray(n, f)).astype(f)).astype(f)

    put("ident", np.eye(P))
    put("tri", i[:, None] <= i[None, :])
    put("strict", i[:, None] < i[None, :])
    put("ones", np.ones((P, P)))
    put("iota", np.tile(i, (P, 1)))
    diff = i[None, :] - i[:, None]
    put("decay", np.stack([np.where(diff >= 0, power(h, np.maximum(diff, 0)), 0) for h in range(RH)], 1))
    put("qdecay", np.stack([np.tile(power(h, i + 1), (P, 1)) for h in range(RH)], 1))
    put("kdecay", np.stack([power(h, P - 1 - i) for h in range(RH)], 1))
    same = (t[:, None] // DS) == (t[None, :] // DS)
    ds = t[None, :] - t[:, None]
    put("decay_s", np.stack([np.where(same & (ds >= 0), power(h, np.maximum(ds, 0)), 0) for h in range(RH)], 1))
    put("qdecay_s", np.stack([np.tile(power(h, t % DS + 1), (P, 1)) for h in range(RH)], 1))
    put("kdecay_s", np.stack([np.where((t[:, None] // DS) == np.arange(DB)[None, :],
                                       power(h, DS - 1 - t % DS)[:, None], 0) for h in range(RH)], 1))
    put("causal", np.where(i[None, :] <= i[:, None], 0, NEG))
    put("causal_s", np.tile(np.where(same & (ds <= 0), 0, NEG), (4, 1)))
    put("tri_s", same & (ds >= 0))
    b = np.zeros((P, 60), f)
    b[:, 28:32] = 1
    put("batch_s", b)
    put("token", i[:, None] + P * np.arange(NT)[None, :])
    put("valid", i[:, None] < np.array(ROWS)[None, :])
    put("steps", np.tile(np.array(STEPS), (P, 1)))
    pos = np.concatenate([np.arange(SEQ), PG * PAGE + t % DS]).astype(f)
    half = RD // 2
    inv = (f(10000.0) ** (-np.arange(half, dtype=f) / f(half))).astype(f)
    ang = (inv[:, None] * pos[None, :]).astype(f)
    cos, sin = np.cos(ang).astype(f), np.sin(ang).astype(f)
    ks = f(RD ** -0.5)
    cs, sn = np.concatenate([cos, cos]), np.concatenate([sin, -sin])
    rope = np.concatenate([cs, sn, cs * ks, sn * ks], axis=1).astype(f)
    return c, rope


def build(nc, x_prompt, x_sample, mem_prompt, state_ret, cache_fox_k, cache_fox_v, cache_fox_logf, cache_mem_k,
          cache_mem_v, page_table, w_in_a, w_in_b, w_kv_shared, b_forget, w_o, w_mem_kv, ln1_g, ln1_b, ln2_g, ln2_b,
          w_group, b_group, w_route, b_route, w_up, w_down, consts, rope, outs):
    (y_prompt, y_sample, ret_prompt, ret_sample, fox_k_p, fox_v_p, fox_f_p, fox_k_s, fox_v_s, fox_f_s,
     mem_k_p, mem_v_p) = outs
    ctx = ExitStack()
    sems = {}

    def S(name):
        if name not in sems:
            sems[name] = ctx.enter_context(nc.semaphore(name))
        return sems[name]

    with ctx:
        def sb(name, w, dt=F32):
            return ctx.enter_context(nc.sbuf_tensor(name, [P, w], dt))

        x_rows_t, x_cols_t, mix_t = sb("x_rows", NT * D), sb("x_cols", KD * TOK), sb("mix_cols", KD * TOK)
        const_t = sb("const", CW)
        big = sb("expert_weights", 4 * 3072)
        ring = sb("weight_ring", 3 * 3072)
        work = sb("work", 2 * NT * RW)
        mem_kv_t, mem_kt_t = sb("mem_kv", 2 * 2 * 512), sb("mem_kt", 2 * 2 * ML)
        ln_t = sb("ln_gb", 2 * D)
        small = sb("small", 1100)
        ints = sb("ints", 200, I32)
        index_t = sb("max_index", 10 * 8, U32)
        ps = ctx.enter_context(nc.psum_tensor("ps", [P, 8 * 512], F32))
        xs = [nc.dram_tensor(f"stream_rows{l}", [TOK, D], F32, kind="Internal").ap() for l in range(LAYERS)]
        ys_all = nc.dram_tensor("expert_rows", [(PAIRS + MORE) * P, D], F32, kind="Internal").ap()
        ys = [ys_all, ys_all]

        def view(t, at, *shape, rows=(0, P)):
            n = int(np.prod(shape))
            v = t[rows[0]:rows[1], at:at + n]
            if len(shape) == 2:
                v = v.rearrange("p (a b) -> p a b", a=shape[0])
            elif len(shape) == 3:
                v = v.rearrange("p (a b c) -> p a b c", a=shape[0], b=shape[1])
            return v

        def C(name, rows=P):
            lo, hi = CONST[name]
            return const_t[0:rows, lo:hi]

        def bank(b, lo=0, hi=512, rows=(0, P)):
            return ps[rows[0]:rows[1], b * 512 + lo:b * 512 + hi]

        X = view(x_rows_t, 0, NT, D)
        XT = view(x_cols_t, 0, KD, TOK)
        MX = view(mix_t, 0, KD, TOK)
        ident = C("ident")
        memkv = view(mem_kv_t, 0, 2, 2, 512)
        memkt = view(mem_kt_t, 0, 2, 2, ML)
        qT = view(big, 0, 6, TOK)
        kT = view(big, 6 * TOK, 6, TOK)
        V = view(big, 12 * TOK, NT, RW)
        free0 = 12 * TOK + NT * RW
        state_p = view(big, free0, RH, P)
        scm = view(big, free0 + 768, 2, P)
        kd = view(big, free0 + 1024, 2, P)
        qd = view(big, free0 + 1280, 2, P)
        qds = view(big, free0 + 1536, 2, NS)
        scs = view(big, free0 + 1600, 2, NS)
        kds = view(big, free0 + 1664, P)
        zeros = view(big, free0, D)
        assert free0 + 1792 <= 4 * 3072
        R = view(work, 0, NT, RW)
        G = view(work, NT * RW, NT, RW)
        rope_v = view(work, 0, 4, TOK)
        mem_rows = view(work, NT * RW, 2, D)
        ropeA = view(mix_t, 0, TOK)
        ropeB = view(mix_t, TOK, TOK)
        memT = view(mix_t, 2 * TOK, KD, ML)
        st_s = view(mix_t, 0, 2, DB * P)
        vbd = view(mix_t, 2048, DB * P)
        rTs = view(mix_t, 3072, RH, NS)
        at = [0]

        def sm(*shape):
            v = view(small, at[0], *shape)
            at[0] += int(np.prod(shape))
            assert at[0] <= 900
            return v

        stats, mv, rstd = sm(NT, 12), sm(NT, 2), sm(NT)
        hstats, hmv, hrs = sm(RH, 6), sm(NT * RH, 2), sm(NT * RH)
        mx, nmx, esum, rsum = sm(4), sm(4), sm(4), sm(4)
        logf = sm(NT, FH)
        cq, negc = sm(NT, FH), sm(NT, FH)
        fz, fe = sm(NT, FH), sm(NT, FH)
        cqs = sm(3)
        past_f = sm(PG, DB * FH)
        bf_b = sm(FH)
        biasr = sm(NG + NE)
        eps_ln, eps_hn = sm(1), sm(1)
        wslot = sm(PAIRS + MORE)
        pages = ints[:, 0:16]
        slot_tok = ints[:, 16:16 + 32]
        pos_i = ints[:, 48:58]
        lists = ints[:, 64:64 + 17]
        idx_now = ints[:, 96:97]
        ib = [ints[:, 100 + 10 * k:110 + 10 * k] for k in range(3)]

        def cols(w, lo, hi):
            return w[:, lo:hi].rearrange("(k p) n -> p k n", p=P)

        chunks = []
        for l in range(LAYERS):
            chunks += [(cols(w_mem_kv[l], 0, 256), ("mkv_mm", 4 * l + 2)),
                       (cols(w_mem_kv[l], 256, 512), ("mkv_mm", 4 * l + 4))]
        for n in range(4):
            chunks.append((cols(w_in_a[0], 384 * n, 384 * n + 384), ("rope_mm", 3 * n + 3)))
        for n in range(4):
            chunks.append((cols(w_in_a[0], 1536 + 384 * n, 1920 + 384 * n), ("tm_mm", 5 * n + 5)))
        chunks.append((cols(w_in_a[0], 3072, 3328), ("fm_mm", 2)))
        for n in range(4):
            chunks.append((cols(w_o[0], 256 * n, 256 * n + 256), ("wo_mm", 5 * n + 5)))
        for n in range(4):
            chunks.append((cols(w_kv_shared, 384 * n, 384 * n + 384), ("tm_mm", 25 + 5 * n)))
        chunks.append((cols(w_kv_shared, 1536, 1548), ("tm_mm", 45)))
        chunks.append((cols(w_in_b[0], 0, 384), ("fm_mm", 5)))
        chunks.append((cols(w_in_b[0], 384, 768), ("fm_mm", 8)))
        chunks.append((cols(w_in_b[0], 768, 1024), ("fm_mm", 10)))
        for n in range(4):
            chunks.append((cols(w_o[1], 256 * n, 256 * n + 256), ("wo_mm", 25 + 5 * n)))
        CH_KV, CH_A, CH_O, CH_S, CH_B, CH_O1 = 0, 4, 13, 17, 22, 25

        def wslot_view(n):
            w = chunks[n][0].shape[-1]
            return view(ring, 3072 * (n % 3), KD, w)

        def chunk_ready(eng, n):
            eng.wait_ge(S(f"w_in{n % 3}"), 16 * (n // 3 + 1))

        wr = view(ring, 0, KD, NG + NE)
        ROUTE_IN = 5

        WU = [view(big, 0, KD, 512), view(big, 4096, KD, 512)]
        WD = [view(big, 8192, 2, D), view(big, 8192 + 2048, 2, D)]
        xg, yb = view(work, 0, D), view(work, D, D)
        xgT = view(work, 2 * D, KD, P)
        sg = view(work, 3 * D, 2, P)
        hid = view(work, 3 * D + 256, 2, 2, SLOTS)
        sgx = view(work, 3 * D + 512, 2, P)
        hidx = view(work, 3 * D + 768, 2, P)
        yg = view(work, 4 * D + 512, 2, D)
        RB = 0
        rl = view(mix_t, RB, NT, 40)
        gm = view(mix_t, 200, NT, 8)
        em = view(mix_t, 240, NT, 8)
        esel = view(mix_t, 280, NT, 8)
        gf = view(mix_t, 320, NT)
        gexp = view(mix_t, 325, NT, NG)
        gw = view(mix_t, 345, NT)
        ohg = view(mix_t, 350, NT, NG)
        ef = view(mix_t, 370, 2, NT)
        wj = view(mix_t, 380, 2, NT)
        tmpw = view(mix_t, 390, NT)
        r10, x10, b10, s10, p10 = [view(mix_t, 400 + 10 * k, 10) for k in range(5)]
        oh = view(mix_t, 450, 10, NE)
        oh_t = view(mix_t, 770, 10, NE)
        cnt = view(mix_t, 1090, NT, NE)
        rank = view(mix_t, 1250, NT + 1, NE)
        nx, xbase = view(mix_t, 1442, NE), view(mix_t, 1474, NE)
        big_cmp = view(mix_t, 1506, NE * NE)
        a1 = view(mix_t, 2530, 10, P)
        bb = view(mix_t, 3810, 5, 64)
        assert 3810 + 320 <= KD * TOK
        bb2 = view(ring, 3072, 5, 64)
        esw = view(ring, 3392, NT * NG * EG)
        nxc = view(ring, 3600, NE * 4)
        lf = view(ring, 3800, 17)
        bt = view(ring, 3840, 10, NE)
        gi = index_t[:, :]

        mvc = view(work, 0, DB, 2 * MW)
        mkc = [view(work, 4096, 2, MW), view(work, 4608, 2, MW)]
        mkcT = view(work, 5120, 2, 2, P)
        ml_t = view(work, 5632, 2, 4, NS)
        ml_r = view(work, 5888, ML)
        mp_s = view(work, 6144, 2, P)
        mpr = view(work, 6400, 2, ML)
        mprT = view(work, 6912, 2, ML)
        k_rows = view(work, NT * RW, NT, FW)
        fnb = view(work, 0, 2, SEQ)
        fpr = view(work, 1024, 2, SEQ)
        fprT = view(work, 2048, 2, SEQ)
        fkc = [view(work, 0, FW), view(work, 768, FW)]
        fvc = [view(work, 1536, FW), view(work, 2304, FW)]
        fkT = [view(work, 3072, 6, P), view(work, 6624, 6, P)]
        fl_t = view(work, 3840, PG, FH, NS)
        FLW = PG * PAGE + NS
        fl_r = view(work, 4608, 3, FLW)
        fs_p = view(work, 5472, 3, 3, P)
        mqT = MX[:, 6:8]
        ckp = view(small, 900, PG, DB * FH)

        block = ctx.enter_context(nc.Block())

        @block.sync
        def _(sp):
            sp.dma_start(const_t[:, :], consts).then_inc(S("inputs"), 16)
            sp.dma_start(X[:, 0:ST, :], x_prompt[0].rearrange("(t p) d -> p t d", p=P)).then_inc(S("inputs"), 16)
            sp.dma_start(X[0:NS, ST, :], x_sample.rearrange("b t d -> (b t) d")).then_inc(S("inputs"), 16)
            sp.dma_start(mem_rows, mem_prompt[0].rearrange("(t p) d -> p t d", p=P)).then_inc(S("tables"), 16)
            sp.dma_start(view(work, 0, 4 * TOK), rope).then_inc(S("tables"), 16)
            sp.dma_start(bf_b, b_forget.rearrange("(a h) -> a h", a=1).partition_broadcast(P)).then_inc(S("tables"), 16)
            sp.dma_start(pages[0:1, :], page_table.rearrange("b g -> (b g)").rearrange("(a n) -> a n", a=1)) \
                .then_inc(S("tables"), 16)

            def chunk(n):
                if n >= 3:
                    sp.wait_ge(S(chunks[n - 3][1][0]), chunks[n - 3][1][1])
                sp.dma_start(wslot_view(n), chunks[n][0]).then_inc(S(f"w_in{n % 3}"), 16)

            def ln_params(p):
                if p:
                    sp.wait_ge(S("x_ready"), NT * p)
                g, b = ((ln1_g, ln1_b), (ln2_g, ln2_b))[p % 2]
                sp.dma_start(ln_t[:, 0:D], g[p // 2:p // 2 + 1, :].partition_broadcast(P)).then_inc(S("ln_in"), 16)
                sp.dma_start(ln_t[:, D:2 * D], b[p // 2:p // 2 + 1, :].partition_broadcast(P)).then_inc(S("ln_in"), 16)

            def router_weights(l):
                sp.wait_ge(S("wo_mm"), 20 * (l + 1))
                s = S("route_in")
                sp.dma_start(wr[:, :, 0:NG], w_group[l].rearrange("(k p) g -> p k g", p=P)).then_inc(s, 16)
                for g in range(NG):
                    sp.dma_start(wr[:, :, NG + EG * g:NG + EG * g + EG],
                                 w_route[l, g].rearrange("(k p) e -> p k e", p=P)).then_inc(s, 16)
                sp.dma_start(biasr[:, 0:NG], b_group[l:l + 1, :].partition_broadcast(P)).then_inc(s, 16)
                sp.dma_start(biasr[:, NG:], b_route[l:l + 1].rearrange("a g e -> a (g e)").partition_broadcast(P)) \
                    .then_inc(s, 16)

            def mem_cache(l):
                sp.wait_ge(S("tok_done"), l + 1)
                for b in range(DB):
                    if b >= 2:
                        sp.wait_ge(S("mk_tr"), 8 * l + b - 1)
                    sp.dma_start(mkc[b % 2], cache_mem_k[l, b].rearrange("(t p) h d -> p t (h d)", p=P)) \
                        .then_inc(S(f"mk_in{b % 2}"), 16)
                    sp.dma_start(mvc[:, b], cache_mem_v[l, b].rearrange("(t p) h d -> p t (h d)", p=P)) \
                        .then_inc(S("mv_in"), 16)

            def experts(l):
                s = l * PAIRS
                sp.wait_ge(S("tok_done"), l + 1)
                if l == 0:
                    sp.wait_ge(S("rs_out"), 16)
                else:
                    sp.wait_ge(S("kv_out"), 64)
                with sp.Fori(0, PAIRS) as i:
                    for j in range(2):
                        sp.wait_ge(S(f"up_free{j}"), i + (s + 1))
                        sp.dma_start(WU[j], w_up[l].rearrange("g e (k p) f -> p (g e) k f", p=P)
                                     [:, bass.ds(i * 2 + j, 1)].rearrange("p a k f -> p (a k) f")) \
                            .then_inc(S(f"up_in{j}"), 16)
                        sp.wait_ge(S(f"down_free{j}"), i + (s + 1))
                        sp.dma_start(WD[j], w_down[l].rearrange("g e (k p) f -> p (g e) k f", p=P)
                                     [:, bass.ds(i * 2 + j, 1)].rearrange("p a k f -> p (a k) f")) \
                            .then_inc(S(f"down_in{j}"), 16)
                sp.wait_ge(S("lists"), l + 1)
                more = sp.value_load(lists[0:1, 16:17], min_val=0, max_val=MORE)
                with sp.If(more > 0):
                    with sp.Fori(0, more) as x:
                        sp.wait_ge(S(f"more_step{l}"), x * 9 + 1)
                        e = sp.value_load(lists[0:1, bass.ds(x, 1)], min_val=0, max_val=NE - 1)
                        sp.dma_start(WU[0], w_up[l].rearrange("g e (k p) f -> p (g e) k f", p=P)
                                     [:, bass.ds(e, 1)].rearrange("p a k f -> p (a k) f")) \
                            .then_inc(S(f"more_w{l}"), 16)
                        sp.dma_start(WD[0], w_down[l].rearrange("g e (k p) f -> p (g e) k f", p=P)
                                     [:, bass.ds(e, 1)].rearrange("p a k f -> p (a k) f")) \
                            .then_inc(S(f"more_w{l}"), 16)

            for n in range(CH_KV, CH_O):
                chunk(n)
            ln_params(0)
            sp.wait_ge(S("rope_ev"), 12)
            sp.wait_ge(S("mkv_mm"), 8)
            for h in range(RH):
                if h >= 2:
                    sp.wait_ge(S(f"st_out{h % 2}"), 16 * (h // 2))
                sp.dma_start(st_s[:, h % 2].rearrange("p (b e) -> p b e", b=DB),
                             state_ret[0, :, h].rearrange("b d e -> d b e")).then_inc(S(f"st_in{h % 2}"), 16)
            for n in range(CH_O, CH_O + 3):
                chunk(n)
            mem_cache(0)
            chunk(CH_O + 3)
            router_weights(0)
            ln_params(1)
            experts(0)
            sp.wait_ge(S("slots"), 1)
            for n in range(CH_S, CH_O1):
                chunk(n)
            ln_params(2)
            sp.wait_ge(S("tables"), 64)
            sp.wait_ge(S("fox_p"), 48)
            sp.wait_ge(S("kv_out"), 64)
            for n in range(DB * PG):
                if n >= 2:
                    sp.wait_ge(S("fk_tr"), n - 1)
                pg = sp.value_load(pages[0:1, n:n + 1], min_val=0, max_val=cache_fox_k.shape[0] - 1)
                sp.dma_start(fkc[n % 2], cache_fox_k.rearrange("n s h d -> s n (h d)")[:, bass.ds(pg, 1)]
                             .rearrange("s a f -> s (a f)")).then_inc(S(f"fk_in{n % 2}"), 16)
            for n in range(DB * PG):
                if n >= 2:
                    sp.wait_ge(S("fs_pv"), n - 1)
                pg = sp.value_load(pages[0:1, n:n + 1], min_val=0, max_val=cache_fox_k.shape[0] - 1)
                sp.dma_start(fvc[n % 2], cache_fox_v.rearrange("n s h d -> s n (h d)")[:, bass.ds(pg, 1)]
                             .rearrange("s a f -> s (a f)")).then_inc(S(f"fv_in{n % 2}"), 16)
            for n in range(CH_O1, CH_O1 + 3):
                chunk(n)
            mem_cache(1)
            chunk(CH_O1 + 3)
            router_weights(1)
            ln_params(3)
            experts(1)

        @block.gpsimd
        def _(pool):
            def pool_chain():
                n = [0]

                def link(ins):
                    n[0] += 1
                    ins.then_inc(S("pool_c"), 1)
                    pool.wait_ge(S("pool_c"), n[0])
                return link

            link = pool_chain()

            def gains(p):
                pool.wait_ge(S("ln_in"), 32 * (p + 1))
                for i in range(NT):
                    n = ROWS[i]
                    pool.wait_ge(S("ln_nm"), NT * p + i + 1)
                    link(nc.gpsimd.tensor_tensor(X[0:n, i], X[0:n, i], ln_t[0:n, 0:D], ALU.mult))
                    nc.gpsimd.tensor_tensor(X[0:n, i], X[0:n, i], ln_t[0:n, D:], ALU.add).then_inc(S("x_ready"), 1)

            def dispatch(l):
                pool.wait_ge(S("x_ready"), NT * (2 * l + 1))
                pool.dma_start(xs[l][0:SEQ].rearrange("(t p) d -> p t d", p=P), X[:, 0:ST]).then_inc(S("xs_out"), 16)
                pool.dma_start(xs[l][SEQ:TOK], X[0:NS, ST]).then_inc(S("xs_out"), 16)
                pool.wait_ge(S("slots"), l + 1)
                pool.wait_ge(S("xs_out"), 32 * (l + 1))
                with pool.Fori(0, PAIRS + 1) as i:
                    b = l * (PAIRS + 1)
                    pool.wait_ge(S("xg_free"), i + (b + 1))
                    nc.gpsimd.tensor_copy(idx_now, slot_tok[:, bass.ds(i, 1)]).then_inc(S("idx"), 1)
                    pool.wait_ge(S("idx"), i + (b + 1))
                    pool.sem_inc(S("gathers"), 1)
                    pool.indirect_dma_start(xg, None, xs[l], bass.IndirectOffsetOnAxis(idx_now, 0)) \
                        .then_inc(S("xg_in"), 16)
                    pool.wait_ge(S("xg_in"), i * 16 + (16 * b + 16))
                more = pool.value_load(lists[0:1, 16:17], min_val=0, max_val=MORE)
                with pool.If(more > 0):
                    with pool.Fori(0, more) as x:
                        pool.wait_ge(S(f"more_step{l}"), x * 9 + 1)
                        nc.gpsimd.tensor_copy(idx_now, slot_tok[:, bass.ds(x + PAIRS, 1)]) \
                            .then_inc(S(f"more_step{l}"), 1)
                        pool.wait_ge(S(f"more_step{l}"), x * 9 + 2)
                        pool.sem_inc(S("gathers"), 1)
                        pool.indirect_dma_start(xg, None, xs[l], bass.IndirectOffsetOnAxis(idx_now, 0)) \
                            .then_inc(S(f"more_x{l}"), 16)
                        pool.wait_ge(S(f"more_step{l}"), x * 9 + 9)
                        pool.dma_start(ys[l].rearrange("(b p) d -> p b d", p=P)[:, bass.ds(x + PAIRS, 1)]
                                       .rearrange("p a d -> p (a d)"), yb).then_inc(S(f"more_out{l}"), 16)
                        pool.wait_ge(S(f"more_out{l}"), x * 16 + 16)
                        pool.sem_inc(S(f"more_step{l}"), 1)
                pool.wait_ge(S("y_out"), 16 * PAIRS * (l + 1))
                for i in range(NT):
                    n = ROWS[i]
                    if i >= 1 or l:
                        pool.wait_ge(S("yg_used"), NT * l + i)
                    for j in range(2):
                        pool.indirect_dma_start(yg[0:n, j], None, ys[l],
                                                bass.IndirectOffsetOnAxis(pos_i[0:n, NT * j + i:NT * j + i + 1], 0)) \
                            .then_inc(S("yg_in"), 16)

            nc.gpsimd.memset(zeros, 0.0).then_inc(S("pool_zero"), 1)
            pool.wait_ge(S("pool_zero"), 1)
            for b in range(MORE):
                pool.dma_start(ys_all[(PAIRS + b) * P:(PAIRS + b + 1) * P], zeros).then_inc(S("zero_out"), 16)
            pool.wait_ge(S("mkv_ev"), 8)
            for l in range(LAYERS):
                for out, lo in ((mem_k_p, 0), (mem_v_p, MW)):
                    pool.dma_start(out[l, 0].rearrange("(t p) h d -> p t (h d)", p=P), memkv[:, l, :, lo:lo + MW]) \
                        .then_inc(S("mp_out"), 16)
            pool.wait_ge(S("rst"), 24)
            pool.dma_start(ret_prompt[0, 0].rearrange("h d e -> d h e"), state_p).then_inc(S("rs_out"), 16)
            for h in range(RH):
                pool.wait_ge(S("rst"), 24 + h + 1)
                pool.dma_start(ret_sample[0, :, h].rearrange("b d e -> d b e"),
                               st_s[:, h % 2].rearrange("p (b e) -> p b e", b=DB)).then_inc(S(f"st_out{h % 2}"), 16)
            gains(0)
            dispatch(0)
            gains(1)
            pool.wait_ge(S("tables"), 64)
            for n in range(DB * PG):
                pg = pool.value_load(pages[0:1, n:n + 1], min_val=0, max_val=cache_fox_k.shape[0] - 1)
                pool.dma_start(past_f[:, n % PG, FH * (n // PG):FH * (n // PG) + FH],
                               cache_fox_logf.rearrange("n s h -> s n h")[:, bass.ds(pg, 1)]
                               .rearrange("s a h -> s (a h)")).then_inc(S("pf_in"), 16)
            pool.wait_ge(S("tm_ev"), 40)
            pool.dma_start(fox_k_p[0].rearrange("(t p) h d -> p t (h d)", p=P), k_rows[:, 0:ST]) \
                .then_inc(S("kv_out"), 16)
            pool.dma_start(fox_k_s.rearrange("b t h d -> (b t) (h d)"), k_rows[0:NS, ST]).then_inc(S("kv_out"), 16)
            pool.dma_start(fox_v_p[0].rearrange("(t p) h d -> p t (h d)", p=P), V[:, 0:ST]).then_inc(S("kv_out"), 16)
            pool.dma_start(fox_v_s.rearrange("b t h d -> (b t) (h d)"), V[0:NS, ST]).then_inc(S("kv_out"), 16)
            pool.wait_ge(S("logf"), 1)
            pool.dma_start(fox_f_p[0].rearrange("(t p) h -> p t h", p=P), logf[:, 0:ST]).then_inc(S("f_out"), 16)
            pool.dma_start(fox_f_s.rearrange("b t h -> (b t) h"), logf[0:NS, ST]).then_inc(S("f_out"), 16)
            gains(2)
            dispatch(1)
            gains(3)
            pool.wait_ge(S("x_ready"), 4 * NT)
            pool.dma_start(y_prompt[0].rearrange("(t p) d -> p t d", p=P), X[:, 0:ST]).then_inc(S("x_out"), 16)
            pool.dma_start(y_sample.rearrange("b t d -> (b t) d"), X[0:NS, ST]).then_inc(S("x_out"), 16)
            pool.wait_ge(S("x_out"), 32)
            pool.wait_ge(S("f_out"), 32)
            pool.wait_ge(S("kv_out"), 64)
            pool.wait_ge(S("mp_out"), 64)
            pool.wait_ge(S("rs_out"), 16)
            pool.wait_ge(S("st_out0"), 48)
            pool.wait_ge(S("st_out1"), 48)

        @block.tensor
        def _(pe):
            mm, tr = nc.tensor.matmul, nc.tensor.transpose

            def cols_of(p):
                for i in range(NT):
                    n = ROWS[i]
                    if p:
                        pe.wait_ge(S("x_ready"), NT * (p - 1) + i + 1)
                    for half in range(2):
                        j = 10 * p + 2 * i + half
                        if j >= 2:
                            pe.wait_ge(S("xt_cp"), j - 1)
                        for k in range(4):
                            kk = 4 * half + k
                            last = tr(bank(j % 2, n * k, n * k + n), X[0:n, i, kk * P:kk * P + P], ident[0:n, 0:n])
                        last.then_inc(S("xt_mm"), 1)

            def feature_major(n, w, lo):
                b = 2 * (n % 2)
                for k in range(KD):
                    mm(bank(b), w[:, k, lo:lo + P], XT[:, k, 0:SEQ], start=(k == 0), stop=(k == KD - 1))
                for k in range(KD):
                    last = mm(bank(b + 1, 0, NS), w[:, k, lo:lo + P], XT[:, k, SEQ:TOK], start=(k == 0),
                              stop=(k == KD - 1))
                return last

            def token_major(n, w, src, i, width):
                for k in range(KD):
                    last = mm(bank(4 + n % 4, 0, width, rows=(0, ROWS[i])), src[:, k, P * i:P * i + ROWS[i]],
                              w[:, k, :], start=(k == 0), stop=(k == KD - 1))
                return last

            def mem_prompt_attention(l):
                u0 = 16 * l

                def logits(u):
                    i, h = u // 4, u % 4
                    if u0 + u >= 2:
                        pe.wait_ge(S("mp_e"), u0 + u - 1)
                    f = slice(64 * (h % 2), 64 * (h % 2) + 64)
                    mm(bank(u % 2, 0, ML), mqT[f, h // 2, P * i:P * i + P], memkt[f, l, h // 2, :],
                       start=True, stop=True).then_inc(S("mp_l"), 1)

                def turn(u):
                    pe.wait_ge(S("mp_n"), u0 + u + 1)
                    if u0 + u >= 2:
                        pe.wait_ge(S("mp_c"), u0 + u - 1)
                    for m in range(2):
                        last = tr(bank(2 + u % 2, P * m, P * m + P), mpr[:, u % 2, P * m:P * m + P], ident)
                    last.then_inc(S("mp_t"), 1)

                def values(u):
                    i, h = u // 4, u % 4
                    pe.wait_ge(S("mp_c"), u0 + u + 1)
                    if h == 0 and 4 * l + i >= 2:
                        pe.wait_ge(S("mp_ev"), 4 * l + i - 1)
                    o = bank(4 + i % 2, P * (h // 2), P * (h // 2) + P, rows=(64 * (h % 2), 64 * (h % 2) + 64))
                    for m in range(2):
                        last = mm(o, memkv[:, l, m, MW + 64 * h:MW + 64 * h + 64], mprT[:, u % 2, P * m:P * m + P],
                                  start=(m == 0), stop=(m == 1))
                    last.then_inc(S("mp_o"), 1)

                for s in range(16 + 2):
                    if s < 16:
                        logits(s)
                    if 1 <= s <= 16:
                        turn(s - 1)
                    if s >= 2:
                        values(s - 2)

            def mem_sample_attention(l):
                for b in range(DB):
                    n = DB * l + b
                    pe.wait_ge(S(f"mk_in{b % 2}"), 16 * (4 * l + b // 2 + 1))
                    if n >= 2:
                        pe.wait_ge(S("mk_cp"), n - 1)
                    for hp in range(2):
                        for m in range(2):
                            o = P * (2 * hp + m)
                            last = tr(bank(6 + b % 2, o, o + P), mkc[b % 2][:, m, P * hp:P * hp + P], ident)
                    last.then_inc(S("mk_tr"), 1)
                    pe.wait_ge(S("mk_cp"), n + 1)
                    if b == 0:
                        pe.wait_ge(S("mp_e"), 16 * (l + 1))
                    for h in range(MH):
                        f = slice(64 * (h % 2), 64 * (h % 2) + 64)
                        for m in range(2):
                            o = NS * (2 * m + h // 2) + DS * b
                            last = mm(bank(h % 2, o, o + DS), mkcT[f, h // 2, m, :],
                                      mqT[f, h // 2, SEQ + DS * b:SEQ + DS * b + DS], start=True, stop=True,
                                      skip_group_check=True)
                    last.then_inc(S("ms_l"), 1)
                pe.wait_ge(S("ms_lt"), l + 1)
                pe.wait_ge(S("mp_c"), 16 * (l + 1))
                for m in range(2):
                    last = tr(bank(2, P * m, P * m + P), ml_t[:, m].rearrange("p h t -> p (h t)"), ident)
                last.then_inc(S("ms_r"), 1)
                pe.wait_ge(S("ms_n"), l + 1)
                for m in range(2):
                    last = tr(bank(3, P * m, P * m + P), ml_r[:, P * m:P * m + P], ident)
                last.then_inc(S("ms_t"), 1)
                pe.wait_ge(S("ms_c"), l + 1)
                pe.wait_ge(S("mv_in"), 128 * (l + 1))
                pe.wait_ge(S("mp_ev"), 4 * (l + 1))
                for b in range(DB):
                    for h in range(MH):
                        o = NS * (h // 2) + DS * b
                        for m in range(2):
                            last = mm(bank(4, o, o + DS, rows=(64 * (h % 2), 64 * (h % 2) + 64)),
                                      mvc[:, b, MW * m + 64 * h:MW * m + 64 * h + 64],
                                      mp_s[:, m, NS * h + DS * b:NS * h + DS * b + DS],
                                      start=(m == 0), stop=(m == 1), skip_group_check=True)
                last.then_inc(S("ms_o"), 1)

            def output_projection(l, c0):
                pe.wait_ge(S("ms_ev"), l + 1)
                for c in range(4):
                    chunk_ready(pe, c0 + c)
                    for i in range(NT):
                        j = 20 * l + 5 * c + i
                        if j >= 4:
                            pe.wait_ge(S("wo_ev"), j - 3)
                        token_major(j, wslot_view(c0 + c), MX, i, 256).then_inc(S("wo_mm"), 1)

            def router(l):
                pe.wait_ge(S("route_in"), 16 * 7 * (l + 1))
                for i in range(NT):
                    n = ROWS[i]
                    j = NT * l + i
                    pe.wait_ge(S("xt_cp"), 10 * (2 * l + 1) + 2 * i + 2)
                    if j >= 2:
                        pe.wait_ge(S("rt_ev"), j - 1)
                    for k in range(KD):
                        last = mm(bank(2 + j % 2, 0, NG + NE, rows=(0, n)), XT[:, k, P * i:P * i + n], wr[:, k, :],
                                  start=(k == 0), stop=(k == KD - 1))
                    last.then_inc(S("rt_mm"), 1)
                pe.wait_ge(S("onehot"), l + 1)
                pe.wait_ge(S("wo_ev"), 20 * (l + 1))
                for i in range(NT):
                    for q in range(i + 1):
                        mm(bank(4, NE * i, NE * i + NE), C("strict") if q == i else C("ones"), cnt[:, q, :],
                           start=(q == 0), stop=(q == i))
                for q in range(NT):
                    last = mm(bank(4, NE * NT, NE * NT + NE), C("ones"), cnt[:, q, :], start=(q == 0),
                              stop=(q == NT - 1))
                last.then_inc(S("rank_mm"), 1)
                pe.wait_ge(S("places"), l + 1)
                for n in range(10):
                    last = mm(bank(5, 0, 64), a1[:, n, :], (bb if n < 5 else bb2)[:, n % 5, :], start=(n == 0),
                              stop=(n == 9))
                last.then_inc(S("slot_mm"), 1)

            def turn_rows(waits_done=None):
                for half in range(2):
                    for k in range(4):
                        kk = 4 * half + k
                        last = tr(bank(2 + half, P * k, P * k + P), xg[:, kk * P:kk * P + P], ident)
                return last

            def experts(l):
                s = l * PAIRS
                g = l * (PAIRS + 1)
                for j in range(2):
                    pe.sem_inc(S(f"up_free{j}"), 1 if l == 0 else 0) if l == 0 else None
                    pe.sem_inc(S(f"down_free{j}"), 1) if l == 0 else None
                if l == 0:
                    pe.sem_inc(S("xg_free"), 1)
                pe.wait_ge(S("slots"), l + 1)
                pe.wait_ge(S("xg_in"), 16 * (g + 1))
                turn_rows().then_inc(S("xg_free"), 1)
                with pe.Fori(0, PAIRS) as i:
                    pe.wait_ge(S("xgt"), i + (g + 1))
                    for j in range(2):
                        pe.wait_ge(S(f"up_in{j}"), i * 16 + (16 * s + 16))
                        for f in range(4):
                            for k in range(KD):
                                last = mm(bank(j, SLOTS * f, SLOTS * f + SLOTS), WU[j][:, k, P * f:P * f + P],
                                          xgT[:, k, SLOTS * j:SLOTS * j + SLOTS], start=(k == 0),
                                          stop=(k == KD - 1))
                        last.then_inc(S(f"up_free{j}"), 1)
                    pe.wait_ge(S("xg_in"), i * 16 + (16 * g + 32))
                    turn_rows().then_inc(S("xg_free"), 1)
                    pe.wait_ge(S("y_ev"), i + (s + 1))
                    for j in range(2):
                        pe.wait_ge(S(f"down_in{j}"), i * 16 + (16 * s + 16))
                        pe.wait_ge(S("hid"), i * 2 + (2 * s + j + 1))
                        for half in range(2):
                            for f in range(2):
                                last = mm(bank(4 + half, rows=(SLOTS * j, SLOTS * j + SLOTS)), hid[:, j, f, :],
                                          WD[j][:, f, 512 * half:512 * half + 512], start=(f == 0), stop=(f == 1))
                        last.then_inc(S(f"down_free{j}"), 1)
                more = pe.value_load(lists[0:1, 16:17], min_val=0, max_val=MORE)
                pe.wait_ge(S("xgt"), g + PAIRS + 1)
                pe.wait_ge(S("y_ev"), s + PAIRS + 1)
                pe.sem_inc(S(f"more_step{l}"), 1)
                with pe.If(more > 0):
                    with pe.Fori(0, more) as x:
                        pe.wait_ge(S(f"more_step{l}"), x * 9 + 2)
                        pe.wait_ge(S(f"more_x{l}"), x * 16 + 16)
                        turn_rows().then_inc(S(f"more_step{l}"), 1)
                        pe.wait_ge(S(f"more_step{l}"), x * 9 + 4)
                        pe.wait_ge(S(f"more_w{l}"), x * 32 + 32)
                        for f in range(4):
                            for k in range(KD):
                                last = mm(bank(0, P * f, P * f + P), WU[0][:, k, P * f:P * f + P], xgT[:, k, :],
                                          start=(k == 0), stop=(k == KD - 1))
                        last.then_inc(S(f"more_step{l}"), 1)
                        pe.wait_ge(S(f"more_step{l}"), x * 9 + 7)
                        for half in range(2):
                            for f in range(2):
                                last = mm(bank(4 + half), hidx[:, f, :], WD[0][:, f, 512 * half:512 * half + 512],
                                          start=(f == 0), stop=(f == 1))
                        last.then_inc(S(f"more_step{l}"), 1)

            pe.wait_ge(S("inputs"), 48)
            cols_of(0)
            pe.wait_ge(S("tables"), 64)
            for m in range(2):
                for half in range(2):
                    j = 2 * m + half
                    if j >= 2:
                        pe.wait_ge(S("mt_cp"), j - 1)
                    for k in range(4):
                        kk = 4 * half + k
                        last = tr(bank(2 + j % 2, P * k, P * k + P), mem_rows[:, m, kk * P:kk * P + P], ident)
                    last.then_inc(S("mt_mm"), 1)
            pe.wait_ge(S("mt_cp"), 4)
            for l in range(LAYERS):
                for kv in range(2):
                    chunk_ready(pe, CH_KV + 2 * l + kv)
                    for m in range(2):
                        j = 4 * l + 2 * kv + m
                        if j >= 4:
                            pe.wait_ge(S("mkv_ev"), j - 3)
                        for k in range(KD):
                            last = mm(bank(4 + j % 4, 0, 256), memT[:, k, P * m:P * m + P],
                                      wslot_view(CH_KV + 2 * l + kv)[:, k, :], start=(k == 0), stop=(k == KD - 1))
                        last.then_inc(S("mkv_mm"), 1)
                pe.wait_ge(S("mkv_ev"), 4 * l + 2)
                for hp in range(2):
                    for m in range(2):
                        o = P * (2 * hp + m)
                        last = tr(bank(2 + l, o, o + P), memkv[:, l, m, P * hp:P * hp + P], ident)
                last.then_inc(S("mkt_mm"), 1)
            pe.wait_ge(S("xt_cp"), 10)
            for h in range(2 * RH):
                n = CH_A + h // 3
                if h % 3 == 0:
                    chunk_ready(pe, n)
                if h >= 2:
                    pe.wait_ge(S("rope_ev"), h - 1)
                elif h == 1:
                    pe.wait_ge(S("mkt_ev"), 2)
                feature_major(h, wslot_view(n), P * (h % 3)).then_inc(S("rope_mm"), 1)
            pe.wait_ge(S("mkv_ev"), 8)
            for j in range(20):
                n = CH_A + 4 + j // 5
                if j % 5 == 0:
                    chunk_ready(pe, n)
                if j >= 4:
                    pe.wait_ge(S("tm_ev"), j - 3)
                token_major(j, wslot_view(n), XT, j % 5, 384).then_inc(S("tm_mm"), 1)
            pe.wait_ge(S("rope_ev"), 12)
            chunk_ready(pe, CH_A + 8)
            for n in range(2):
                feature_major(n, wslot_view(CH_A + 8), P * n).then_inc(S("fm_mm"), 1)

            def front(u):
                n, h = u // RH, u % RH
                if u == 0:
                    pe.wait_ge(S("fm_ev"), 2)
                if u >= 2:
                    pe.wait_ge(S("rsm"), u - 1)
                mm(bank(u % 2, 0, P), kT[:, h, P * n:P * n + P], qT[:, h, P * n:P * n + P], start=True,
                   stop=True).then_inc(S("rsc"), 1)
                if u >= 2:
                    pe.wait_ge(S("rkd"), u - 1)
                tr(bank(2 + u % 2, 0, P), kT[:, h, P * n:P * n + P], ident).then_inc(S("rkt"), 1)

            def back(u):
                n, h = u // RH, u % RH
                if u == 0:
                    pe.wait_ge(S("tm_ev"), 20)
                pe.wait_ge(S("rsm"), u + 1)
                if u >= 2:
                    pe.wait_ge(S("rcp"), u - 1)
                v = V[:, n, P * h:P * h + P]
                last = mm(bank(4 + u % 2, 0, P), scm[:, u % 2, :], v, start=True, stop=(n == 0))
                if n:
                    pe.wait_ge(S("rst"), u - RH + 1)
                    last = mm(bank(4 + u % 2, 0, P), qd[:, u % 2, :], state_p[:, h, :], start=False, stop=True)
                last.then_inc(S("rr"), 1)
                pe.wait_ge(S("rkd"), u + 1)
                if u >= 2:
                    pe.wait_ge(S("rst"), u - 1)
                mm(bank(6 + u % 2, 0, P), kd[:, u % 2, :], v, start=True, stop=True).then_inc(S("rkv"), 1)

            for u in range(4 * RH + 1):
                if u < 4 * RH:
                    front(u)
                if u:
                    back(u - 1)
            pe.wait_ge(S("rst"), 24)
            pe.wait_ge(S("rcp"), 24)
            pe.wait_ge(S("rkd"), 24)
            for h in range(RH):
                b = h % 2
                if h >= 2:
                    pe.wait_ge(S("rsm"), 24 + h - 1)
                    pe.wait_ge(S("rkd"), 24 + h - 1)
                    pe.wait_ge(S("rcp"), 24 + h - 1)
                mm(bank(b, 0, NS, rows=(0, NS)), kT[:, h, SEQ:TOK], qT[:, h, SEQ:TOK], start=True,
                   stop=True).then_inc(S("rsc"), 1)
                tr(bank(2 + b, 0, P, rows=(0, NS)), kT[:, h, SEQ:TOK], ident).then_inc(S("rkt"), 1)
                pe.wait_ge(S("rsm"), 24 + h + 1)
                pe.wait_ge(S(f"st_in{b}"), 16 * (h // 2 + 1))
                mm(bank(4 + b, 0, NS), V[0:NS, ST, P * h:P * h + P], scs[0:NS, b, :], start=True, stop=False,
                   skip_group_check=True)
                for q in range(DB):
                    last = mm(bank(4 + b, DS * q, DS * q + DS), st_s[:, b, P * q:P * q + P],
                              qds[:, b, DS * q:DS * q + DS], start=False, stop=(q == DB - 1), skip_group_check=True)
                last.then_inc(S("rr"), 1)
                pe.wait_ge(S("rkd"), 24 + h + 1)
                if h:
                    pe.wait_ge(S("rst"), 24 + h)
                for q in range(2):
                    last = mm(bank(6 + q), kds[0:NS, :], vbd[0:NS, 512 * q:512 * q + 512], start=True, stop=True)
                last.then_inc(S("rkv"), 1)
            pe.wait_ge(S("rcp"), 24 + RH)
            pe.wait_ge(S("rsm"), 24 + RH)
            for h in range(RH):
                last = tr(bank(h // 4, P * (h % 4), P * (h % 4) + P, rows=(0, NS)), rTs[:, h, :], ident)
            last.then_inc(S("srt"), 1)
            pe.wait_ge(S("srow"), 1)
            pe.wait_ge(S("rkd"), 24 + RH)
            for i in range(NT):
                n = ROWS[i]
                pe.wait_ge(S("gated"), i + 1)
                if i >= 2:
                    pe.wait_ge(S("tk_cp"), i - 1)
                for h in range(RH):
                    o = 1024 * (i % 2) + n * h
                    last = tr(ps[:, o:o + n], R[0:n, i, P * h:P * h + P], ident[0:n, 0:n])
                last.then_inc(S("tk_mm"), 1)
            pe.wait_ge(S("tk_cp"), NT)
            pe.wait_ge(S("rst"), 24 + RH)
            pe.sem_inc(S("tok_done"), 1)
            mem_prompt_attention(0)
            mem_sample_attention(0)
            output_projection(0, CH_O)
            cols_of(1)
            router(0)
            experts(0)
            cols_of(2)

            pe.wait_ge(S("xt_cp"), 30)
            for j in range(20, 45):
                n = CH_S + (j - 20) // 5
                if j % 5 == 0:
                    chunk_ready(pe, n)
                if j >= 24:
                    pe.wait_ge(S("tm_ev"), j - 3)
                token_major(j, wslot_view(n), XT, j % 5, 12 if j >= 40 else 384).then_inc(S("tm_mm"), 1)
            for i in range(NT):
                n = ROWS[i]
                pe.wait_ge(S("tm_ev"), 30)
                if i >= 2:
                    pe.wait_ge(S("tk_cp"), NT + i - 1)
                for h in range(6):
                    o = 1024 * (i % 2) + n * h
                    last = tr(ps[:, o:o + n], k_rows[0:n, i, P * h:P * h + P], ident[0:n, 0:n])
                last.then_inc(S("tk_mm"), 1)
            pe.wait_ge(S("tk_cp"), NT + NT)
            for n in range(2, 10):
                c = CH_B + (n - 2) // 3
                if (n - 2) % 3 == 0:
                    chunk_ready(pe, c)
                if n >= 4:
                    pe.wait_ge(S("fm_ev"), n - 1)
                feature_major(n, wslot_view(c), P * ((n - 2) % 3)).then_inc(S("fm_mm"), 1)
            pe.wait_ge(S("logf"), 1)
            pe.wait_ge(S("tm_ev"), 45)
            pe.wait_ge(S("pf_in"), 16 * DB * PG)
            for i in range(ST):
                for q in range(i + 1):
                    mm(bank(4, FH * i, FH * i + FH), C("tri") if q == i else C("ones"), logf[:, q, :],
                       start=(q == 0), stop=(q == i))
            o = bank(4, FH * ST, FH * NT, rows=(0, NS))
            mm(o, C("tri_s", NS), logf[0:NS, ST, :], start=True, stop=False)
            for b in range(DB):
                for g in range(PG):
                    last = mm(o, C("batch_s")[:, 28 - DS * b:60 - DS * b], past_f[:, g, FH * b:FH * b + FH],
                              start=False, stop=(b == DB - 1 and g == PG - 1))
            mm(bank(5, 0, DB * FH), C("tri"), past_f[:, 0, :], start=True, stop=True)
            mm(bank(5, DB * FH, 2 * DB * FH), C("ones"), past_f[:, 0, :], start=True, stop=False)
            mm(bank(5, DB * FH, 2 * DB * FH), C("tri"), past_f[:, 1, :], start=False, stop=True) \
                .then_inc(S("cum"), 1)
            pe.wait_ge(S("cum_ev"), 1)
            pe.wait_ge(S("fm_ev"), 10)

            units = [(2 * hp + r, i) for hp in range(6) for i in range(ST) for r in range(2)]

            def minus_c(h):
                if h >= 2:
                    pe.wait_ge(S("fnb_cp"), h - 1)
                for q in range(ST):
                    last = mm(bank(6 + h % 2, P * q, P * q + P), negc[:, q, h:h + 1].broadcast_to([P, P]), ident,
                              start=True, stop=True)
                last.then_inc(S("fnb"), 1)

            def fox_logits(u):
                h, i = units[u]
                if i == 0:
                    minus_c(h)
                if u >= 2:
                    pe.wait_ge(S("fp_s"), u - 1)
                f = slice(64 * (h % 2), 64 * (h % 2) + 64)
                mm(bank(u % 2, 0, P * (i + 1)), qT[f, h // 2, P * i:P * i + P], kT[f, h // 2, 0:P * (i + 1)],
                   start=True, stop=True).then_inc(S("fp_l"), 1)

            def fox_turn(u):
                h, i = units[u]
                pe.wait_ge(S("fp_n"), u + 1)
                if u >= 2:
                    pe.wait_ge(S("fp_c"), u - 1)
                for q in range(i + 1):
                    last = tr(bank(2 + u % 2, P * q, P * q + P), fpr[:, u % 2, P * q:P * q + P], ident)
                last.then_inc(S("fp_t"), 1)

            def fox_values(u):
                h, i = units[u]
                pe.wait_ge(S("fp_c"), u + 1)
                if u % 2 == 0 and u >= 4:
                    pe.wait_ge(S("fp_ev"), u // 2 - 1)
                for q in range(i + 1):
                    last = mm(bank(4 + (u // 2) % 2, 0, P, rows=(64 * (h % 2), 64 * (h % 2) + 64)),
                              V[:, q, FD * h:FD * h + FD], fprT[:, u % 2, P * q:P * q + P], start=(q == 0),
                              stop=(q == i))
                last.then_inc(S("fox_p"), 1)

            for s in range(48 + 2):
                if s < 48:
                    fox_logits(s)
                if 1 <= s <= 48:
                    fox_turn(s - 1)
                if s >= 2:
                    fox_values(s - 2)
            pe.wait_ge(S("fp_ev"), 24)
            for n in range(DB * PG):
                b, g = n // PG, n % PG
                pe.wait_ge(S(f"fk_in{n % 2}"), 16 * (n // 2 + 1))
                if n:
                    pe.wait_ge(S("fk_cp"), n)
                for h in range(6):
                    last = tr(ps[:, 3072 + P * h:3072 + P * h + P], fkc[n % 2][:, P * h:P * h + P], ident)
                last.then_inc(S("fk_tr"), 1)
                pe.wait_ge(S("fk_cp"), n + 1)
                for h in range(FH):
                    f = slice(64 * (h % 2), 64 * (h % 2) + 64)
                    o = NS * (h // 2) + DS * b
                    last = mm(bank(2 * g + h % 2, o, o + DS), fkT[n % 2][f, h // 2, :],
                              qT[f, h // 2, SEQ + DS * b:SEQ + DS * b + DS], start=True, stop=True,
                              skip_group_check=True)
                last.then_inc(S("fs_l"), 1)
            for h in range(FH):
                f = slice(64 * (h % 2), 64 * (h % 2) + 64)
                rr = (NS * (h % 4), NS * (h % 4) + NS)
                o = bank(4 + h % 2, NS * (h // 4), NS * (h // 4) + NS, rows=rr)
                mm(o, qT[f, h // 2, SEQ:TOK], kT[f, h // 2, SEQ:TOK], start=True, stop=False, skip_group_check=True)
                last = mm(o, negc[0:NS, ST, h:h + 1].broadcast_to([NS, NS]), ident[0:NS, 0:NS], start=False,
                          stop=True, skip_group_check=True)
            last.then_inc(S("fs_new"), 1)
            for r in range(3):
                pe.wait_ge(S("fs_lt"), PG)
                if r >= 1:
                    pe.wait_ge(S("fs_lr"), r)
                for g in range(PG):
                    last = tr(bank(6, PAGE * g, PAGE * g + PAGE),
                              fl_t[:, g, 4 * r:4 * r + 4].rearrange("p h t -> p (h t)"), ident)
                last.then_inc(S("fs_r"), 1)
            for r in range(3):
                pe.wait_ge(S("fs_n"), r + 1)
                if r:
                    pe.wait_ge(S("fs_c"), r)
                for g in range(PG):
                    tr(bank(7, PAGE * g, PAGE * g + PAGE), fl_r[:, r, PAGE * g:PAGE * g + PAGE], ident)
                tr(bank(7, PG * PAGE, PG * PAGE + P, rows=(0, NS)), fl_r[:, r, PG * PAGE:], ident) \
                    .then_inc(S("fs_t"), 1)
            pe.wait_ge(S("fs_c"), 3)
            for h in range(FH):
                mm(bank(0, NS * (h // 2), NS * (h // 2) + NS, rows=(64 * (h % 2), 64 * (h % 2) + 64)),
                   V[0:NS, ST, FD * h:FD * h + FD], fs_p[0:NS, h // 4, 2, NS * (h % 4):NS * (h % 4) + NS],
                   start=(h < 2), stop=False, skip_group_check=True)
            for n in range(DB * PG):
                b, g = n // PG, n % PG
                pe.wait_ge(S(f"fv_in{n % 2}"), 16 * (n // 2 + 1))
                for h in range(FH):
                    o = NS * (h // 2) + DS * b
                    c = NS * (h % 4) + DS * b
                    last = mm(bank(0, o, o + DS, rows=(64 * (h % 2), 64 * (h % 2) + 64)),
                              fvc[n % 2][:, FD * h:FD * h + FD], fs_p[:, h // 4, g, c:c + DS], start=False,
                              stop=(n == DB * PG - 1), skip_group_check=True)
                last.then_inc(S("fs_pv"), 1)
            pe.wait_ge(S("fs_ev"), 1)
            pe.sem_inc(S("tok_done"), 1)
            mem_prompt_attention(1)
            mem_sample_attention(1)
            output_projection(1, CH_O1)
            cols_of(3)
            router(1)
            experts(1)

        @block.scalar
        def _(act):
            af = nc.scalar.activation

            def copy_cols(p):
                for j in range(2 * NT):
                    i, half, n = j // 2, j % 2, ROWS[j // 2]
                    act.wait_ge(S("xt_mm"), 10 * p + j + 1)
                    af(XT[:, 4 * half:4 * half + 4, P * i:P * i + n],
                       bank(j % 2, 0, 4 * n).rearrange("p (k n) -> p k n", k=4), ACT.Copy).then_inc(S("xt_cp"), 1)

            def mem_prompt(l):
                u0 = 16 * l
                for s in range(17):
                    if s < 16:
                        act.wait_ge(S("mp_m"), u0 + s + 1)
                        if u0 + s >= 2:
                            act.wait_ge(S("mp_t"), u0 + s - 1)
                        af(mpr[:, s % 2, :], bank(s % 2, 0, ML), ACT.Exp, bias=nmx[:, s % 4:s % 4 + 1],
                           accum_out=esum[:, s % 4:s % 4 + 1]).then_inc(S("mp_e"), 1)
                    if s:
                        u = s - 1
                        act.wait_ge(S("mp_t"), u0 + u + 1)
                        if u0 + u >= 2:
                            act.wait_ge(S("mp_o"), u0 + u - 1)
                        af(mprT[:, u % 2, :], bank(2 + u % 2, 0, ML), ACT.Copy).then_inc(S("mp_c"), 1)

            def mem_sample(l):
                for b in range(DB):
                    n = DB * l + b
                    act.wait_ge(S("mk_tr"), n + 1)
                    if n:
                        act.wait_ge(S("ms_l"), n)
                    af(mkcT, bank(6 + b % 2).rearrange("p (a m t) -> p a m t", a=2, m=2), ACT.Copy) \
                        .then_inc(S("mk_cp"), 1)
                act.wait_ge(S("ms_l"), DB * (l + 1))
                for r in range(2):
                    last = af(ml_t[:, :, r::2, :], bank(r, 0, 128).rearrange("p (m a t) -> p m a t", m=2, a=2),
                              ACT.Copy)
                last.then_inc(S("ms_lt"), 1)
                act.wait_ge(S("ms_m"), l + 1)
                af(ml_r, bank(2, 0, ML), ACT.Exp, bias=nmx[:, 0:1], accum_out=esum[:, 0:1]).then_inc(S("ms_e"), 1)
                act.wait_ge(S("ms_t"), l + 1)
                af(mp_s, bank(3, 0, ML).rearrange("p (m t) -> p m t", m=2), ACT.Copy).then_inc(S("ms_c"), 1)
                act.wait_ge(S("ms_o"), l + 1)
                af(MX[:, 6:8, SEQ:TOK], bank(4, 0, 2 * NS).rearrange("p (a t) -> p a t", a=2), ACT.Copy) \
                    .then_inc(S("ms_ev"), 1)

            def deviation(p):
                act.wait_ge(S("ln_st"), p + 1)
                af(rstd, mv[:, :, 1], ACT.Sqrt, bias=eps_ln[:, 0:1]).then_inc(S("ln_sd"), 1)

            def routing(l):
                act.wait_ge(S("r_step"), 4 * l + 1)
                af(gexp, gexp, ACT.Exp).then_inc(S("r_step"), 1)
                act.wait_ge(S("r_step"), 4 * l + 3)
                af(tmpw, tmpw, ACT.Exp).then_inc(S("r_step"), 1)

            def turn_copy(sem):
                for half in range(2):
                    last = af(xgT[:, 4 * half:4 * half + 4, :],
                              bank(2 + half).rearrange("p (k n) -> p k n", k=4), ACT.Copy)
                last.then_inc(sem, 1)

            def experts(l):
                s, g = l * PAIRS, l * (PAIRS + 1)
                if l == 0:
                    act.sem_inc(S("y_ev"), 1)
                act.wait_ge(S("xg_free"), g + 2)
                turn_copy(S("xgt"))
                with act.Fori(0, PAIRS) as i:
                    for j in range(2):
                        act.wait_ge(S(f"up_free{j}"), i + (s + 2))
                        af(sg[:, j, :], bank(j, 0, 2 * SLOTS), ACT.Silu).then_inc(S("gate"), 1)
                    act.wait_ge(S("xg_free"), i + (g + 3))
                    turn_copy(S("xgt"))
                    act.wait_ge(S("down_free1"), i + (s + 2))
                    for half in range(2):
                        last = af(yb[:, 512 * half:512 * half + 512], bank(4 + half), ACT.Copy,
                                  scale=wslot[:, bass.ds(i, 1)])
                    last.then_inc(S("y_ev"), 1)
                    act.wait_ge(S("y_ev"), i + (s + 2))
                    act.dma_start(ys[l].rearrange("(b p) d -> p b d", p=P)[:, bass.ds(i, 1)]
                                  .rearrange("p a d -> p (a d)"), yb).then_inc(S("y_out"), 16)
                    act.wait_ge(S("y_out"), i * 16 + (16 * s + 16))
                more = act.value_load(lists[0:1, 16:17], min_val=0, max_val=MORE)
                with act.If(more > 0):
                    with act.Fori(0, more) as x:
                        act.wait_ge(S(f"more_step{l}"), x * 9 + 3)
                        turn_copy(S(f"more_step{l}"))
                        act.wait_ge(S(f"more_step{l}"), x * 9 + 5)
                        af(sgx, bank(0, 0, 2 * P).rearrange("p (f n) -> p f n", f=2), ACT.Silu) \
                            .then_inc(S(f"more_step{l}"), 1)
                        act.wait_ge(S(f"more_step{l}"), x * 9 + 8)
                        for half in range(2):
                            last = af(yb[:, 512 * half:512 * half + 512], bank(4 + half), ACT.Copy,
                                      scale=wslot[:, bass.ds(x + PAIRS, 1)])
                        last.then_inc(S(f"more_step{l}"), 1)

            copy_cols(0)
            for j in range(4):
                act.wait_ge(S("mt_mm"), j + 1)
                af(memT[:, 4 * (j % 2):4 * (j % 2) + 4, P * (j // 2):P * (j // 2) + P],
                   bank(2 + j % 2).rearrange("p (k n) -> p k n", k=4), ACT.Copy).then_inc(S("mt_cp"), 1)
            for l in range(LAYERS):
                for j in range(4):
                    act.wait_ge(S("mkv_mm"), 4 * l + j + 1)
                    af(memkv[:, l, j % 2, MW * (j // 2):MW * (j // 2) + MW], bank(4 + j, 0, 256), ACT.Copy) \
                        .then_inc(S("mkv_ev"), 1)
                act.wait_ge(S("mkt_mm"), l + 1)
                af(memkt[:, l], bank(2 + l).rearrange("p (a t) -> p a t", a=2), ACT.Copy).then_inc(S("mkt_ev"), 1)
            for j in range(20):
                n, i = ROWS[j % 5], j % 5
                act.wait_ge(S("tm_mm"), j + 1)
                c = 384 * ((j // 5) % 2)
                if j < 10:
                    af(V[0:n, i, c:c + 384], bank(4 + j % 4, 0, 384, rows=(0, n)), ACT.Copy).then_inc(S("tm_ev"), 1)
                else:
                    af(G[0:n, i, c:c + 384], bank(4 + j % 4, 0, 384, rows=(0, n)), ACT.Silu).then_inc(S("tm_ev"), 1)

            def queries(n, dst, scale):
                act.wait_ge(S("fm_mm"), n + 1)
                o = 1024 * (n % 2)
                af(dst, ps[:, o:o + TOK], ACT.Copy, scale=scale).then_inc(S("fm_ev"), 1)

            for n in range(2):
                queries(n, mqT[:, n, :], MD ** -0.5)

            def decayed_keys(u):
                act.wait_ge(S("rkt"), u + 1)
                if u >= 2:
                    act.wait_ge(S("rkv"), u - 1)
                af(kd[:, u % 2, :], bank(2 + u % 2, 0, P), ACT.Copy,
                   scale=C("kdecay")[:, u % RH:u % RH + 1]).then_inc(S("rkd"), 1)

            act.wait_ge(S("rope_ev"), 12)
            decayed_keys(0)
            for u in range(4 * RH):
                if u + 1 < 4 * RH:
                    decayed_keys(u + 1)
                act.wait_ge(S("rr"), u + 1)
                af(R[:, u // RH, P * (u % RH):P * (u % RH) + P], bank(4 + u % 2, 0, P), ACT.Copy) \
                    .then_inc(S("rcp"), 1)
            for h in range(RH):
                act.wait_ge(S("rkt"), 24 + h + 1)
                if h:
                    act.wait_ge(S("rkv"), 24 + h)
                af(kds[0:NS, :], bank(2 + h % 2, 0, P, rows=(0, NS)), ACT.Copy).then_inc(S("rkd"), 1)
                act.wait_ge(S("rr"), 24 + h + 1)
                af(rTs[:, h, :], bank(4 + h % 2, 0, NS), ACT.Copy).then_inc(S("rcp"), 1)
            act.wait_ge(S("srt"), 1)
            af(R[0:NS, ST, :], ps[0:NS, 0:RW], ACT.Copy).then_inc(S("srow"), 1)
            act.wait_ge(S("hmv"), 1)
            af(hrs, hmv[:, :, 1], ACT.Sqrt, bias=eps_hn[:, 0:1]).then_inc(S("hsd"), 1)
            act.wait_ge(S("st_out0"), 48)
            act.wait_ge(S("st_out1"), 48)
            for i in range(NT):
                n = ROWS[i]
                act.wait_ge(S("tk_mm"), i + 1)
                o = 1024 * (i % 2)
                af(MX[:, 0:6, P * i:P * i + n], ps[:, o:o + 6 * n].rearrange("p (h n) -> p h n", h=6), ACT.Copy) \
                    .then_inc(S("tk_cp"), 1)
            mem_prompt(0)
            mem_sample(0)
            deviation(0)
            copy_cols(1)
            routing(0)
            experts(0)
            deviation(1)
            copy_cols(2)

            for j in range(20, 45):
                n, i = ROWS[j % 5], j % 5
                act.wait_ge(S("tm_mm"), j + 1)
                c = 384 * ((j // 5) % 2)
                if j < 40:
                    dst = (k_rows if j < 30 else V)[0:n, i, c:c + 384]
                    af(dst, bank(4 + j % 4, 0, 384, rows=(0, n)), ACT.Copy).then_inc(S("tm_ev"), 1)
                else:
                    af(fz[0:n, i, :], bank(4 + j % 4, 0, FH, rows=(0, n)), ACT.Copy).then_inc(S("tm_ev"), 1)
            for i in range(NT):
                n = ROWS[i]
                act.wait_ge(S("tk_mm"), NT + i + 1)
                o = 1024 * (i % 2)
                af(kT[:, :, P * i:P * i + n], ps[:, o:o + 6 * n].rearrange("p (h n) -> p h n", h=6), ACT.Copy) \
                    .then_inc(S("tk_cp"), 1)
            for n in range(2, 10):
                queries(n, qT[:, n - 2, :] if n < 8 else mqT[:, n - 8, :], FD ** -0.5)
            act.wait_ge(S("f_step"), 1)
            af(fe, fe, ACT.Exp, scale=-1.0).then_inc(S("f_step"), 1)
            act.wait_ge(S("f_step"), 3)
            af(fe, fe, ACT.Ln).then_inc(S("f_step"), 1)

            def prompt_unit(s):
                h, i = 2 * (s // 8) + s % 2, (s // 2) % 4
                if i == 0:
                    act.wait_ge(S("fnb"), h + 1)
                    if h >= 2:
                        act.wait_ge(S("fp_s"), s - 1)
                    af(fnb[:, h % 2, :], bank(6 + h % 2), ACT.Copy).then_inc(S("fnb_cp"), 1)
                act.wait_ge(S("fp_m"), s + 1)
                af(fpr[:, s % 2, 0:P * (i + 1)], fpr[:, s % 2, 0:P * (i + 1)], ACT.Exp,
                   bias=nmx[:, s % 4:s % 4 + 1], accum_out=esum[:, s % 4:s % 4 + 1]).then_inc(S("fp_e"), 1)

            def prompt_turn(u):
                i = (u // 2) % 4
                act.wait_ge(S("fp_t"), u + 1)
                if u >= 2:
                    act.wait_ge(S("fox_p"), u - 1)
                af(fprT[:, u % 2, 0:P * (i + 1)], bank(2 + u % 2, 0, P * (i + 1)), ACT.Copy).then_inc(S("fp_c"), 1)

            act.wait_ge(S("x_ready"), 2 * NT)
            for s in range(49):
                if s < 48:
                    prompt_unit(s)
                if s:
                    prompt_turn(s - 1)
            for n in range(DB * PG):
                act.wait_ge(S("fk_tr"), n + 1)
                if n >= 2:
                    act.wait_ge(S("fs_l"), n - 1)
                af(fkT[n % 2], ps[:, 3072:3072 + FW].rearrange("p (h t) -> p h t", h=6), ACT.Copy) \
                    .then_inc(S("fk_cp"), 1)
            for r in range(3):
                act.wait_ge(S("fs_m"), r + 1)
                af(fl_r[:, r, :], fl_r[:, r, :], ACT.Exp, bias=nmx[:, r:r + 1], accum_out=esum[:, r:r + 1]) \
                    .then_inc(S("fs_e"), 1)
            for r in range(3):
                act.wait_ge(S("fs_t"), r + 1)
                af(fs_p[:, r, 0:2, :], bank(7, 0, 2 * P).rearrange("p (g t) -> p g t", g=2), ACT.Copy)
                af(fs_p[0:NS, r, 2, :], bank(7, 2 * P, 3 * P, rows=(0, NS)), ACT.Copy).then_inc(S("fs_c"), 1)
            act.wait_ge(S("fs_pv"), DB * PG)
            af(MX[:, 0:6, SEQ:TOK], bank(0, 0, 6 * NS).rearrange("p (h t) -> p h t", h=6), ACT.Copy) \
                .then_inc(S("fs_ev"), 1)
            mem_prompt(1)
            mem_sample(1)
            deviation(2)
            copy_cols(3)
            routing(1)
            experts(1)
            deviation(3)

        @block.vector
        def _(dve):
            v = nc.vector
            count = [0]

            def link(ins):
                count[0] += 1
                ins.then_inc(S("dve_c"), 1)
                dve.wait_ge(S("dve_c"), count[0])

            def bc(ap, shape):
                return ap.broadcast_to(shape)

            def mem_prompt(l):
                u0 = 16 * l

                def softmax_top(u):
                    q = u % 4
                    dve.wait_ge(S("mp_l"), u0 + u + 1)
                    link(v.tensor_reduce(mx[:, q:q + 1], bank(u % 2, 0, ML), AX.X, ALU.max))
                    v.tensor_scalar(nmx[:, q:q + 1], mx[:, q:q + 1], -1.0, None, ALU.mult).then_inc(S("mp_m"), 1)

                def softmax_scale(u):
                    q = u % 4
                    dve.wait_ge(S("mp_e"), u0 + u + 1)
                    link(v.reciprocal(rsum[:, q:q + 1], esum[:, q:q + 1]))
                    v.tensor_scalar(mpr[:, u % 2, :], mpr[:, u % 2, :], rsum[:, q:q + 1], None, ALU.mult) \
                        .then_inc(S("mp_n"), 1)

                def result(i):
                    dve.wait_ge(S("mp_o"), u0 + 4 * i + 4)
                    v.tensor_copy(MX[:, 6:8, P * i:P * i + P],
                                  bank(4 + i % 2, 0, 2 * P).rearrange("p (a t) -> p a t", a=2)) \
                        .then_inc(S("mp_ev"), 1)

                softmax_top(0)
                for u in range(16):
                    if u + 1 < 16:
                        softmax_top(u + 1)
                    softmax_scale(u)
                    if u >= 6 and (u - 6) % 4 == 0:
                        result((u - 6) // 4)
                result(3)

            def mem_sample(l):
                dve.wait_ge(S("ms_r"), l + 1)
                link(v.tensor_reduce(mx[:, 0:1], bank(2, 0, ML), AX.X, ALU.max))
                v.tensor_scalar(nmx[:, 0:1], mx[:, 0:1], -1.0, None, ALU.mult).then_inc(S("ms_m"), 1)
                dve.wait_ge(S("ms_e"), l + 1)
                link(v.reciprocal(rsum[:, 0:1], esum[:, 0:1]))
                v.tensor_scalar(ml_r, ml_r, rsum[:, 0:1], None, ALU.mult).then_inc(S("ms_n"), 1)

            def residual(l):
                for j in range(20):
                    c, i = j // 5, j % 5
                    n = ROWS[i]
                    dve.wait_ge(S("wo_mm"), 20 * l + j + 1)
                    xc = X[0:n, i, 256 * c:256 * c + 256]
                    v.scalar_tensor_tensor(xc, xc, ALPHA, bank(4 + (20 * l + j) % 4, 0, 256, rows=(0, n)), ALU.mult,
                                           ALU.add).then_inc(S("wo_ev"), 1)
                dve.wait_ge(S("wo_ev"), 20 * (l + 1))

            def norm(p):
                for i in range(NT):
                    n = ROWS[i]
                    for half in range(2):
                        ins = v.bn_stats(stats[0:n, i, 6 * half:6 * half + 6], X[0:n, i, 512 * half:512 * half + 512])
                    link(ins)
                    ins = v.bn_aggr(mv[0:n, i, :], stats[0:n, i, :])
                ins.then_inc(S("ln_st"), 1)
                dve.wait_ge(S("ln_sd"), p + 1)
                link(v.reciprocal(rstd, rstd))
                for i in range(NT):
                    n = ROWS[i]
                    v.tensor_scalar(X[0:n, i], X[0:n, i], mv[0:n, i, 0:1], rstd[0:n, i:i + 1], ALU.subtract,
                                    ALU.mult).then_inc(S("ln_nm"), 1)

            def routing(l):
                dve.wait_ge(S("wo_mm"), 20 * (l + 1))
                dve.wait_ge(S("route_in"), 16 * 7 * (l + 1))
                link(v.memset(rl, 0.0))
                link(v.memset(rl[:, :, 4:8], NEG))
                for i in range(NT):
                    n = ROWS[i]
                    b = bank(2 + (NT * l + i) % 2, 0, NG + NE, rows=(0, n))
                    dve.wait_ge(S("rt_mm"), NT * l + i + 1)
                    link(v.tensor_tensor(rl[0:n, i, 0:NG], b[:, 0:NG], biasr[0:n, 0:NG], ALU.add))
                    v.tensor_tensor(rl[0:n, i, 8:], b[:, NG:], biasr[0:n, NG:], ALU.add).then_inc(S("rt_ev"), 1)
                dve.wait_ge(S("rt_ev"), NT * (l + 1))
                for i in range(NT):
                    link(v.max(gm[:, i, :], rl[:, i, 0:8]))
                    link(v.max_index(gi[:, 8 * i:8 * i + 8], gm[:, i, :], rl[:, i, 0:8]))
                giv = gi.rearrange("p (i q) -> p i q", q=8)
                link(v.tensor_copy(gf, giv[:, 0:NT, 0]))
                v.tensor_tensor(gexp, rl[:, :, 0:NG], bc(gm[:, :, 0:1], [P, NT, NG]), ALU.subtract) \
                    .then_inc(S("r_step"), 1)
                dve.wait_ge(S("r_step"), 4 * l + 2)
                link(v.tensor_reduce(gw, gexp, AX.X, ALU.add))
                link(v.reciprocal(gw, gw))
                iota = C("iota")
                link(v.tensor_tensor(ohg, bc(iota[:, 0:NG].unsqueeze(1), [P, NT, NG]),
                                     bc(gf.unsqueeze(2), [P, NT, NG]), ALU.is_equal))
                e4 = esw.rearrange("p (i g e) -> p i g e", i=NT, g=NG)
                link(v.tensor_tensor(e4, rl[:, :, 8:].rearrange("p i (g e) -> p i g e", g=NG),
                                     bc(ohg.unsqueeze(3), [P, NT, NG, EG]), ALU.mult))
                link(v.tensor_reduce(esel, e4.rearrange("p i g e -> p i e g"), AX.X, ALU.add))
                for i in range(NT):
                    link(v.max(em[:, i, :], esel[:, i, :]))
                    link(v.max_index(gi[:, 40 + 8 * i:48 + 8 * i], em[:, i, :], esel[:, i, :]))
                for j in range(2):
                    link(v.tensor_copy(ef[:, j, :], giv[:, NT:2 * NT, j]))
                    link(v.scalar_tensor_tensor(ef[:, j, :], gf, float(EG), ef[:, j, :], ALU.mult, ALU.add))
                v.tensor_tensor(tmpw, em[:, :, 1], em[:, :, 0], ALU.subtract).then_inc(S("r_step"), 1)
                dve.wait_ge(S("r_step"), 4 * l + 4)
                link(v.tensor_scalar(wj[:, 0, :], tmpw, 1.0, None, ALU.add))
                link(v.reciprocal(wj[:, 0, :], wj[:, 0, :]))
                link(v.tensor_tensor(wj[:, 0, :], wj[:, 0, :], gw, ALU.mult))
                link(v.tensor_tensor(wj[:, 1, :], wj[:, 0, :], tmpw, ALU.mult))
                oh4 = oh.rearrange("p (j i) e -> p j i e", j=2)
                efl = ef.rearrange("p j i -> p (j i)")
                link(v.tensor_tensor(oh, bc(iota[:, 0:NE].unsqueeze(1), [P, 10, NE]),
                                     bc(efl.unsqueeze(2), [P, 10, NE]), ALU.is_equal))
                link(v.memset(oh_t, 0.0))
                for j in range(2):
                    link(v.tensor_tensor(oh4[:, j], oh4[:, j], bc(C("valid").unsqueeze(2), [P, NT, NE]), ALU.mult))
                v.tensor_tensor(cnt, oh4[:, 0], oh4[:, 1], ALU.add).then_inc(S("onehot"), 1)
                dve.wait_ge(S("rank_mm"), l + 1)
                link(v.tensor_copy(rank.rearrange("p i e -> p (i e)"), bank(4, 0, NE * (NT + 1))))
                n4 = nxc.rearrange("p (e k) -> p e k", k=4)
                link(v.tensor_tensor(n4, bc(rank[:, NT, :].unsqueeze(2), [P, NE, 4]),
                                     bc(C("steps").unsqueeze(1), [P, NE, 4]), ALU.is_gt))
                link(v.tensor_reduce(nx, n4, AX.X, ALU.add))
                bc3 = big_cmp.rearrange("p (e f) -> p e f", e=NE)
                link(v.tensor_tensor(bc3, bc(iota[:, 0:NE].unsqueeze(1), [P, NE, NE]),
                                     bc(iota[:, 0:NE].unsqueeze(2), [P, NE, NE]), ALU.is_lt))
                link(v.tensor_tensor(bc3, bc(nx.unsqueeze(1), [P, NE, NE]), bc3, ALU.mult))
                link(v.tensor_reduce(xbase, bc3, AX.X, ALU.add))
                th4 = oh_t.rearrange("p (j i) e -> p j i e", j=2)
                for j in range(2):
                    link(v.tensor_tensor(th4[:, j], oh4[:, j], rank[:, 0:NT, :], ALU.mult))
                link(v.tensor_reduce(r10, oh_t, AX.X, ALU.add))
                link(v.tensor_tensor(oh_t, oh, bc(xbase.unsqueeze(1), [P, 10, NE]), ALU.mult))
                link(v.tensor_reduce(x10, oh_t, AX.X, ALU.add))
                link(v.tensor_scalar(b10, x10, float(P), float(PAIRS * P - SLOTS), ALU.mult, ALU.add))
                link(v.scalar_tensor_tensor(b10, efl, -float(SLOTS), b10, ALU.mult, ALU.add))
                link(v.scalar_tensor_tensor(b10, r10, float(SLOTS), b10, ALU.is_ge, ALU.mult))
                link(v.scalar_tensor_tensor(p10, efl, float(SLOTS), b10, ALU.mult, ALU.add))
                link(v.tensor_tensor(p10, p10, r10, ALU.add))
                if l:
                    dve.wait_ge(S("yg_in"), 16 * 10)
                link(v.tensor_copy(pos_i, p10))
                link(v.tensor_scalar(ib[0], pos_i, P - 1, None, ALU.bitwise_and))
                link(v.tensor_scalar(ib[1], pos_i, 7, None, ALU.logical_shift_right))
                link(v.tensor_copy(s10, ib[0]))
                link(v.tensor_copy(b10, ib[1]))
                link(v.tensor_tensor(a1, bc(iota.unsqueeze(1), [P, 10, P]), bc(s10.unsqueeze(2), [P, 10, P]),
                                     ALU.is_equal))
                link(v.tensor_tensor(bt, bc(iota[:, 0:NE].unsqueeze(1), [P, 10, NE]),
                                     bc(b10.unsqueeze(2), [P, 10, NE]), ALU.is_equal))
                bt4 = bt.rearrange("p (j i) e -> p j i e", j=2)
                for j in range(2):
                    link(v.tensor_tensor(bt4[:, j], bt4[:, j], bc(C("valid").unsqueeze(2), [P, NT, NE]), ALU.mult))
                for j, dst in enumerate((bb, bb2)):
                    link(v.tensor_tensor(dst[:, :, 0:NE], bt4[:, j], bc(C("token").unsqueeze(2), [P, NT, NE]),
                                         ALU.mult))
                    link(v.tensor_tensor(dst[:, :, NE:], bt4[:, j], bc(wj[:, j, :].unsqueeze(2), [P, NT, NE]),
                                         ALU.mult))
                v.tensor_copy(r10, r10).then_inc(S("places"), 1)
                link(v.tensor_tensor(xbase, xbase, nx, ALU.add))
                li3 = big_cmp[:, 0:MORE * NE].rearrange("p (x e) -> p x e", x=MORE)
                link(v.tensor_tensor(li3, bc(xbase.unsqueeze(1), [P, MORE, NE]),
                                     bc(iota[:, 0:MORE].unsqueeze(2), [P, MORE, NE]), ALU.is_le))
                link(v.tensor_reduce(lf[:, 0:MORE], li3, AX.X, ALU.add))
                link(v.tensor_scalar(lf[:, 0:MORE], lf[:, 0:MORE], float(NE - 1), None, ALU.min))
                link(v.tensor_copy(lf[:, MORE:], xbase[:, NE - 1:NE]))
                v.tensor_copy(lists, lf).then_inc(S("lists"), 1)
                dve.wait_ge(S("slot_mm"), l + 1)
                link(v.tensor_copy(wslot, bank(5, NE, 2 * NE)))
                dve.wait_ge(S("lists"), l + 1)
                v.tensor_copy(slot_tok, bank(5, 0, NE)).then_inc(S("slots"), 1)

            def experts(l):
                s = l * PAIRS
                with dve.Fori(0, PAIRS) as i:
                    for j in range(2):
                        dve.wait_ge(S("gate"), i * 2 + (2 * s + j + 1))
                        v.tensor_tensor(hid[:, j].rearrange("p f n -> p (f n)"), bank(j, 2 * SLOTS, 4 * SLOTS),
                                        sg[:, j, :], ALU.mult).then_inc(S("hid"), 1)
                more = dve.value_load(lists[0:1, 16:17], min_val=0, max_val=MORE)
                with dve.If(more > 0):
                    with dve.Fori(0, more) as x:
                        dve.wait_ge(S(f"more_step{l}"), x * 9 + 6)
                        v.tensor_tensor(hidx.rearrange("p f n -> p (f n)"), bank(0, 2 * P, 4 * P),
                                        sgx.rearrange("p f n -> p (f n)"), ALU.mult).then_inc(S(f"more_step{l}"), 1)

            def combine(l):
                for i in range(NT):
                    n = ROWS[i]
                    dve.wait_ge(S("yg_in"), 32 * (NT * l + i + 1))
                    link(v.scalar_tensor_tensor(X[0:n, i], X[0:n, i], ALPHA, yg[0:n, 0], ALU.mult, ALU.add))
                    v.tensor_tensor(X[0:n, i], X[0:n, i], yg[0:n, 1], ALU.add).then_inc(S("yg_used"), 1)
                dve.wait_ge(S("yg_used"), NT * (l + 1))

            v.memset(eps_ln, LN_EPS)
            v.memset(eps_hn, HN_EPS)
            v.memset(hmv, 1.0)
            v.memset(mv, 1.0)
            v.memset(hrs, 1.0)
            v.memset(ints[:, 16:], 0)
            link(v.memset(fz, 0.0))
            dve.wait_ge(S("tables"), 64)
            dve.wait_ge(S("inputs"), 48)
            for h in range(2 * RH):
                t = 2 * (h // RH)
                src = ps[:, 1024 * (h % 2):1024 * (h % 2) + TOK]
                dve.wait_ge(S("rope_mm"), h + 1)
                v.tensor_tensor(ropeA, src, rope_v[:, t, :], ALU.mult)
                v.tensor_tensor(ropeB[0:64], src[64:128], rope_v[64:128, t + 1, :], ALU.mult)
                link(v.tensor_tensor(ropeB[64:128], src[0:64], rope_v[0:64, t + 1, :], ALU.mult))
                ins = v.tensor_tensor((qT if h < RH else kT)[:, h % RH, :], ropeA, ropeB, ALU.add)
                ins.then_inc(S("rope_ev"), 1)
                dve.wait_ge(S("rope_ev"), h + 1)
            lg = np.log(np.float32(1) - np.float32(2) ** (np.float32(-5) - np.arange(RH, dtype=np.float32)))
            g_chunk = [float(x) for x in np.exp(lg.astype(np.float32) * np.float32(P))]
            g_step = [float(x) for x in np.exp(lg.astype(np.float32) * np.float32(DS))]

            def decayed(u):
                n, h = u // RH, u % RH
                if u >= 2:
                    dve.wait_ge(S("rr"), u - 1)
                if n:
                    v.tensor_tensor(qd[:, u % 2, :], qT[:, h, P * n:P * n + P], C("qdecay")[:, P * h:P * h + P],
                                    ALU.mult)
                dve.wait_ge(S("rsc"), u + 1)
                v.tensor_tensor(scm[:, u % 2, :], bank(u % 2, 0, P), C("decay")[:, P * h:P * h + P], ALU.mult) \
                    .then_inc(S("rsm"), 1)

            dve.wait_ge(S("zero_out"), 16 * MORE)
            decayed(0)
            for u in range(4 * RH):
                n, h = u // RH, u % RH
                if u + 1 < 4 * RH:
                    decayed(u + 1)
                dve.wait_ge(S("rcp"), u + 1)
                v.bn_stats(hstats[:, h, :], R[:, n, P * h:P * h + P]).then_inc(S("rbs"), 1)
                dve.wait_ge(S("rbs"), u + 1)
                v.bn_aggr(hmv[:, u, :], hstats[:, h, :])
                dve.wait_ge(S("rkv"), u + 1)
                kv = bank(6 + u % 2, 0, P)
                if n == 0:
                    v.tensor_copy(state_p[:, h, :], kv).then_inc(S("rst"), 1)
                else:
                    v.scalar_tensor_tensor(state_p[:, h, :], state_p[:, h, :], g_chunk[h], kv, ALU.mult, ALU.add) \
                        .then_inc(S("rst"), 1)
            for h in range(RH):
                b = h % 2
                if h >= 2:
                    dve.wait_ge(S("rr"), 24 + h - 1)
                v.tensor_tensor(qds[:, b, :], qT[:, h, SEQ:TOK], C("qdecay_s")[:, NS * h:NS * h + NS], ALU.mult)
                dve.wait_ge(S("rsc"), 24 + h + 1)
                v.tensor_tensor(scs[0:NS, b, :], bank(b, 0, NS, rows=(0, NS)),
                                C("decay_s", NS)[:, NS * h:NS * h + NS], ALU.mult)
                if h:
                    dve.wait_ge(S("rkv"), 24 + h)
                v.tensor_tensor(vbd[0:NS].rearrange("p (b e) -> p b e", b=DB),
                                bc(V[0:NS, ST, P * h:P * h + P].unsqueeze(1), [NS, DB, P]),
                                bc(C("kdecay_s", NS)[:, DB * h:DB * h + DB].unsqueeze(2), [NS, DB, P]), ALU.mult) \
                    .then_inc(S("rsm"), 1)
                dve.wait_ge(S("rkv"), 24 + h + 1)
                v.scalar_tensor_tensor(st_s[:, b, :], st_s[:, b, :], g_step[h], ps[:, 3072:4096], ALU.mult, ALU.add) \
                    .then_inc(S("rst"), 1)
            dve.wait_ge(S("srow"), 1)
            for h in range(RH):
                link(v.bn_stats(hstats[0:NS, h, :], R[0:NS, ST, P * h:P * h + P]))
                ins = v.bn_aggr(hmv[0:NS, 24 + h, :], hstats[0:NS, h, :])
            ins.then_inc(S("hmv"), 1)
            dve.wait_ge(S("hsd"), 1)
            dve.wait_ge(S("rcp"), 24)
            link(v.reciprocal(hrs, hrs))
            for i in range(NT):
                n = ROWS[i]
                for h in range(RH):
                    r = R[0:n, i, P * h:P * h + P]
                    q = RH * i + h
                    ins = v.tensor_scalar(r, r, hmv[0:n, q, 0:1], hrs[0:n, q:q + 1], ALU.subtract, ALU.mult)
                link(ins)
                v.tensor_tensor(R[0:n, i], R[0:n, i], G[0:n, i], ALU.mult).then_inc(S("gated"), 1)
            mem_prompt(0)
            mem_sample(0)
            residual(0)
            norm(0)
            routing(0)
            experts(0)
            combine(0)
            norm(1)

            dve.wait_ge(S("tm_ev"), 45)
            link(v.tensor_tensor(fz, fz, bc(bf_b.unsqueeze(1), [P, NT, FH]), ALU.add))
            link(v.tensor_scalar(fe, fz, -1.0, None, ALU.mult))
            v.tensor_tensor(fe, fe, fz, ALU.max).then_inc(S("f_step"), 1)
            dve.wait_ge(S("f_step"), 2)
            v.tensor_scalar(fe, fe, 1.0, None, ALU.add).then_inc(S("f_step"), 1)
            dve.wait_ge(S("f_step"), 4)
            v.scalar_tensor_tensor(logf, fz, 0.0, fe, ALU.min, ALU.subtract).then_inc(S("logf"), 1)
            dve.wait_ge(S("cum"), 1)
            v.tensor_copy(cq[:, 0:ST, :], bank(4, 0, FH * ST).rearrange("p (i h) -> p i h", i=ST))
            link(v.tensor_copy(cq[0:NS, ST, :], bank(4, FH * ST, FH * NT, rows=(0, NS))))
            v.tensor_scalar(negc[:, 0:ST, :], cq[:, 0:ST, :], -1.0, None, ALU.mult)
            v.tensor_scalar(negc[0:NS, ST, :], cq[0:NS, ST, :], -1.0, None, ALU.mult)
            for hh in range(4):
                v.tensor_copy(cqs[NS * hh:NS * hh + NS, :], cq[0:NS, ST, hh::4])
            v.tensor_copy(ckp.rearrange("p g c -> p (g c)"), bank(5, 0, PG * DB * FH)).then_inc(S("cum_ev"), 1)

            def prompt_top(s):
                h, i = 2 * (s // 8) + s % 2, (s // 2) % 4
                w, q = P * (i + 1), s % 4
                row = fpr[:, s % 2, 0:w]
                dve.wait_ge(S("fp_l"), s + 1)
                if s >= 2:
                    dve.wait_ge(S("fp_t"), s - 1)
                if i == 0:
                    dve.wait_ge(S("fnb_cp"), h + 1)
                v.scalar_tensor_tensor(row, bank(s % 2, 0, w), cq[:, i, h:h + 1], fnb[:, h % 2, 0:w], ALU.add,
                                       ALU.add).then_inc(S("fp_s"), 1)
                dve.wait_ge(S("fp_s"), s + 1)
                link(v.tensor_tensor(row[:, w - P:w], row[:, w - P:w], C("causal"), ALU.add))
                link(v.tensor_reduce(mx[:, q:q + 1], row, AX.X, ALU.max))
                v.tensor_scalar(nmx[:, q:q + 1], mx[:, q:q + 1], -1.0, None, ALU.mult).then_inc(S("fp_m"), 1)

            def prompt_scale(s):
                i = (s // 2) % 4
                w, q = P * (i + 1), s % 4
                dve.wait_ge(S("fp_e"), s + 1)
                link(v.reciprocal(rsum[:, q:q + 1], esum[:, q:q + 1]))
                v.tensor_scalar(fpr[:, s % 2, 0:w], fpr[:, s % 2, 0:w], rsum[:, q:q + 1], None, ALU.mult) \
                    .then_inc(S("fp_n"), 1)

            def prompt_result(t):
                dve.wait_ge(S("fox_p"), 2 * t + 2)
                v.tensor_copy(MX[:, t // 4, P * (t % 4):P * (t % 4) + P], bank(4 + t % 2, 0, P)) \
                    .then_inc(S("fp_ev"), 1)

            prompt_top(0)
            for s in range(48):
                if s + 1 < 48:
                    prompt_top(s + 1)
                prompt_scale(s)
                if s >= 4 and s % 2 == 0:
                    prompt_result((s - 4) // 2)
            for t in (22, 23):
                prompt_result(t)
            dve.wait_ge(S("fs_new"), 1)
            for g in range(PG):
                for r in range(2):
                    ins = v.tensor_tensor(
                        fl_t[:, g, r::2, :].rearrange("p h (b t) -> p h b t", t=DS),
                        bank(2 * g + r, 0, 6 * NS).rearrange("p (h b t) -> p h b t", h=6, t=DS),
                        bc(ckp[:, g, :].rearrange("p (b h) -> p h b", h=FH)[:, r::2, :].unsqueeze(3), [P, 6, DB, DS]),
                        ALU.subtract)
                ins.then_inc(S("fs_lt"), 1)
            for hh in range(4):
                rr = (NS * hh, NS * hh + NS)
                ins = v.tensor_tensor(fl_r[rr[0]:rr[1], :, PG * PAGE:],
                                      bank(4 + hh % 2, 0, 3 * NS, rows=rr).rearrange("p (r t) -> p r t", r=3),
                                      bc(C("causal_s")[rr[0]:rr[1]].unsqueeze(1), [NS, 3, NS]), ALU.add)
            link(ins)
            for r in range(3):
                dve.wait_ge(S("fs_r"), r + 1)
                v.tensor_scalar(fl_r[:, r, 0:PG * PAGE], bank(6, 0, PG * PAGE), cqs[:, r:r + 1], None, ALU.add) \
                    .then_inc(S("fs_lr"), 1)
                link(v.tensor_scalar(fl_r[:, r, PG * PAGE:], fl_r[:, r, PG * PAGE:], cqs[:, r:r + 1], None, ALU.add))
                link(v.tensor_reduce(mx[:, r:r + 1], fl_r[:, r, :], AX.X, ALU.max))
                v.tensor_scalar(nmx[:, r:r + 1], mx[:, r:r + 1], -1.0, None, ALU.mult).then_inc(S("fs_m"), 1)
            for r in range(3):
                dve.wait_ge(S("fs_e"), r + 1)
                link(v.reciprocal(rsum[:, r:r + 1], esum[:, r:r + 1]))
                v.tensor_scalar(fl_r[:, r, :], fl_r[:, r, :], rsum[:, r:r + 1], None, ALU.mult) \
                    .then_inc(S("fs_n"), 1)
            mem_prompt(1)
            mem_sample(1)
            residual(1)
            norm(2)
            routing(1)
            experts(1)
            combine(1)
            norm(3)


_INS = ['x_prompt', 'x_sample', 'mem_prompt', 'state_ret', 'cache_fox_k', 'cache_fox_v', 'cache_fox_logf',
        'cache_mem_k', 'cache_mem_v', 'page_table', 'w_in_a', 'w_in_b', 'w_kv_shared', 'b_forget', 'w_o', 'w_mem_kv',
        'ln1_g', 'ln1_b', 'ln2_g', 'ln2_b', 'w_group', 'b_group', 'w_route', 'b_route', 'w_up', 'w_down']
_OUTS = [(1, SEQ, D), (DB, DS, D), (1, 1, RH, RD, RD), (1, DB, RH, RD, RD), (1, SEQ, FH, FD), (1, SEQ, FH, FD),
         (1, SEQ, FH), (DB, DS, FH, FD), (DB, DS, FH, FD), (DB, DS, FH), (LAYERS, 1, ML, MH, MD),
         (LAYERS, 1, ML, MH, MD)]


def kernel(**inputs):
    import concourse.bacc as _bacc
    from concourse.bass_utils import run_bass_kernel_spmd as _run

    nc = _bacc.Bacc("TRN2", target_bir_lowering=False, num_devices=1)
    consts, rope = shape_constants()
    given = [(n, np.ascontiguousarray(inputs[n])) for n in _INS] + [("consts", consts), ("rope", rope)]
    arrays, args = {}, []
    for name, a in given:
        arrays[f"in_{name}_dram"] = a
        args.append(nc.dram_tensor(f"in_{name}_dram", a.shape, mybir.dt.from_np(a.dtype), kind="ExternalInput").ap())
    outs = [nc.dram_tensor(f"out_{i}_dram", s, F32, kind="ExternalOutput").ap() for i, s in enumerate(_OUTS)]
    build(nc, *args, outs)
    r = _run(nc, [arrays], core_ids=[0])
    return tuple(r.results[0][f"out_{i}_dram"] for i in range(len(_OUTS)))
```

```python
from contextlib import ExitStack

import numpy as np

import concourse.bass as bass
from concourse import mybir

F32 = mybir.dt.float32
I32 = mybir.dt.int32
U32 = mybir.dt.uint32
ALU = mybir.AluOpType
ACT = mybir.ActivationFunctionType
AX = mybir.AxisListType

P = 128
D = 1024
KD = D // P
SEQ, DB, DS = 512, 8, 4
NS = DB * DS
NT = SEQ // P + 1
ST = NT - 1
ROWS = [P] * ST + [NS]
TOK = SEQ + NS
LAYERS = 2
RH, RD = 6, 128
RW = RH * RD
FH, FD = 12, 64
FW = FH * FD
MH, MD, ML = 4, 64, 256
MW = MH * MD
PG, PAGE = 2, 128
NG, EG = 4, 8
NE = NG * EG
DE = 256
ALPHA = float(np.float32((2 * LAYERS) ** 0.25))
LN_EPS, HN_EPS = 1e-5, 1e-6
SLOTS = 64
PAIRS = NE // 2
MORE = 16
STEPS = [SLOTS + P * k for k in range(4)]
NEG = -1.0e30

CONST = {}
CW = 0
for _name, _w in (("ident", P), ("tri", P), ("strict", P), ("ones", P), ("iota", P), 
                  ("decay", RH * P), ("qdecay", RH * P), ("kdecay", RH), ("decay_s", RH * NS), ("qdecay_s", RH * NS),
                  ("kdecay_s", RH * DB), ("causal", P), ("causal_s", NS), ("tri_s", NS), ("batch_s", 60),
                  ("token", NT), ("valid", NT), ("steps", 4)):
    CONST[_name] = (CW, CW + _w)
    CW += _w


def shape_constants():
    f = np.float32
    c = np.zeros((P, CW), f)

    def put(name, a):
        lo, hi = CONST[name]
        a = np.asarray(a, f)
        c[:a.shape[0], lo:hi] = a.reshape(a.shape[0], hi - lo)

    i = np.arange(P)
    t = np.arange(NS)
    lg = np.log(f(1.0) - f(2.0) ** (f(-5.0) - np.arange(RH, dtype=f))).astype(f)

    def power(h, n):
        return np.exp((lg[h] * np.asarray(n, f)).astype(f)).astype(f)

    put("ident", np.eye(P))
    put("tri", i[:, None] <= i[None, :])
    put("strict", i[:, None] < i[None, :])
    put("ones", np.ones((P, P)))
    put("iota", np.tile(i, (P, 1)))
    diff = i[None, :] - i[:, None]
    put("decay", np.stack([np.where(diff >= 0, power(h, np.maximum(diff, 0)), 0) for h in range(RH)], 1))
    put("qdecay", np.stack([np.tile(power(h, i + 1), (P, 1)) for h in range(RH)], 1))
    put("kdecay", np.stack([power(h, P - 1 - i) for h in range(RH)], 1))
    same = (t[:, None] // DS) == (t[None, :] // DS)
    ds = t[None, :] - t[:, None]
    put("decay_s", np.stack([np.where(same & (ds >= 0), power(h, np.maximum(ds, 0)), 0) for h in range(RH)], 1))
    put("qdecay_s", np.stack([np.tile(power(h, t % DS + 1), (P, 1)) for h in range(RH)], 1))
    put("kdecay_s", np.stack([np.where((t[:, None] // DS) == np.arange(DB)[None, :],
                                       power(h, DS - 1 - t % DS)[:, None], 0) for h in range(RH)], 1))
    put("causal", np.where(i[None, :] <= i[:, None], 0, NEG))
    put("causal_s", np.tile(np.where(same & (ds <= 0), 0, NEG), (4, 1)))
    put("tri_s", same & (ds >= 0))
    b = np.zeros((P, 60), f)
    b[:, 28:32] = 1
    put("batch_s", b)
    put("token", i[:, None] + P * np.arange(NT)[None, :])
    put("valid", i[:, None] < np.array(ROWS)[None, :])
    put("steps", np.tile(np.array(STEPS), (P, 1)))
    pos = np.concatenate([np.arange(SEQ), PG * PAGE + t % DS]).astype(f)
    half = RD // 2
    inv = (f(10000.0) ** (-np.arange(half, dtype=f) / f(half))).astype(f)
    ang = (inv[:, None] * pos[None, :]).astype(f)
    cos, sin = np.cos(ang).astype(f), np.sin(ang).astype(f)
    ks = f(RD ** -0.5)
    cs, sn = np.concatenate([cos, cos]), np.concatenate([sin, -sin])
    rope = np.concatenate([cs, sn, cs * ks, sn * ks], axis=1).astype(f)
    return c, rope


def build(nc, x_prompt, x_sample, mem_prompt, state_ret, cache_fox_k, cache_fox_v, cache_fox_logf, cache_mem_k,
          cache_mem_v, page_table, w_in_a, w_in_b, w_kv_shared, b_forget, w_o, w_mem_kv, ln1_g, ln1_b, ln2_g, ln2_b,
          w_group, b_group, w_route, b_route, w_up, w_down, consts, rope, outs):
    (y_prompt, y_sample, ret_prompt, ret_sample, fox_k_p, fox_v_p, fox_f_p, fox_k_s, fox_v_s, fox_f_s,
     mem_k_p, mem_v_p) = outs
    ctx = ExitStack()
    sems = {}

    def S(name):
        if name not in sems:
            sems[name] = ctx.enter_context(nc.semaphore(name))
        return sems[name]

    with ctx:
        def sb(name, w, dt=F32):
            return ctx.enter_context(nc.sbuf_tensor(name, [P, w], dt))

        x_rows_t, x_cols_t, mix_t = sb("x_rows", NT * D), sb("x_cols", KD * TOK), sb("mix_cols", KD * TOK)
        const_t = sb("const", CW)
        big = sb("expert_weights", 4 * 3072)
        ring = sb("weight_ring", 3 * 3072)
        work = sb("work", 2 * NT * RW)
        mem_kv_t, mem_kt_t = sb("mem_kv", 2 * 2 * 512), sb("mem_kt", 2 * 2 * ML)
        ln_t = sb("ln_gb", 2 * D)
        small = sb("small", 1100)
        ints = sb("ints", 200, I32)
        index_t = sb("max_index", 10 * 8, U32)
        ps = ctx.enter_context(nc.psum_tensor("ps", [P, 8 * 512], F32))
        xs = [nc.dram_tensor(f"stream_rows{l}", [TOK, D], F32, kind="Internal").ap() for l in range(LAYERS)]
        ys_all = nc.dram_tensor("expert_rows", [(PAIRS + MORE) * P, D], F32, kind="Internal").ap()
        ys = [ys_all, ys_all]

        def view(t, at, *shape, rows=(0, P)):
            n = int(np.prod(shape))
            v = t[rows[0]:rows[1], at:at + n]
            if len(shape) == 2:
                v = v.rearrange("p (a b) -> p a b", a=shape[0])
            elif len(shape) == 3:
                v = v.rearrange("p (a b c) -> p a b c", a=shape[0], b=shape[1])
            return v

        def C(name, rows=P):
            lo, hi = CONST[name]
            return const_t[0:rows, lo:hi]

        def bank(b, lo=0, hi=512, rows=(0, P)):
            return ps[rows[0]:rows[1], b * 512 + lo:b * 512 + hi]

        X = view(x_rows_t, 0, NT, D)
        XT = view(x_cols_t, 0, KD, TOK)
        MX = view(mix_t, 0, KD, TOK)
        ident = C("ident")
        memkv = view(mem_kv_t, 0, 2, 2, 512)
        memkt = view(mem_kt_t, 0, 2, 2, ML)
        qT = view(big, 0, 6, TOK)
        kT = view(big, 6 * TOK, 6, TOK)
        V = view(big, 12 * TOK, NT, RW)
        free0 = 12 * TOK + NT * RW
        state_p = view(big, free0, RH, P)
        scm = view(big, free0 + 768, 2, P)
        kd = view(big, free0 + 1024, 2, P)
        qd = view(big, free0 + 1280, 2, P)
        qds = view(big, free0 + 1536, 2, NS)
        scs = view(big, free0 + 1600, 2, NS)
        kds = view(big, free0 + 1664, P)
        zeros = view(big, free0, D)
        assert free0 + 1792 <= 4 * 3072
        R = view(work, 0, NT, RW)
        G = view(work, NT * RW, NT, RW)
        rope_v = view(work, 0, 4, TOK)
        mem_rows = view(work, NT * RW, 2, D)
        ropeA = view(mix_t, 0, TOK)
        ropeB = view(mix_t, TOK, TOK)
        memT = view(mix_t, 2 * TOK, KD, ML)
        st_s = view(mix_t, 0, 2, DB * P)
        vbd = view(mix_t, 2048, DB * P)
        rTs = view(mix_t, 3072, RH, NS)
        at = [0]

        def sm(*shape):
            v = view(small, at[0], *shape)
            at[0] += int(np.prod(shape))
            assert at[0] <= 900
            return v

        stats, mv, rstd = sm(NT, 12), sm(NT, 2), sm(NT)
        hstats, hmv, hrs = sm(RH, 6), sm(NT * RH, 2), sm(NT * RH)
        mx, nmx, esum, rsum = sm(4), sm(4), sm(4), sm(4)
        mx2, nmx2, esum2, rsum2 = sm(2, 4), sm(2, 4), sm(2, 4), sm(2, 4)
        logf = sm(NT, FH)
        cq, negc = sm(NT, FH), sm(NT, FH)
        fz, fe = sm(NT, FH), sm(NT, FH)
        cqs = sm(3)
        past_f = sm(PG, DB * FH)
        bf_b = sm(FH)
        biasr = sm(NG + NE)
        eps_ln, eps_hn = sm(1), sm(1)
        wslot = sm(PAIRS + MORE)
        pages = ints[:, 0:16]
        slot_tok = ints[:, 16:16 + 32]
        pos_i = ints[:, 48:58]
        lists = ints[:, 64:64 + 17]
        idx_now = ints[:, 96:97]
        ib = [ints[:, 100 + 10 * k:110 + 10 * k] for k in range(3)]

        def cols(w, lo, hi):
            return w[:, lo:hi].rearrange("(k p) n -> p k n", p=P)

        chunks = []
        for l in range(LAYERS):
            chunks += [(cols(w_mem_kv[l], 0, 256), ("mkv_mm", 4 * l + 2)),
                       (cols(w_mem_kv[l], 256, 512), ("mkv_mm", 4 * l + 4))]
        for n in range(4):
            chunks.append((cols(w_in_a[0], 384 * n, 384 * n + 384), ("rope_mm", 3 * n + 3)))
        for n in range(4):
            chunks.append((cols(w_in_a[0], 1536 + 384 * n, 1920 + 384 * n), ("tm_mm", 5 * n + 5)))
        chunks.append((cols(w_in_a[0], 3072, 3328), ("fm_mm", 2)))
        for n in range(4):
            chunks.append((cols(w_kv_shared, 384 * n, 384 * n + 384), ("tm_mm", 25 + 5 * n)))
        chunks.append((cols(w_kv_shared, 1536, 1548), ("tm_mm", 45)))
        chunks.append((cols(w_in_b[0], 0, 384), ("fm_mm", 5)))
        chunks.append((cols(w_in_b[0], 384, 768), ("fm_mm", 8)))
        chunks.append((cols(w_in_b[0], 768, 1024), ("fm_mm", 10)))
        CH_KV, CH_A, CH_S, CH_B, CH_END = 0, 4, 13, 18, 21

        def wslot_view(n):
            w = chunks[n][0].shape[-1]
            return view(ring, 3072 * (n % 3), KD, w)

        def chunk_ready(eng, n):
            eng.wait_ge(S(f"w_in{n % 3}"), 16 * (n // 3 + 1))

        wo_v = view(ring, 0, KD, D)
        wr = view(ring, KD * D, KD, NG + NE)

        WU = [view(big, 0, KD, 512), view(big, 4096, KD, 512), view(ring, 0, KD, 512), view(ring, 4096, KD, 512)]
        WD = [view(big, 8192, 2, D), view(big, 8192 + 2048, 2, D), view(mix_t, 0, 2, D), view(mix_t, 2048, 2, D)]
        xg, yb = view(work, 0, D), view(work, D, D)
        xgT = view(work, 2 * D, KD, P)
        sg = view(work, 3 * D, 2, P)
        hid = view(work, 3 * D + 256, 2, 2, SLOTS)
        sgx = view(work, 3 * D + 512, 2, P)
        hidx = view(work, 3 * D + 768, 2, P)
        yg = [view(work, 0, 2, D), view(mix_t, 0, 2, D)]
        RB = 0
        rl = view(work, RB, NT, 40)
        gm = view(work, 200, NT, 8)
        em = view(work, 240, NT, 8)
        esel = view(work, 280, NT, 8)
        gf = view(work, 320, NT)
        gexp = view(work, 325, NT, NG)
        gw = view(work, 345, NT)
        ohg = view(work, 350, NT, NG)
        ef = view(work, 370, 2, NT)
        wj = view(work, 380, 2, NT)
        tmpw = view(work, 390, NT)
        r10, x10, b10, s10, p10 = [view(work, 400 + 10 * k, 10) for k in range(5)]
        oh = view(work, 450, 10, NE)
        oh_t = view(work, 770, 10, NE)
        cnt = view(work, 1090, NT, NE)
        rank = view(work, 1250, NT + 1, NE)
        nx, xbase = view(work, 1442, NE), view(work, 1474, NE)
        big_cmp = view(work, 1506, NE * NE)
        a1 = view(work, 2530, 10, P)
        bb = view(work, 3810, 5, 64)
        assert 3810 + 320 <= 6144
        bb2 = view(work, 6656, 5, 64)
        esw = view(work, 6976, NT * NG * EG)
        nxc = view(work, 7136, NE * 4)
        lf = view(work, 7264, 17)
        bt = view(work, 7296, 10, NE)
        gi = index_t[:, :]

        mvc = view(work, 0, DB, 2 * MW)
        mkc = [view(work, 4096, 2, MW), view(work, 4608, 2, MW)]
        mkcT = view(work, 5120, 2, 2, P)
        ml_t = view(work, 5632, 2, 4, NS)
        ml_r = view(work, 5888, ML)
        mp_s = view(work, 6144, 2, P)
        mpr = view(work, 6400, 2, ML)
        mprT = view(work, 6912, 2, ML)
        k_rows = view(work, NT * RW, NT, FW)
        fpr = [view(work, 4 * SEQ * k, ST, SEQ) for k in range(2)]
        fdiag = [view(work, 4 * SEQ * k, ST, SEQ + P)[:, :, 0:P] for k in range(2)]
        fprT = view(work, 8 * SEQ, 2, 10 * P)
        fnb = view(work, 8 * SEQ + 20 * P, 2, SEQ)
        PT_AT = {3: 0, 2: 4 * P, 0: 7 * P, 1: 8 * P}
        LOGIT_AT = {1: (0, 0), 0: (1, 0), 2: (1, P), 3: (2, 0)}
        o_rows = view(x_cols_t, 0, ST, FW)
        pages_at = [view(ring, FW * n, FW) for n in range(12)] + [view(big, free0 + FW * n, FW) for n in range(2)] \
            + [view(x_cols_t, ST * FW, FW)]
        fkc = pages_at + [view(mix_t, 0, FW)]
        fvc = pages_at + [view(work, FW, FW)]
        qbd = view(x_cols_t, (ST + 1) * FW, 6, 2, NS)
        fkT = [view(work, 3072, 6, P), view(work, 6624, 6, P)]
        fl_t = view(work, 3840, PG, FH, NS)
        FLW = PG * PAGE + NS
        fl_r = view(work, 4608, 3, FLW)
        fs_p = view(work, 5472, 3, 3, P)
        mqT = MX[:, 6:8]
        ckp = view(small, 900, PG, DB * FH)

        block = ctx.enter_context(nc.Block())

        @block.sync
        def _(sp):
            sp.dma_start(const_t[:, :], consts).then_inc(S("inputs"), 16)
            sp.dma_start(X[:, 0:ST, :], x_prompt[0].rearrange("(t p) d -> p t d", p=P)).then_inc(S("inputs"), 16)
            sp.dma_start(X[0:NS, ST, :], x_sample.rearrange("b t d -> (b t) d")).then_inc(S("inputs"), 16)
            sp.dma_start(mem_rows, mem_prompt[0].rearrange("(t p) d -> p t d", p=P)).then_inc(S("tables"), 16)
            sp.dma_start(view(work, 0, 4 * TOK), rope).then_inc(S("tables"), 16)
            sp.dma_start(bf_b, b_forget.rearrange("(a h) -> a h", a=1).partition_broadcast(P)).then_inc(S("tables"), 16)
            sp.dma_start(pages[0:1, :], page_table.rearrange("b g -> (b g)").rearrange("(a n) -> a n", a=1)) \
                .then_inc(S("tables"), 16)

            def chunk(n):
                if n >= 3:
                    sp.wait_ge(S(chunks[n - 3][1][0]), chunks[n - 3][1][1])
                sp.dma_start(wslot_view(n), chunks[n][0]).then_inc(S(f"w_in{n % 3}"), 16)

            def ln_params(p):
                if p:
                    sp.wait_ge(S("x_ready"), NT * p)
                g, b = ((ln1_g, ln1_b), (ln2_g, ln2_b))[p % 2]
                sp.dma_start(ln_t[:, 0:D], g[p // 2:p // 2 + 1, :].partition_broadcast(P)).then_inc(S("ln_in"), 16)
                sp.dma_start(ln_t[:, D:2 * D], b[p // 2:p // 2 + 1, :].partition_broadcast(P)).then_inc(S("ln_in"), 16)

            def output_weights(l):
                sp.wait_ge(S("fm_mm"), 2 if l == 0 else 10)
                if l:
                    sp.wait_ge(S("tok_done"), 2)
                for half in range(2):
                    sp.dma_start(wo_v[:, :, 512 * half:512 * half + 512], cols(w_o[l], 512 * half, 512 * half + 512)) \
                        .then_inc(S("wo_in"), 16)
                s = S("route_in")
                sp.dma_start(wr[:, :, 0:NG], w_group[l].rearrange("(k p) g -> p k g", p=P)).then_inc(s, 16)
                for g in range(NG):
                    sp.dma_start(wr[:, :, NG + EG * g:NG + EG * g + EG],
                                 w_route[l, g].rearrange("(k p) e -> p k e", p=P)).then_inc(s, 16)
                sp.dma_start(biasr[:, 0:NG], b_group[l:l + 1, :].partition_broadcast(P)).then_inc(s, 16)
                sp.dma_start(biasr[:, NG:], b_route[l:l + 1].rearrange("a g e -> a (g e)").partition_broadcast(P)) \
                    .then_inc(s, 16)

            def mem_cache(l):
                sp.wait_ge(S("tok_done"), l + 1)
                for b in range(DB):
                    if b >= 2:
                        sp.wait_ge(S("mk_tr"), 8 * l + b - 1)
                    sp.dma_start(mkc[b % 2], cache_mem_k[l, b].rearrange("(t p) h d -> p t (h d)", p=P)) \
                        .then_inc(S(f"mk_in{b % 2}"), 16)
                    sp.dma_start(mvc[:, b], cache_mem_v[l, b].rearrange("(t p) h d -> p t (h d)", p=P)) \
                        .then_inc(S("mv_in"), 16)

            def expert(l, e, b):
                sp.dma_start(WU[b], w_up[l].rearrange("g e (k p) f -> p (g e) k f", p=P)[:, bass.ds(e, 1)]
                             .rearrange("p a k f -> p (a k) f")).then_inc(S(f"exp_in{b}"), 16)
                sp.dma_start(WD[b], w_down[l].rearrange("g e (k p) f -> p (g e) k f", p=P)[:, bass.ds(e, 1)]
                             .rearrange("p a k f -> p (a k) f")).then_inc(S(f"exp_in{b}"), 16)

            def experts(l):
                sp.wait_ge(S("tok_done"), l + 1)
                if l == 0:
                    sp.wait_ge(S("rs_out"), 16)
                else:
                    sp.wait_ge(S("kv_out"), 64)
                for b in range(2):
                    expert(l, b, b)
                sp.wait_ge(S("rt_mm"), NT * (l + 1))
                for b in range(2, 4):
                    expert(l, b, b)
                ln_params(2 * l + 1)
                with sp.Fori(1, NE // 4) as r:
                    for b in range(4):
                        sp.wait_ge(S("down_done"), r * 4 + (NE * l + b - 3))
                        expert(l, r * 4 + b, b)
                sp.wait_ge(S("lists"), l + 1)
                more = sp.value_load(lists[0:1, 16:17], min_val=0, max_val=MORE)
                with sp.If(more > 0):
                    with sp.Fori(0, more) as x:
                        sp.wait_ge(S(f"more_step{l}"), x * 9 + 1)
                        e = sp.value_load(lists[0:1, bass.ds(x, 1)], min_val=0, max_val=NE - 1)
                        sp.dma_start(WU[0], w_up[l].rearrange("g e (k p) f -> p (g e) k f", p=P)
                                     [:, bass.ds(e, 1)].rearrange("p a k f -> p (a k) f")) \
                            .then_inc(S(f"more_w{l}"), 16)
                        sp.dma_start(WD[0], w_down[l].rearrange("g e (k p) f -> p (g e) k f", p=P)
                                     [:, bass.ds(e, 1)].rearrange("p a k f -> p (a k) f")) \
                            .then_inc(S(f"more_w{l}"), 16)
                sp.wait_ge(S("down_done"), NE * (l + 1))

            for n in range(CH_KV, CH_S):
                chunk(n)
            ln_params(0)
            sp.wait_ge(S("rope_ev"), 12)
            sp.wait_ge(S("mkv_mm"), 8)
            for h in range(RH):
                if h >= 2:
                    sp.wait_ge(S(f"st_out{h % 2}"), 16 * (h // 2))
                sp.dma_start(st_s[:, h % 2].rearrange("p (b e) -> p b e", b=DB),
                             state_ret[0, :, h].rearrange("b d e -> d b e")).then_inc(S(f"st_in{h % 2}"), 16)
            output_weights(0)
            mem_cache(0)
            experts(0)
            for n in range(CH_S, CH_END):
                chunk(n)
            ln_params(2)
            sp.wait_ge(S("tables"), 64)
            sp.wait_ge(S("fm_mm"), 10)
            sp.wait_ge(S("x_ready"), 2 * NT)
            for n in range(DB * PG):
                pg = sp.value_load(pages[0:1, n:n + 1], min_val=0, max_val=cache_fox_k.shape[0] - 1)
                sp.dma_start(fkc[n], cache_fox_k.rearrange("n s h d -> s n (h d)")[:, bass.ds(pg, 1)]
                             .rearrange("s a f -> s (a f)")).then_inc(S("fk_in"), 16)
            for n in range(DB * PG):
                sp.wait_ge(S("fk_tr"), n + 1)
                pg = sp.value_load(pages[0:1, n:n + 1], min_val=0, max_val=cache_fox_k.shape[0] - 1)
                sp.dma_start(fvc[n], cache_fox_v.rearrange("n s h d -> s n (h d)")[:, bass.ds(pg, 1)]
                             .rearrange("s a f -> s (a f)")).then_inc(S("fv_in"), 16)
            output_weights(1)
            mem_cache(1)
            experts(1)

        @block.gpsimd
        def _(pool):
            def dispatch(l):
                for i in range(NT):
                    pool.wait_ge(S("x_ready"), NT * 2 * l + i + 1)
                    pool.dma_start(xs[l][P * i:P * i + ROWS[i]], X[0:ROWS[i], i]).then_inc(S("xs_out"), 16)
                pool.wait_ge(S("slots"), l + 1)
                pool.wait_ge(S("xs_out"), 80 * (l + 1))
                with pool.Fori(0, PAIRS + 1) as i:
                    b = l * (PAIRS + 1)
                    pool.wait_ge(S("xg_free"), i + (b + 1))
                    nc.gpsimd.tensor_copy(idx_now, slot_tok[:, bass.ds(i, 1)]).then_inc(S("idx"), 1)
                    pool.wait_ge(S("idx"), i + (b + 1))
                    pool.sem_inc(S("gathers"), 1)
                    pool.indirect_dma_start(xg, None, xs[l], bass.IndirectOffsetOnAxis(idx_now, 0)) \
                        .then_inc(S("xg_in"), 16)
                    pool.wait_ge(S("xg_in"), i * 16 + (16 * b + 16))
                more = pool.value_load(lists[0:1, 16:17], min_val=0, max_val=MORE)
                with pool.If(more > 0):
                    with pool.Fori(0, more) as x:
                        pool.wait_ge(S(f"more_step{l}"), x * 9 + 1)
                        nc.gpsimd.tensor_copy(idx_now, slot_tok[:, bass.ds(x + PAIRS, 1)]) \
                            .then_inc(S(f"more_step{l}"), 1)
                        pool.wait_ge(S(f"more_step{l}"), x * 9 + 2)
                        pool.sem_inc(S("gathers"), 1)
                        pool.indirect_dma_start(xg, None, xs[l], bass.IndirectOffsetOnAxis(idx_now, 0)) \
                            .then_inc(S(f"more_x{l}"), 16)
                        pool.wait_ge(S(f"more_step{l}"), x * 9 + 9)
                        pool.dma_start(ys[l].rearrange("(b p) d -> p b d", p=P)[:, bass.ds(x + PAIRS, 1)]
                                       .rearrange("p a d -> p (a d)"), yb).then_inc(S(f"more_out{l}"), 16)
                        pool.wait_ge(S(f"more_out{l}"), x * 16 + 16)
                        pool.sem_inc(S(f"more_step{l}"), 1)
                pool.wait_ge(S("y_out"), 16 * PAIRS * (l + 1) + 16)
                for i in range(NT):
                    n = ROWS[i]
                    if i >= 2:
                        pool.wait_ge(S("yg_used"), NT * l + i - 1)
                    for j in range(2):
                        pool.indirect_dma_start(yg[i % 2][0:n, j], None, ys[l],
                                                bass.IndirectOffsetOnAxis(pos_i[0:n, NT * j + i:NT * j + i + 1], 0)) \
                            .then_inc(S(f"yg_in{i % 2}"), 16)

            nc.gpsimd.memset(zeros, 0.0).then_inc(S("pool_zero"), 1)
            pool.wait_ge(S("pool_zero"), 1)
            for b in range(MORE):
                pool.dma_start(ys_all[(PAIRS + b) * P:(PAIRS + b + 1) * P], zeros).then_inc(S("zero_out"), 16)
            pool.wait_ge(S("mkv_ev"), 8)
            for l in range(LAYERS):
                for out, lo in ((mem_k_p, 0), (mem_v_p, MW)):
                    pool.dma_start(out[l, 0].rearrange("(t p) h d -> p t (h d)", p=P), memkv[:, l, :, lo:lo + MW]) \
                        .then_inc(S("mp_out"), 16)
            pool.wait_ge(S("rst"), 24)
            pool.dma_start(ret_prompt[0, 0].rearrange("h d e -> d h e"), state_p).then_inc(S("rs_out"), 16)
            for h in range(RH):
                pool.wait_ge(S("rst"), 24 + h + 1)
                pool.dma_start(ret_sample[0, :, h].rearrange("b d e -> d b e"),
                               st_s[:, h % 2].rearrange("p (b e) -> p b e", b=DB)).then_inc(S(f"st_out{h % 2}"), 16)
            dispatch(0)
            pool.wait_ge(S("tables"), 64)
            for n in range(DB * PG):
                pg = pool.value_load(pages[0:1, n:n + 1], min_val=0, max_val=cache_fox_k.shape[0] - 1)
                pool.dma_start(past_f[:, n % PG, FH * (n // PG):FH * (n // PG) + FH],
                               cache_fox_logf.rearrange("n s h -> s n h")[:, bass.ds(pg, 1)]
                               .rearrange("s a h -> s (a h)")).then_inc(S("pf_in"), 16)
            pool.wait_ge(S("tm_ev"), 40)
            pool.dma_start(fox_k_p[0].rearrange("(t p) h d -> p t (h d)", p=P), k_rows[:, 0:ST]) \
                .then_inc(S("kv_out"), 16)
            pool.dma_start(fox_k_s.rearrange("b t h d -> (b t) (h d)"), k_rows[0:NS, ST]).then_inc(S("kv_out"), 16)
            pool.dma_start(fox_v_p[0].rearrange("(t p) h d -> p t (h d)", p=P), V[:, 0:ST]).then_inc(S("kv_out"), 16)
            pool.dma_start(fox_v_s.rearrange("b t h d -> (b t) (h d)"), V[0:NS, ST]).then_inc(S("kv_out"), 16)
            pool.wait_ge(S("logf"), 1)
            pool.dma_start(fox_f_p[0].rearrange("(t p) h -> p t h", p=P), logf[:, 0:ST]).then_inc(S("f_out"), 16)
            pool.dma_start(fox_f_s.rearrange("b t h -> (b t) h"), logf[0:NS, ST]).then_inc(S("f_out"), 16)
            dispatch(1)
            pool.wait_ge(S("x_ready"), 4 * NT)
            pool.dma_start(y_prompt[0].rearrange("(t p) d -> p t d", p=P), X[:, 0:ST]).then_inc(S("x_out"), 16)
            pool.dma_start(y_sample.rearrange("b t d -> (b t) d"), X[0:NS, ST]).then_inc(S("x_out"), 16)
            pool.wait_ge(S("x_out"), 32)
            pool.wait_ge(S("f_out"), 32)
            pool.wait_ge(S("kv_out"), 64)
            pool.wait_ge(S("mp_out"), 64)
            pool.wait_ge(S("rs_out"), 16)
            pool.wait_ge(S("st_out0"), 48)
            pool.wait_ge(S("st_out1"), 48)

        @block.tensor
        def _(pe):
            mm, tr = nc.tensor.matmul, nc.tensor.transpose

            def cols_of(p, i):
                n = ROWS[i]
                if p:
                    pe.wait_ge(S("x_ready"), NT * (p - 1) + i + 1)
                for half in range(2):
                    j = 10 * p + 2 * i + half
                    if j >= 2:
                        pe.wait_ge(S("xt_cp"), j - 1)
                    for k in range(4):
                        kk = 4 * half + k
                        last = tr(bank(j % 2, n * k, n * k + n), X[0:n, i, kk * P:kk * P + P], ident[0:n, 0:n])
                    last.then_inc(S("xt_mm"), 1)

            def feature_major(n, w, lo):
                b = 2 * (n % 2)
                for k in range(KD):
                    mm(bank(b), w[:, k, lo:lo + P], XT[:, k, 0:SEQ], start=(k == 0), stop=(k == KD - 1))
                for k in range(KD):
                    last = mm(bank(b + 1, 0, NS), w[:, k, lo:lo + P], XT[:, k, SEQ:TOK], start=(k == 0),
                              stop=(k == KD - 1))
                return last

            def token_major(n, w, src, i, width):
                for k in range(KD):
                    last = mm(bank(4 + n % 4, 0, width, rows=(0, ROWS[i])), src[:, k, P * i:P * i + ROWS[i]],
                              w[:, k, :], start=(k == 0), stop=(k == KD - 1))
                return last

            def mem_prompt_attention(l):
                u0 = 16 * l

                def logits(u):
                    i, h = u // 4, u % 4
                    if u0 + u >= 2:
                        pe.wait_ge(S("mp_e"), u0 + u - 1)
                    f = slice(64 * (h % 2), 64 * (h % 2) + 64)
                    mm(bank(u % 2, 0, ML), mqT[f, h // 2, P * i:P * i + P], memkt[f, l, h // 2, :],
                       start=True, stop=True).then_inc(S("mp_l"), 1)

                def turn(u):
                    pe.wait_ge(S("mp_n"), u0 + u + 1)
                    if u0 + u >= 2:
                        pe.wait_ge(S("mp_c"), u0 + u - 1)
                    for m in range(2):
                        last = tr(bank(2 + u % 2, P * m, P * m + P), mpr[:, u % 2, P * m:P * m + P], ident)
                    last.then_inc(S("mp_t"), 1)

                def values(u):
                    i, h = u // 4, u % 4
                    pe.wait_ge(S("mp_c"), u0 + u + 1)
                    if h == 0 and 4 * l + i >= 2:
                        pe.wait_ge(S("mp_ev"), 4 * l + i - 1)
                    o = bank(4 + i % 2, P * (h // 2), P * (h // 2) + P, rows=(64 * (h % 2), 64 * (h % 2) + 64))
                    for m in range(2):
                        last = mm(o, memkv[:, l, m, MW + 64 * h:MW + 64 * h + 64], mprT[:, u % 2, P * m:P * m + P],
                                  start=(m == 0), stop=(m == 1))
                    last.then_inc(S("mp_o"), 1)

                for s in range(16 + 2):
                    if s < 16:
                        logits(s)
                    if 1 <= s <= 16:
                        turn(s - 1)
                    if s >= 2:
                        values(s - 2)

            def mem_sample_attention(l):
                for b in range(DB):
                    n = DB * l + b
                    pe.wait_ge(S(f"mk_in{b % 2}"), 16 * (4 * l + b // 2 + 1))
                    if n >= 2:
                        pe.wait_ge(S("mk_cp"), n - 1)
                    for hp in range(2):
                        for m in range(2):
                            o = P * (2 * hp + m)
                            last = tr(bank(6 + b % 2, o, o + P), mkc[b % 2][:, m, P * hp:P * hp + P], ident)
                    last.then_inc(S("mk_tr"), 1)
                    pe.wait_ge(S("mk_cp"), n + 1)
                    if b == 0:
                        pe.wait_ge(S("mp_e"), 16 * (l + 1))
                    for h in range(MH):
                        f = slice(64 * (h % 2), 64 * (h % 2) + 64)
                        for m in range(2):
                            o = NS * (2 * m + h // 2) + DS * b
                            last = mm(bank(h % 2, o, o + DS), mkcT[f, h // 2, m, :],
                                      mqT[f, h // 2, SEQ + DS * b:SEQ + DS * b + DS], start=True, stop=True,
                                      skip_group_check=True)
                    last.then_inc(S("ms_l"), 1)
                pe.wait_ge(S("ms_lt"), l + 1)
                pe.wait_ge(S("mp_c"), 16 * (l + 1))
                for m in range(2):
                    last = tr(bank(2, P * m, P * m + P), ml_t[:, m].rearrange("p h t -> p (h t)"), ident)
                last.then_inc(S("ms_r"), 1)
                pe.wait_ge(S("ms_n"), l + 1)
                for m in range(2):
                    last = tr(bank(3, P * m, P * m + P), ml_r[:, P * m:P * m + P], ident)
                last.then_inc(S("ms_t"), 1)
                pe.wait_ge(S("ms_c"), l + 1)
                pe.wait_ge(S("mv_in"), 128 * (l + 1))
                pe.wait_ge(S("mp_ev"), 4 * (l + 1))
                for b in range(DB):
                    for h in range(MH):
                        o = NS * (h // 2) + DS * b
                        for m in range(2):
                            last = mm(bank(4, o, o + DS, rows=(64 * (h % 2), 64 * (h % 2) + 64)),
                                      mvc[:, b, MW * m + 64 * h:MW * m + 64 * h + 64],
                                      mp_s[:, m, NS * h + DS * b:NS * h + DS * b + DS],
                                      start=(m == 0), stop=(m == 1), skip_group_check=True)
                last.then_inc(S("ms_o"), 1)

            def router_tile(l, i):
                n, j = ROWS[i], NT * l + i
                pe.wait_ge(S("xt_cp"), 10 * (2 * l + 1) + 2 * i + 2)
                if j >= 2:
                    pe.wait_ge(S("rt_ev"), j - 1)
                for k in range(KD):
                    last = mm(bank(2 + j % 2, 0, NG + NE, rows=(0, n)), XT[:, k, P * i:P * i + n], wr[:, k, :],
                              start=(k == 0), stop=(k == KD - 1))
                last.then_inc(S("rt_mm"), 1)

            def project_and_route(l):
                pe.wait_ge(S("ms_ev"), l + 1)
                pe.wait_ge(S("wo_in"), 32 * (l + 1))
                pe.wait_ge(S("route_in"), 16 * 7 * (l + 1))
                for i in range(NT + 1):
                    if i < NT:
                        for half in range(2):
                            j = 10 * l + 2 * i + half
                            if j >= 4:
                                pe.wait_ge(S("wo_ev"), j - 3)
                            for k in range(KD):
                                last = mm(bank(4 + j % 4, rows=(0, ROWS[i])), MX[:, k, P * i:P * i + ROWS[i]],
                                          wo_v[:, k, 512 * half:512 * half + 512], start=(k == 0),
                                          stop=(k == KD - 1))
                            last.then_inc(S("wo_mm"), 1)
                    if i:
                        cols_of(2 * l + 1, i - 1)
                        router_tile(l, i - 1)
                pe.wait_ge(S("onehot"), l + 1)
                pe.wait_ge(S("wo_ev"), 10 * (l + 1))
                for i in range(NT):
                    for q in range(i + 1):
                        mm(bank(4, NE * i, NE * i + NE), C("strict") if q == i else C("ones"), cnt[:, q, :],
                           start=(q == 0), stop=(q == i))
                for q in range(NT):
                    last = mm(bank(4, NE * NT, NE * NT + NE), C("ones"), cnt[:, q, :], start=(q == 0),
                              stop=(q == NT - 1))
                last.then_inc(S("rank_mm"), 1)
                pe.wait_ge(S("places"), l + 1)
                for n in range(10):
                    last = mm(bank(5, 0, 64), a1[:, n, :], (bb if n < 5 else bb2)[:, n % 5, :], start=(n == 0),
                              stop=(n == 9))
                last.then_inc(S("slot_mm"), 1)

            def turn_rows():
                for half in range(2):
                    for k in range(4):
                        kk = 4 * half + k
                        last = tr(bank(2 + half, P * k, P * k + P), xg[:, kk * P:kk * P + P], ident)
                return last

            def experts(l):
                s = l * PAIRS
                g = l * (PAIRS + 1)
                if l == 0:
                    pe.sem_inc(S("xg_free"), 1)
                pe.wait_ge(S("slots"), l + 1)
                pe.wait_ge(S("xg_in"), 16 * (g + 1))
                turn_rows().then_inc(S("xg_free"), 1)
                with pe.Fori(0, PAIRS // 2) as r:
                    for q in range(2):
                        pe.wait_ge(S("xgt"), r * 2 + (g + q + 1))
                        for j in range(2):
                            b = 2 * q + j
                            pe.wait_ge(S(f"exp_in{b}"), r * 32 + (16 * s + 32))
                            for f in range(4):
                                for k in range(KD):
                                    last = mm(bank(j, SLOTS * f, SLOTS * f + SLOTS), WU[b][:, k, P * f:P * f + P],
                                              xgT[:, k, SLOTS * j:SLOTS * j + SLOTS], start=(k == 0),
                                              stop=(k == KD - 1))
                            last.then_inc(S("up_done"), 1)
                        pe.wait_ge(S("xg_in"), r * 32 + (16 * (g + q) + 32))
                        turn_rows().then_inc(S("xg_free"), 1)
                        pe.wait_ge(S("y_ev"), r * 2 + (s + q + 1))
                        for j in range(2):
                            b = 2 * q + j
                            pe.wait_ge(S("hid"), r * 4 + (2 * (s + q) + j + 1))
                            for half in range(2):
                                for f in range(2):
                                    last = mm(bank(4 + half, rows=(SLOTS * j, SLOTS * j + SLOTS)), hid[:, j, f, :],
                                              WD[b][:, f, 512 * half:512 * half + 512], start=(f == 0),
                                              stop=(f == 1))
                            last.then_inc(S("down_done"), 1)
                more = pe.value_load(lists[0:1, 16:17], min_val=0, max_val=MORE)
                pe.wait_ge(S("xgt"), g + PAIRS + 1)
                pe.wait_ge(S("y_ev"), s + PAIRS + 1)
                pe.sem_inc(S(f"more_step{l}"), 1)
                with pe.If(more > 0):
                    with pe.Fori(0, more) as x:
                        pe.wait_ge(S(f"more_step{l}"), x * 9 + 2)
                        pe.wait_ge(S(f"more_x{l}"), x * 16 + 16)
                        turn_rows().then_inc(S(f"more_step{l}"), 1)
                        pe.wait_ge(S(f"more_step{l}"), x * 9 + 4)
                        pe.wait_ge(S(f"more_w{l}"), x * 32 + 32)
                        for f in range(4):
                            for k in range(KD):
                                last = mm(bank(0, P * f, P * f + P), WU[0][:, k, P * f:P * f + P], xgT[:, k, :],
                                          start=(k == 0), stop=(k == KD - 1))
                        last.then_inc(S(f"more_step{l}"), 1)
                        pe.wait_ge(S(f"more_step{l}"), x * 9 + 7)
                        for half in range(2):
                            for f in range(2):
                                last = mm(bank(4 + half), hidx[:, f, :], WD[0][:, f, 512 * half:512 * half + 512],
                                          start=(f == 0), stop=(f == 1))
                        last.then_inc(S(f"more_step{l}"), 1)

            pe.wait_ge(S("inputs"), 48)
            for i in range(NT):
                cols_of(0, i)
            pe.wait_ge(S("tables"), 64)
            for m in range(2):
                for half in range(2):
                    j = 2 * m + half
                    if j >= 2:
                        pe.wait_ge(S("mt_cp"), j - 1)
                    for k in range(4):
                        kk = 4 * half + k
                        last = tr(bank(2 + j % 2, P * k, P * k + P), mem_rows[:, m, kk * P:kk * P + P], ident)
                    last.then_inc(S("mt_mm"), 1)
            pe.wait_ge(S("mt_cp"), 4)
            for l in range(LAYERS):
                for kv in range(2):
                    chunk_ready(pe, CH_KV + 2 * l + kv)
                    for m in range(2):
                        j = 4 * l + 2 * kv + m
                        if j >= 4:
                            pe.wait_ge(S("mkv_ev"), j - 3)
                        for k in range(KD):
                            last = mm(bank(4 + j % 4, 0, 256), memT[:, k, P * m:P * m + P],
                                      wslot_view(CH_KV + 2 * l + kv)[:, k, :], start=(k == 0), stop=(k == KD - 1))
                        last.then_inc(S("mkv_mm"), 1)
                pe.wait_ge(S("mkv_ev"), 4 * l + 2)
                for hp in range(2):
                    for m in range(2):
                        o = P * (2 * hp + m)
                        last = tr(bank(2 + l, o, o + P), memkv[:, l, m, P * hp:P * hp + P], ident)
                last.then_inc(S("mkt_mm"), 1)
            pe.wait_ge(S("xt_cp"), 10)
            for h in range(2 * RH):
                n = CH_A + h // 3
                if h % 3 == 0:
                    chunk_ready(pe, n)
                if h >= 2:
                    pe.wait_ge(S("rope_ev"), h - 1)
                elif h == 1:
                    pe.wait_ge(S("mkt_ev"), 2)
                feature_major(h, wslot_view(n), P * (h % 3)).then_inc(S("rope_mm"), 1)
            pe.wait_ge(S("mkv_ev"), 8)
            for j in range(20):
                n = CH_A + 4 + j // 5
                if j % 5 == 0:
                    chunk_ready(pe, n)
                if j >= 4:
                    pe.wait_ge(S("tm_ev"), j - 3)
                token_major(j, wslot_view(n), XT, j % 5, 384).then_inc(S("tm_mm"), 1)
            pe.wait_ge(S("rope_ev"), 12)
            chunk_ready(pe, CH_A + 8)
            for n in range(2):
                feature_major(n, wslot_view(CH_A + 8), P * n).then_inc(S("fm_mm"), 1)

            def front(u):
                n, h = u // RH, u % RH
                if u == 0:
                    pe.wait_ge(S("fm_ev"), 2)
                if u >= 2:
                    pe.wait_ge(S("rsm"), u - 1)
                mm(bank(u % 2, 0, P), kT[:, h, P * n:P * n + P], qT[:, h, P * n:P * n + P], start=True,
                   stop=True).then_inc(S("rsc"), 1)
                if u >= 2:
                    pe.wait_ge(S("rkd"), u - 1)
                tr(bank(2 + u % 2, 0, P), kT[:, h, P * n:P * n + P], ident).then_inc(S("rkt"), 1)

            def back(u):
                n, h = u // RH, u % RH
                if u == 0:
                    pe.wait_ge(S("tm_ev"), 20)
                pe.wait_ge(S("rsm"), u + 1)
                if u >= 2:
                    pe.wait_ge(S("rcp"), u - 1)
                v = V[:, n, P * h:P * h + P]
                last = mm(bank(4 + u % 2, 0, P), scm[:, u % 2, :], v, start=True, stop=(n == 0))
                if n:
                    pe.wait_ge(S("rst"), u - RH + 1)
                    last = mm(bank(4 + u % 2, 0, P), qd[:, u % 2, :], state_p[:, h, :], start=False, stop=True)
                last.then_inc(S("rr"), 1)
                pe.wait_ge(S("rkd"), u + 1)
                if u >= 2:
                    pe.wait_ge(S("rst"), u - 1)
                mm(bank(6 + u % 2, 0, P), kd[:, u % 2, :], v, start=True, stop=True).then_inc(S("rkv"), 1)

            for u in range(4 * RH + 1):
                if u < 4 * RH:
                    front(u)
                if u:
                    back(u - 1)
            pe.wait_ge(S("rst"), 24)
            pe.wait_ge(S("rcp"), 24)
            pe.wait_ge(S("rkd"), 24)
            for h in range(RH):
                b = h % 2
                if h >= 2:
                    pe.wait_ge(S("rsm"), 24 + h - 1)
                    pe.wait_ge(S("rkd"), 24 + h - 1)
                    pe.wait_ge(S("rcp"), 24 + h - 1)
                mm(bank(b, 0, NS, rows=(0, NS)), kT[:, h, SEQ:TOK], qT[:, h, SEQ:TOK], start=True,
                   stop=True).then_inc(S("rsc"), 1)
                tr(bank(2 + b, 0, P, rows=(0, NS)), kT[:, h, SEQ:TOK], ident).then_inc(S("rkt"), 1)
                pe.wait_ge(S("rsm"), 24 + h + 1)
                pe.wait_ge(S(f"st_in{b}"), 16 * (h // 2 + 1))
                mm(bank(4 + b, 0, NS), V[0:NS, ST, P * h:P * h + P], scs[0:NS, b, :], start=True, stop=False,
                   skip_group_check=True)
                for q in range(DB):
                    last = mm(bank(4 + b, DS * q, DS * q + DS), st_s[:, b, P * q:P * q + P],
                              qds[:, b, DS * q:DS * q + DS], start=False, stop=(q == DB - 1), skip_group_check=True)
                last.then_inc(S("rr"), 1)
                pe.wait_ge(S("rkd"), 24 + h + 1)
                if h:
                    pe.wait_ge(S("rst"), 24 + h)
                for q in range(2):
                    last = mm(bank(6 + q), kds[0:NS, :], vbd[0:NS, 512 * q:512 * q + 512], start=True, stop=True)
                last.then_inc(S("rkv"), 1)
            pe.wait_ge(S("rcp"), 24 + RH)
            pe.wait_ge(S("rsm"), 24 + RH)
            for h in range(RH):
                last = tr(bank(h // 4, P * (h % 4), P * (h % 4) + P, rows=(0, NS)), rTs[:, h, :], ident)
            last.then_inc(S("srt"), 1)
            pe.wait_ge(S("srow"), 1)
            pe.wait_ge(S("rkd"), 24 + RH)
            for i in range(NT):
                n = ROWS[i]
                pe.wait_ge(S("gated"), i + 1)
                if i >= 2:
                    pe.wait_ge(S("tk_cp"), i - 1)
                for h in range(RH):
                    o = 1024 * (i % 2) + n * h
                    last = tr(ps[:, o:o + n], R[0:n, i, P * h:P * h + P], ident[0:n, 0:n])
                last.then_inc(S("tk_mm"), 1)
            pe.wait_ge(S("tk_cp"), NT)
            pe.wait_ge(S("rst"), 24 + RH)
            pe.sem_inc(S("tok_done"), 1)
            mem_prompt_attention(0)
            mem_sample_attention(0)
            project_and_route(0)
            experts(0)

            for j in range(20, 45):
                n = CH_S + (j - 20) // 5
                if j % 5 == 0:
                    chunk_ready(pe, n)
                if j < 25:
                    cols_of(2, j - 20)
                    pe.wait_ge(S("xt_cp"), 20 + 2 * (j - 20) + 2)
                if j >= 24:
                    pe.wait_ge(S("tm_ev"), j - 3)
                token_major(j, wslot_view(n), XT, j % 5, 12 if j >= 40 else 384).then_inc(S("tm_mm"), 1)
            for i in range(NT):
                n = ROWS[i]
                pe.wait_ge(S("tm_ev"), 30)
                if i >= 2:
                    pe.wait_ge(S("tk_cp"), NT + i - 1)
                for h in range(6):
                    o = 1024 * (i % 2) + n * h
                    last = tr(ps[:, o:o + n], k_rows[0:n, i, P * h:P * h + P], ident[0:n, 0:n])
                last.then_inc(S("tk_mm"), 1)
            pe.wait_ge(S("tk_cp"), NT + NT)
            for n in range(2, 10):
                c = CH_B + (n - 2) // 3
                if (n - 2) % 3 == 0:
                    chunk_ready(pe, c)
                if n >= 4:
                    pe.wait_ge(S("fm_ev"), n - 1)
                feature_major(n, wslot_view(c), P * ((n - 2) % 3)).then_inc(S("fm_mm"), 1)
            pe.wait_ge(S("logf"), 1)
            pe.wait_ge(S("tm_ev"), 45)
            pe.wait_ge(S("pf_in"), 16 * DB * PG)
            for i in range(ST):
                for q in range(i + 1):
                    mm(bank(4, FH * i, FH * i + FH), C("tri") if q == i else C("ones"), logf[:, q, :],
                       start=(q == 0), stop=(q == i))
            o = bank(4, FH * ST, FH * NT, rows=(0, NS))
            mm(o, C("tri_s", NS), logf[0:NS, ST, :], start=True, stop=False)
            for b in range(DB):
                for g in range(PG):
                    last = mm(o, C("batch_s")[:, 28 - DS * b:60 - DS * b], past_f[:, g, FH * b:FH * b + FH],
                              start=False, stop=(b == DB - 1 and g == PG - 1))
            mm(bank(5, 0, DB * FH), C("tri"), past_f[:, 0, :], start=True, stop=True)
            mm(bank(5, DB * FH, 2 * DB * FH), C("ones"), past_f[:, 0, :], start=True, stop=False)
            mm(bank(5, DB * FH, 2 * DB * FH), C("tri"), past_f[:, 1, :], start=False, stop=True) \
                .then_inc(S("cum"), 1)
            pe.wait_ge(S("cum_ev"), 1)
            pe.wait_ge(S("fm_ev"), 10)

            def minus_c(h):
                if h:
                    pe.wait_ge(S("fnb_cp"), h)
                for q in range(ST):
                    last = mm(bank(3, P * q, P * q + P), negc[:, q, h:h + 1].broadcast_to([P, P]), ident,
                              start=True, stop=True)
                last.then_inc(S("fnb"), 1)

            def fox_logits(h):
                f = slice(64 * (h % 2), 64 * (h % 2) + 64)
                for n, tiles in enumerate(((1,), (0, 2), (3,))):
                    if h:
                        pe.wait_ge(S("fp_s"), 3 * h - 2 + n)
                    for i in tiles:
                        b, o = LOGIT_AT[i]
                        last = mm(bank(b, o, o + P * (i + 1)), qT[f, h // 2, P * i:P * i + P],
                                  kT[f, h // 2, 0:P * (i + 1)], start=True, stop=True)
                    last.then_inc(S("fp_l"), 1)

            def fox_turn(h):
                for n, tiles in enumerate(((3,), (2, 0), (1,))):
                    pe.wait_ge(S("fp_e"), 4 * h + (1, 3, 4)[n])
                    if h:
                        pe.wait_ge(S("fp_c"), 3 * h - 2 + n)
                    for i in tiles:
                        for q in range(i + 1):
                            o = 4 * SEQ + PT_AT[i] + P * q
                            last = tr(ps[:, o:o + P], fpr[h % 2][:, i, P * q:P * q + P], ident)
                    last.then_inc(S("fp_t"), 1)

            def fox_values(h):
                pe.wait_ge(S("fp_c"), 3 * h + 3)
                if h:
                    pe.wait_ge(S("fp_ev"), h)
                for i in range(ST):
                    for q in range(i + 1):
                        o = PT_AT[i] + P * q
                        last = mm(bank(7, FD * i, FD * i + FD), fprT[:, h % 2, o:o + P],
                                  V[:, q, FD * h:FD * h + FD], start=(q == 0), stop=(q == i))
                last.then_inc(S("fox_p"), 1)

            minus_c(0)
            for s in range(FH + 2):
                if s < FH:
                    fox_logits(s)
                if 1 <= s <= FH:
                    fox_turn(s - 1)
                if s >= 2:
                    fox_values(s - 2)
                if s + 1 < FH:
                    minus_c(s + 1)
            pe.wait_ge(S("fp_ev"), FH)
            def turn_page(n):
                if n >= 2:
                    pe.wait_ge(S("fk_cp"), n - 1)
                    pe.wait_ge(S("fk_cp2"), n - 1)
                for h in range(6):
                    o = 1024 + 2048 * (n % 2) + P * h
                    last = tr(ps[:, o:o + P], fkc[n][:, P * h:P * h + P], ident)
                last.then_inc(S("fk_tr"), 1)

            pe.wait_ge(S("fk_in"), 16 * DB * PG)
            pe.wait_ge(S("qbd"), 1)
            turn_page(0)
            for n in range(DB * PG):
                b, g = n // PG, n % PG
                if n + 1 < DB * PG:
                    turn_page(n + 1)
                pe.wait_ge(S("fk_cp"), n + 1)
                pe.wait_ge(S("fk_cp2"), n + 1)
                for h in range(6):
                    o = bank(g, 2 * NS * h, 2 * NS * h + 2 * NS).rearrange("p (r t) -> p r t", r=2)
                    last = mm(o[:, :, DS * b:DS * b + DS], fkT[n % 2][:, h, :], qbd[:, h, :, DS * b:DS * b + DS],
                              start=True, stop=True, skip_group_check=True)
                last.then_inc(S("fs_l"), 1)
            for h in range(FH):
                f = slice(64 * (h % 2), 64 * (h % 2) + 64)
                rr = (NS * (h % 4), NS * (h % 4) + NS)
                o = bank(4 + h % 2, NS * (h // 4), NS * (h // 4) + NS, rows=rr)
                mm(o, qT[f, h // 2, SEQ:TOK], kT[f, h // 2, SEQ:TOK], start=True, stop=False, skip_group_check=True)
                last = mm(o, negc[0:NS, ST, h:h + 1].broadcast_to([NS, NS]), ident[0:NS, 0:NS], start=False,
                          stop=True, skip_group_check=True)
            last.then_inc(S("fs_new"), 1)
            for i in range(ST):
                if i >= 2:
                    pe.wait_ge(S("tk_cp"), 2 * NT + i - 1)
                else:
                    pe.wait_ge(S("fk_cp"), DB * PG)
                    pe.wait_ge(S("fk_cp2"), DB * PG)
                for h in range(6):
                    o = 1024 + 2048 * (i % 2) + P * h
                    last = tr(ps[:, o:o + P], o_rows[:, i, P * h:P * h + P], ident)
                last.then_inc(S("tk_mm"), 1)
            pe.wait_ge(S("tk_cp"), 2 * NT + ST)
            pe.wait_ge(S("fs_lt"), PG)
            for r in range(3):
                for g in range(PG):
                    last = tr(bank((6, 7, 2)[r], PAGE * g, PAGE * g + PAGE),
                              fl_t[:, g, 4 * r:4 * r + 4].rearrange("p h t -> p (h t)"), ident)
                last.then_inc(S("fs_r"), 1)
            pe.wait_ge(S("fs_n"), 1)
            for r in range(3):
                for g in range(PG):
                    tr(bank(3 + r, PAGE * g, PAGE * g + PAGE), fl_r[:, r, PAGE * g:PAGE * g + PAGE], ident)
                tr(bank(3 + r, PG * PAGE, PG * PAGE + P, rows=(0, NS)), fl_r[:, r, PG * PAGE:], ident) \
                    .then_inc(S("fs_t"), 1)
            pe.wait_ge(S("fs_c"), 3)
            pe.wait_ge(S("fv_in"), 16 * DB * PG)

            def pair_probs(hp, g, rows, lo, hi):
                return fs_p[0:rows, hp // 2, g, :].rearrange("p (h t) -> p h t", t=NS) \
                    [:, 2 * (hp % 2):2 * (hp % 2) + 2, lo:hi]

            for hp in range(6):
                o = bank(0, 2 * NS * hp, 2 * NS * hp + 2 * NS).rearrange("p (r t) -> p r t", r=2)
                mm(o, V[0:NS, ST, P * hp:P * hp + P], pair_probs(hp, 2, NS, 0, NS), start=(hp == 0), stop=False,
                   skip_group_check=True)
            for n in range(DB * PG):
                b, g = n // PG, n % PG
                for hp in range(6):
                    o = bank(0, 2 * NS * hp, 2 * NS * hp + 2 * NS).rearrange("p (r t) -> p r t", r=2)
                    last = mm(o[:, :, DS * b:DS * b + DS], fvc[n][:, P * hp:P * hp + P],
                              pair_probs(hp, g, P, DS * b, DS * b + DS), start=False,
                              stop=(n == DB * PG - 1), skip_group_check=True)
            last.then_inc(S("fs_pv"), 1)
            pe.wait_ge(S("fs_ev"), 1)
            pe.sem_inc(S("tok_done"), 1)
            mem_prompt_attention(1)
            mem_sample_attention(1)
            project_and_route(1)
            experts(1)

        @block.scalar
        def _(act):
            af = nc.scalar.activation

            def copy_cols(p, i):
                n = ROWS[i]
                for half in range(2):
                    j = 2 * i + half
                    act.wait_ge(S("xt_mm"), 10 * p + j + 1)
                    af(XT[:, 4 * half:4 * half + 4, P * i:P * i + n],
                       bank(j % 2, 0, 4 * n).rearrange("p (k n) -> p k n", k=4), ACT.Copy).then_inc(S("xt_cp"), 1)

            def norm_and_columns(p, columns=True):
                for i in range(NT + 1):
                    if i < NT:
                        act.wait_ge(S("ln_st"), NT * p + i + 1)
                        af(rstd[:, i:i + 1], mv[:, i, 1:2], ACT.Sqrt, bias=eps_ln[:, 0:1]).then_inc(S("ln_sd"), 1)
                    if i and columns:
                        copy_cols(p + 1, i - 1)

            def mem_prompt(l):
                u0 = 16 * l
                for s in range(17):
                    if s < 16:
                        act.wait_ge(S("mp_m"), u0 + s + 1)
                        if u0 + s >= 2:
                            act.wait_ge(S("mp_t"), u0 + s - 1)
                        af(mpr[:, s % 2, :], bank(s % 2, 0, ML), ACT.Exp, bias=nmx[:, s % 4:s % 4 + 1],
                           accum_out=esum[:, s % 4:s % 4 + 1]).then_inc(S("mp_e"), 1)
                    if s:
                        u = s - 1
                        act.wait_ge(S("mp_t"), u0 + u + 1)
                        if u0 + u >= 2:
                            act.wait_ge(S("mp_o"), u0 + u - 1)
                        af(mprT[:, u % 2, :], bank(2 + u % 2, 0, ML), ACT.Copy).then_inc(S("mp_c"), 1)

            def mem_sample(l):
                for b in range(DB):
                    n = DB * l + b
                    act.wait_ge(S("mk_tr"), n + 1)
                    if n:
                        act.wait_ge(S("ms_l"), n)
                    af(mkcT, bank(6 + b % 2).rearrange("p (a m t) -> p a m t", a=2, m=2), ACT.Copy) \
                        .then_inc(S("mk_cp"), 1)
                act.wait_ge(S("ms_l"), DB * (l + 1))
                for r in range(2):
                    last = af(ml_t[:, :, r::2, :], bank(r, 0, 128).rearrange("p (m a t) -> p m a t", m=2, a=2),
                              ACT.Copy)
                last.then_inc(S("ms_lt"), 1)
                act.wait_ge(S("ms_m"), l + 1)
                af(ml_r, bank(2, 0, ML), ACT.Exp, bias=nmx[:, 0:1], accum_out=esum[:, 0:1]).then_inc(S("ms_e"), 1)
                act.wait_ge(S("ms_t"), l + 1)
                af(mp_s, bank(3, 0, ML).rearrange("p (m t) -> p m t", m=2), ACT.Copy).then_inc(S("ms_c"), 1)
                act.wait_ge(S("ms_o"), l + 1)
                af(MX[:, 6:8, SEQ:TOK], bank(4, 0, 2 * NS).rearrange("p (a t) -> p a t", a=2), ACT.Copy) \
                    .then_inc(S("ms_ev"), 1)

            def routing(l):
                act.wait_ge(S("r_step"), 4 * l + 1)
                af(gexp, gexp, ACT.Exp).then_inc(S("r_step"), 1)
                act.wait_ge(S("r_step"), 4 * l + 3)
                af(tmpw, tmpw, ACT.Exp).then_inc(S("r_step"), 1)

            def turn_copy(sem):
                for half in range(2):
                    last = af(xgT[:, 4 * half:4 * half + 4, :],
                              bank(2 + half).rearrange("p (k n) -> p k n", k=4), ACT.Copy)
                last.then_inc(sem, 1)

            def experts(l):
                s, g = l * PAIRS, l * (PAIRS + 1)
                if l == 0:
                    act.sem_inc(S("y_ev"), 1)
                    act.sem_inc(S("y_out"), 16)
                act.wait_ge(S("xg_free"), g + 2)
                turn_copy(S("xgt"))
                with act.Fori(0, PAIRS) as i:
                    for j in range(2):
                        act.wait_ge(S("up_done"), i * 2 + (2 * s + j + 1))
                        af(sg[:, j, :], bank(j, 0, 2 * SLOTS), ACT.Silu).then_inc(S("gate"), 1)
                    act.wait_ge(S("xg_free"), i + (g + 3))
                    turn_copy(S("xgt"))
                    act.wait_ge(S("y_out"), i * 16 + (16 * s + 16))
                    act.wait_ge(S("down_done"), i * 2 + (2 * s + 2))
                    for half in range(2):
                        last = af(yb[:, 512 * half:512 * half + 512], bank(4 + half), ACT.Copy,
                                  scale=wslot[:, bass.ds(i, 1)])
                    last.then_inc(S("y_ev"), 1)
                    act.wait_ge(S("y_ev"), i + (s + 2))
                    act.dma_start(ys[l].rearrange("(b p) d -> p b d", p=P)[:, bass.ds(i, 1)]
                                  .rearrange("p a d -> p (a d)"), yb).then_inc(S("y_out"), 16)
                act.wait_ge(S("y_out"), 16 * (s + PAIRS) + 16)
                more = act.value_load(lists[0:1, 16:17], min_val=0, max_val=MORE)
                with act.If(more > 0):
                    with act.Fori(0, more) as x:
                        act.wait_ge(S(f"more_step{l}"), x * 9 + 3)
                        turn_copy(S(f"more_step{l}"))
                        act.wait_ge(S(f"more_step{l}"), x * 9 + 5)
                        af(sgx, bank(0, 0, 2 * P).rearrange("p (f n) -> p f n", f=2), ACT.Silu) \
                            .then_inc(S(f"more_step{l}"), 1)
                        act.wait_ge(S(f"more_step{l}"), x * 9 + 8)
                        for half in range(2):
                            last = af(yb[:, 512 * half:512 * half + 512], bank(4 + half), ACT.Copy,
                                      scale=wslot[:, bass.ds(x + PAIRS, 1)])
                        last.then_inc(S(f"more_step{l}"), 1)

            for i in range(NT):
                copy_cols(0, i)
            for j in range(4):
                act.wait_ge(S("mt_mm"), j + 1)
                af(memT[:, 4 * (j % 2):4 * (j % 2) + 4, P * (j // 2):P * (j // 2) + P],
                   bank(2 + j % 2).rearrange("p (k n) -> p k n", k=4), ACT.Copy).then_inc(S("mt_cp"), 1)
            for l in range(LAYERS):
                for j in range(4):
                    act.wait_ge(S("mkv_mm"), 4 * l + j + 1)
                    af(memkv[:, l, j % 2, MW * (j // 2):MW * (j // 2) + MW], bank(4 + j, 0, 256), ACT.Copy) \
                        .then_inc(S("mkv_ev"), 1)
                act.wait_ge(S("mkt_mm"), l + 1)
                af(memkt[:, l], bank(2 + l).rearrange("p (a t) -> p a t", a=2), ACT.Copy).then_inc(S("mkt_ev"), 1)
            for j in range(20):
                n, i = ROWS[j % 5], j % 5
                act.wait_ge(S("tm_mm"), j + 1)
                c = 384 * ((j // 5) % 2)
                if j < 10:
                    af(V[0:n, i, c:c + 384], bank(4 + j % 4, 0, 384, rows=(0, n)), ACT.Copy).then_inc(S("tm_ev"), 1)
                else:
                    af(G[0:n, i, c:c + 384], bank(4 + j % 4, 0, 384, rows=(0, n)), ACT.Silu).then_inc(S("tm_ev"), 1)

            def queries(n, dst, scale):
                act.wait_ge(S("fm_mm"), n + 1)
                o = 1024 * (n % 2)
                af(dst, ps[:, o:o + TOK], ACT.Copy, scale=scale).then_inc(S("fm_ev"), 1)

            for n in range(2):
                queries(n, mqT[:, n, :], MD ** -0.5)

            def decayed_keys(u):
                act.wait_ge(S("rkt"), u + 1)
                if u >= 2:
                    act.wait_ge(S("rkv"), u - 1)
                af(kd[:, u % 2, :], bank(2 + u % 2, 0, P), ACT.Copy,
                   scale=C("kdecay")[:, u % RH:u % RH + 1]).then_inc(S("rkd"), 1)

            act.wait_ge(S("rope_ev"), 12)
            decayed_keys(0)
            for u in range(4 * RH):
                if u + 1 < 4 * RH:
                    decayed_keys(u + 1)
                act.wait_ge(S("rr"), u + 1)
                af(R[:, u // RH, P * (u % RH):P * (u % RH) + P], bank(4 + u % 2, 0, P), ACT.Copy) \
                    .then_inc(S("rcp"), 1)
            for h in range(RH):
                act.wait_ge(S("rkt"), 24 + h + 1)
                if h:
                    act.wait_ge(S("rkv"), 24 + h)
                af(kds[0:NS, :], bank(2 + h % 2, 0, P, rows=(0, NS)), ACT.Copy).then_inc(S("rkd"), 1)
                act.wait_ge(S("rr"), 24 + h + 1)
                af(rTs[:, h, :], bank(4 + h % 2, 0, NS), ACT.Copy).then_inc(S("rcp"), 1)
            act.wait_ge(S("srt"), 1)
            af(R[0:NS, ST, :], ps[0:NS, 0:RW], ACT.Copy).then_inc(S("srow"), 1)
            act.wait_ge(S("hmv"), 1)
            af(hrs, hmv[:, :, 1], ACT.Sqrt, bias=eps_hn[:, 0:1]).then_inc(S("hsd"), 1)
            act.wait_ge(S("st_out0"), 48)
            act.wait_ge(S("st_out1"), 48)
            for i in range(NT):
                n = ROWS[i]
                act.wait_ge(S("tk_mm"), i + 1)
                o = 1024 * (i % 2)
                af(MX[:, 0:6, P * i:P * i + n], ps[:, o:o + 6 * n].rearrange("p (h n) -> p h n", h=6), ACT.Copy) \
                    .then_inc(S("tk_cp"), 1)
            mem_prompt(0)
            mem_sample(0)
            norm_and_columns(0)
            routing(0)
            experts(0)

            for j in range(20, 45):
                n, i = ROWS[j % 5], j % 5
                if j < 25:
                    act.wait_ge(S("ln_st"), NT + i + 1)
                    af(rstd[:, i:i + 1], mv[:, i, 1:2], ACT.Sqrt, bias=eps_ln[:, 0:1]).then_inc(S("ln_sd"), 1)
                    copy_cols(2, i)
                act.wait_ge(S("tm_mm"), j + 1)
                c = 384 * ((j // 5) % 2)
                if j < 40:
                    dst = (k_rows if j < 30 else V)[0:n, i, c:c + 384]
                    af(dst, bank(4 + j % 4, 0, 384, rows=(0, n)), ACT.Copy).then_inc(S("tm_ev"), 1)
                else:
                    af(fz[0:n, i, :], bank(4 + j % 4, 0, FH, rows=(0, n)), ACT.Copy).then_inc(S("tm_ev"), 1)
            for i in range(NT):
                n = ROWS[i]
                act.wait_ge(S("tk_mm"), NT + i + 1)
                o = 1024 * (i % 2)
                af(kT[:, :, P * i:P * i + n], ps[:, o:o + 6 * n].rearrange("p (h n) -> p h n", h=6), ACT.Copy) \
                    .then_inc(S("tk_cp"), 1)
            for n in range(2, 10):
                queries(n, qT[:, n - 2, :] if n < 8 else mqT[:, n - 8, :], FD ** -0.5)
            act.wait_ge(S("f_step"), 1)
            af(fe, fe, ACT.Exp, scale=-1.0).then_inc(S("f_step"), 1)
            act.wait_ge(S("f_step"), 3)
            af(fe, fe, ACT.Ln).then_inc(S("f_step"), 1)

            def keys_sum(h):
                act.wait_ge(S("fnb"), h + 1)
                if h >= 2:
                    act.wait_ge(S("fp_s"), 3 * (h - 1))
                af(fnb[:, h % 2, :], bank(3), ACT.Copy).then_inc(S("fnb_cp"), 1)

            act.wait_ge(S("x_ready"), 2 * NT)
            act.wait_ge(S("kv_out"), 64)
            keys_sum(0)
            keys_sum(1)
            for h in range(FH):
                act.wait_ge(S("fp_m"), h + 1)
                if h >= 2:
                    act.wait_ge(S("fp_ev"), h - 1)
                for i in (3, 2, 0, 1):
                    row = fpr[h % 2][:, i, 0:P * (i + 1)]
                    af(row, row, ACT.Exp, bias=nmx2[:, h % 2, i:i + 1],
                       accum_out=esum2[:, h % 2, i:i + 1]).then_inc(S("fp_e"), 1)
                for n in range(3):
                    act.wait_ge(S("fp_t"), 3 * h + n + 1)
                    if n == 0 and h >= 2:
                        act.wait_ge(S("fox_p"), h - 1)
                    w = 4 * P if n < 2 else 2 * P
                    af(fprT[:, h % 2, 4 * P * n:4 * P * n + w], bank(4 + n, 0, w), ACT.Copy).then_inc(S("fp_c"), 1)
                if h + 2 < FH:
                    keys_sum(h + 2)
            for n in range(DB * PG):
                act.wait_ge(S("fk_tr"), n + 1)
                if n >= 2:
                    act.wait_ge(S("fs_l"), n - 1)
                af(fkT[n % 2][:, 0:4, :], bank(2 + 4 * (n % 2)).rearrange("p (h t) -> p h t", h=4), ACT.Copy) \
                    .then_inc(S("fk_cp"), 1)
            for i in range(ST):
                act.wait_ge(S("tk_mm"), 2 * NT + i + 1)
                o = 1024 + 2048 * (i % 2)
                af(MX[:, 0:6, P * i:P * i + P], ps[:, o:o + 6 * P].rearrange("p (h n) -> p h n", h=6), ACT.Copy) \
                    .then_inc(S("tk_cp"), 1)
            act.wait_ge(S("fs_m"), 1)
            for r in range(3):
                last = af(fl_r[:, r, :], fl_r[:, r, :], ACT.Exp, bias=nmx[:, r:r + 1], accum_out=esum[:, r:r + 1])
            last.then_inc(S("fs_e"), 1)
            for r in range(3):
                act.wait_ge(S("fs_t"), r + 1)
                af(fs_p[:, r, 0:2, :], bank(3 + r, 0, 2 * P).rearrange("p (g t) -> p g t", g=2), ACT.Copy)
                af(fs_p[0:NS, r, 2, :], bank(3 + r, 2 * P, 3 * P, rows=(0, NS)), ACT.Copy).then_inc(S("fs_c"), 1)
            act.wait_ge(S("fs_pv"), 1)
            for r in range(2):
                rr = (64 * r, 64 * r + 64)
                last = af(MX[rr[0]:rr[1], 0:6, SEQ:TOK], bank(0, 0, 12 * NS, rows=rr)
                          .rearrange("p (h r t) -> p h r t", h=6, r=2)[:, :, r, :], ACT.Copy)
            last.then_inc(S("fs_ev"), 1)
            mem_prompt(1)
            mem_sample(1)
            norm_and_columns(2)
            routing(1)
            experts(1)
            norm_and_columns(3, columns=False)

        @block.vector
        def _(dve):
            v = nc.vector
            count = [0]

            def link(ins):
                count[0] += 1
                ins.then_inc(S("dve_c"), 1)
                dve.wait_ge(S("dve_c"), count[0])

            def bc(ap, shape):
                return ap.broadcast_to(shape)

            def mem_prompt(l):
                u0 = 16 * l

                def softmax_top(u):
                    q = u % 4
                    dve.wait_ge(S("mp_l"), u0 + u + 1)
                    link(v.tensor_reduce(mx[:, q:q + 1], bank(u % 2, 0, ML), AX.X, ALU.max))
                    v.tensor_scalar(nmx[:, q:q + 1], mx[:, q:q + 1], -1.0, None, ALU.mult).then_inc(S("mp_m"), 1)

                def softmax_scale(u):
                    q = u % 4
                    dve.wait_ge(S("mp_e"), u0 + u + 1)
                    link(v.reciprocal(rsum[:, q:q + 1], esum[:, q:q + 1]))
                    v.tensor_scalar(mpr[:, u % 2, :], mpr[:, u % 2, :], rsum[:, q:q + 1], None, ALU.mult) \
                        .then_inc(S("mp_n"), 1)

                def result(i):
                    dve.wait_ge(S("mp_o"), u0 + 4 * i + 4)
                    v.tensor_copy(MX[:, 6:8, P * i:P * i + P],
                                  bank(4 + i % 2, 0, 2 * P).rearrange("p (a t) -> p a t", a=2)) \
                        .then_inc(S("mp_ev"), 1)

                softmax_top(0)
                for u in range(16):
                    if u + 1 < 16:
                        softmax_top(u + 1)
                    softmax_scale(u)
                    if u >= 6 and (u - 6) % 4 == 0:
                        result((u - 6) // 4)
                result(3)

            def mem_sample(l):
                dve.wait_ge(S("ms_r"), l + 1)
                link(v.tensor_reduce(mx[:, 0:1], bank(2, 0, ML), AX.X, ALU.max))
                v.tensor_scalar(nmx[:, 0:1], mx[:, 0:1], -1.0, None, ALU.mult).then_inc(S("ms_m"), 1)
                dve.wait_ge(S("ms_e"), l + 1)
                link(v.reciprocal(rsum[:, 0:1], esum[:, 0:1]))
                v.tensor_scalar(ml_r, ml_r, rsum[:, 0:1], None, ALU.mult).then_inc(S("ms_n"), 1)

            def norm_tile(p, i):
                n = ROWS[i]
                if i == 0:
                    dve.wait_ge(S("ln_in"), 32 * (p + 1))
                for half in range(2):
                    ins = v.bn_stats(stats[0:n, i, 6 * half:6 * half + 6], X[0:n, i, 512 * half:512 * half + 512])
                link(ins)
                v.bn_aggr(mv[0:n, i, :], stats[0:n, i, :]).then_inc(S("ln_st"), 1)
                dve.wait_ge(S("ln_st"), NT * p + i + 1)
                link(v.scalar_tensor_tensor(X[0:n, i], X[0:n, i], mv[0:n, i, 0:1], ln_t[0:n, 0:D], ALU.subtract,
                                            ALU.mult))
                dve.wait_ge(S("ln_sd"), NT * p + i + 1)
                link(v.reciprocal(rstd[:, i:i + 1], rstd[:, i:i + 1]))
                v.scalar_tensor_tensor(X[0:n, i], X[0:n, i], rstd[0:n, i:i + 1], ln_t[0:n, D:], ALU.mult,
                                       ALU.add).then_inc(S("x_ready"), 1)

            def residual_tile(l, i):
                n = ROWS[i]
                for half in range(2):
                    j = 10 * l + 2 * i + half
                    dve.wait_ge(S("wo_mm"), j + 1)
                    xc = X[0:n, i, 512 * half:512 * half + 512]
                    v.scalar_tensor_tensor(xc, xc, ALPHA, bank(4 + j % 4, rows=(0, n)), ALU.mult,
                                           ALU.add).then_inc(S("wo_ev"), 1)
                dve.wait_ge(S("wo_ev"), 10 * l + 2 * i + 2)

            iota = C("iota")
            giv = gi.rearrange("p (i q) -> p i q", q=8)
            e4 = esw.rearrange("p (i g e) -> p i g e", i=NT, g=NG)

            def route_tile(l, i):
                n = ROWS[i]
                if i == 0:
                    link(v.memset(rl, 0.0))
                    link(v.memset(rl[:, :, 4:8], NEG))
                b = bank(2 + (NT * l + i) % 2, 0, NG + NE, rows=(0, n))
                dve.wait_ge(S("rt_mm"), NT * l + i + 1)
                v.tensor_tensor(rl[0:n, i, 0:NG], b[:, 0:NG], biasr[0:n, 0:NG], ALU.add)
                v.tensor_tensor(rl[0:n, i, 8:], b[:, NG:], biasr[0:n, NG:], ALU.add).then_inc(S("rt_ev"), 1)
                dve.wait_ge(S("rt_ev"), NT * l + i + 1)
                link(v.max(gm[:, i, :], rl[:, i, 0:8]))
                link(v.max_index(gi[:, 8 * i:8 * i + 8], gm[:, i, :], rl[:, i, 0:8]))
                link(v.tensor_copy(gf[:, i:i + 1], giv[:, i, 0:1]))
                link(v.tensor_tensor(ohg[:, i, :], iota[:, 0:NG], bc(gf[:, i:i + 1], [P, NG]), ALU.is_equal))
                link(v.tensor_tensor(e4[:, i], rl[:, i, 8:].rearrange("p (g e) -> p g e", g=NG),
                                     bc(ohg[:, i, :].unsqueeze(2), [P, NG, EG]), ALU.mult))
                link(v.tensor_reduce(esel[:, i, :], e4[:, i].rearrange("p g e -> p e g"), AX.X, ALU.add))
                link(v.max(em[:, i, :], esel[:, i, :]))
                link(v.max_index(gi[:, 40 + 8 * i:48 + 8 * i], em[:, i, :], esel[:, i, :]))

            def attention_to_routes(l):
                for i in range(NT + 1):
                    if i < NT:
                        residual_tile(l, i)
                        norm_tile(2 * l, i)
                    if i:
                        route_tile(l, i - 1)
                routing(l)

            def routing(l):
                v.tensor_tensor(gexp, rl[:, :, 0:NG], bc(gm[:, :, 0:1], [P, NT, NG]), ALU.subtract) \
                    .then_inc(S("r_step"), 1)
                dve.wait_ge(S("r_step"), 4 * l + 2)
                link(v.tensor_reduce(gw, gexp, AX.X, ALU.add))
                link(v.reciprocal(gw, gw))
                for j in range(2):
                    link(v.tensor_copy(ef[:, j, :], giv[:, NT:2 * NT, j]))
                    link(v.scalar_tensor_tensor(ef[:, j, :], gf, float(EG), ef[:, j, :], ALU.mult, ALU.add))
                v.tensor_tensor(tmpw, em[:, :, 1], em[:, :, 0], ALU.subtract).then_inc(S("r_step"), 1)
                dve.wait_ge(S("r_step"), 4 * l + 4)
                link(v.tensor_scalar(wj[:, 0, :], tmpw, 1.0, None, ALU.add))
                link(v.reciprocal(wj[:, 0, :], wj[:, 0, :]))
                link(v.tensor_tensor(wj[:, 0, :], wj[:, 0, :], gw, ALU.mult))
                link(v.tensor_tensor(wj[:, 1, :], wj[:, 0, :], tmpw, ALU.mult))
                oh4 = oh.rearrange("p (j i) e -> p j i e", j=2)
                efl = ef.rearrange("p j i -> p (j i)")
                link(v.tensor_tensor(oh, bc(iota[:, 0:NE].unsqueeze(1), [P, 10, NE]),
                                     bc(efl.unsqueeze(2), [P, 10, NE]), ALU.is_equal))
                for j in range(2):
                    link(v.tensor_tensor(oh4[:, j], oh4[:, j], bc(C("valid").unsqueeze(2), [P, NT, NE]), ALU.mult))
                v.tensor_tensor(cnt, oh4[:, 0], oh4[:, 1], ALU.add).then_inc(S("onehot"), 1)
                dve.wait_ge(S("rank_mm"), l + 1)
                link(v.tensor_copy(rank.rearrange("p i e -> p (i e)"), bank(4, 0, NE * (NT + 1))))
                n4 = nxc.rearrange("p (e k) -> p e k", k=4)
                link(v.tensor_tensor(n4, bc(rank[:, NT, :].unsqueeze(2), [P, NE, 4]),
                                     bc(C("steps").unsqueeze(1), [P, NE, 4]), ALU.is_gt))
                link(v.tensor_reduce(nx, n4, AX.X, ALU.add))
                bc3 = big_cmp.rearrange("p (e f) -> p e f", e=NE)
                link(v.tensor_tensor(bc3, bc(iota[:, 0:NE].unsqueeze(1), [P, NE, NE]),
                                     bc(iota[:, 0:NE].unsqueeze(2), [P, NE, NE]), ALU.is_lt))
                link(v.tensor_tensor(bc3, bc(nx.unsqueeze(1), [P, NE, NE]), bc3, ALU.mult))
                link(v.tensor_reduce(xbase, bc3, AX.X, ALU.add))
                th4 = oh_t.rearrange("p (j i) e -> p j i e", j=2)
                for j in range(2):
                    link(v.tensor_tensor(th4[:, j], oh4[:, j], rank[:, 0:NT, :], ALU.mult))
                link(v.tensor_reduce(r10, oh_t, AX.X, ALU.add))
                link(v.tensor_tensor(oh_t, oh, bc(xbase.unsqueeze(1), [P, 10, NE]), ALU.mult))
                link(v.tensor_reduce(x10, oh_t, AX.X, ALU.add))
                link(v.tensor_scalar(b10, x10, float(P), float(PAIRS * P - SLOTS), ALU.mult, ALU.add))
                link(v.scalar_tensor_tensor(b10, efl, -float(SLOTS), b10, ALU.mult, ALU.add))
                link(v.scalar_tensor_tensor(b10, r10, float(SLOTS), b10, ALU.is_ge, ALU.mult))
                link(v.scalar_tensor_tensor(p10, efl, float(SLOTS), b10, ALU.mult, ALU.add))
                link(v.tensor_tensor(p10, p10, r10, ALU.add))
                link(v.tensor_copy(pos_i, p10))
                link(v.tensor_scalar(ib[0], pos_i, P - 1, None, ALU.bitwise_and))
                link(v.tensor_scalar(ib[1], pos_i, 7, None, ALU.logical_shift_right))
                link(v.tensor_copy(s10, ib[0]))
                link(v.tensor_copy(b10, ib[1]))
                link(v.tensor_tensor(a1, bc(iota.unsqueeze(1), [P, 10, P]), bc(s10.unsqueeze(2), [P, 10, P]),
                                     ALU.is_equal))
                link(v.tensor_tensor(bt, bc(iota[:, 0:NE].unsqueeze(1), [P, 10, NE]),
                                     bc(b10.unsqueeze(2), [P, 10, NE]), ALU.is_equal))
                bt4 = bt.rearrange("p (j i) e -> p j i e", j=2)
                for j in range(2):
                    link(v.tensor_tensor(bt4[:, j], bt4[:, j], bc(C("valid").unsqueeze(2), [P, NT, NE]), ALU.mult))
                for j, dst in enumerate((bb, bb2)):
                    link(v.tensor_tensor(dst[:, :, 0:NE], bt4[:, j], bc(C("token").unsqueeze(2), [P, NT, NE]),
                                         ALU.mult))
                    link(v.tensor_tensor(dst[:, :, NE:], bt4[:, j], bc(wj[:, j, :].unsqueeze(2), [P, NT, NE]),
                                         ALU.mult))
                v.tensor_copy(r10, r10).then_inc(S("places"), 1)
                link(v.tensor_tensor(xbase, xbase, nx, ALU.add))
                li3 = big_cmp[:, 0:MORE * NE].rearrange("p (x e) -> p x e", x=MORE)
                link(v.tensor_tensor(li3, bc(xbase.unsqueeze(1), [P, MORE, NE]),
                                     bc(iota[:, 0:MORE].unsqueeze(2), [P, MORE, NE]), ALU.is_le))
                link(v.tensor_reduce(lf[:, 0:MORE], li3, AX.X, ALU.add))
                link(v.tensor_scalar(lf[:, 0:MORE], lf[:, 0:MORE], float(NE - 1), None, ALU.min))
                link(v.tensor_copy(lf[:, MORE:], xbase[:, NE - 1:NE]))
                v.tensor_copy(lists, lf).then_inc(S("lists"), 1)
                dve.wait_ge(S("slot_mm"), l + 1)
                link(v.tensor_copy(wslot, bank(5, NE, 2 * NE)))
                dve.wait_ge(S("lists"), l + 1)
                v.tensor_copy(slot_tok, bank(5, 0, NE)).then_inc(S("slots"), 1)

            def experts(l):
                s = l * PAIRS
                with dve.Fori(0, PAIRS) as i:
                    for j in range(2):
                        dve.wait_ge(S("gate"), i * 2 + (2 * s + j + 1))
                        v.tensor_tensor(hid[:, j].rearrange("p f n -> p (f n)"), bank(j, 2 * SLOTS, 4 * SLOTS),
                                        sg[:, j, :], ALU.mult).then_inc(S("hid"), 1)
                more = dve.value_load(lists[0:1, 16:17], min_val=0, max_val=MORE)
                with dve.If(more > 0):
                    with dve.Fori(0, more) as x:
                        dve.wait_ge(S(f"more_step{l}"), x * 9 + 6)
                        v.tensor_tensor(hidx.rearrange("p f n -> p (f n)"), bank(0, 2 * P, 4 * P),
                                        sgx.rearrange("p f n -> p (f n)"), ALU.mult).then_inc(S(f"more_step{l}"), 1)

            def combine(l):
                for i in range(NT):
                    n = ROWS[i]
                    dve.wait_ge(S(f"yg_in{i % 2}"), 32 * ((3 if i % 2 == 0 else 2) * l + i // 2 + 1))
                    y = yg[i % 2]
                    link(v.scalar_tensor_tensor(X[0:n, i], X[0:n, i], ALPHA, y[0:n, 0], ALU.mult, ALU.add))
                    v.tensor_tensor(X[0:n, i], X[0:n, i], y[0:n, 1], ALU.add).then_inc(S("yg_used"), 1)
                    dve.wait_ge(S("yg_used"), NT * l + i + 1)
                    norm_tile(2 * l + 1, i)

            v.memset(eps_ln, LN_EPS)
            v.memset(eps_hn, HN_EPS)
            v.memset(hmv, 1.0)
            v.memset(mv, 1.0)
            v.memset(hrs, 1.0)
            v.memset(ints[:, 16:], 0)
            link(v.memset(fz, 0.0))
            dve.wait_ge(S("tables"), 64)
            dve.wait_ge(S("inputs"), 48)
            for h in range(2 * RH):
                t = 2 * (h // RH)
                src = ps[:, 1024 * (h % 2):1024 * (h % 2) + TOK]
                dve.wait_ge(S("rope_mm"), h + 1)
                v.tensor_tensor(ropeA, src, rope_v[:, t, :], ALU.mult)
                v.tensor_tensor(ropeB[0:64], src[64:128], rope_v[64:128, t + 1, :], ALU.mult)
                link(v.tensor_tensor(ropeB[64:128], src[0:64], rope_v[0:64, t + 1, :], ALU.mult))
                ins = v.tensor_tensor((qT if h < RH else kT)[:, h % RH, :], ropeA, ropeB, ALU.add)
                ins.then_inc(S("rope_ev"), 1)
                dve.wait_ge(S("rope_ev"), h + 1)
            lg = np.log(np.float32(1) - np.float32(2) ** (np.float32(-5) - np.arange(RH, dtype=np.float32)))
            g_chunk = [float(x) for x in np.exp(lg.astype(np.float32) * np.float32(P))]
            g_step = [float(x) for x in np.exp(lg.astype(np.float32) * np.float32(DS))]

            def decayed(u):
                n, h = u // RH, u % RH
                if u >= 2:
                    dve.wait_ge(S("rr"), u - 1)
                if n:
                    v.tensor_tensor(qd[:, u % 2, :], qT[:, h, P * n:P * n + P], C("qdecay")[:, P * h:P * h + P],
                                    ALU.mult)
                dve.wait_ge(S("rsc"), u + 1)
                v.tensor_tensor(scm[:, u % 2, :], bank(u % 2, 0, P), C("decay")[:, P * h:P * h + P], ALU.mult) \
                    .then_inc(S("rsm"), 1)

            dve.wait_ge(S("zero_out"), 16 * MORE)
            decayed(0)
            for u in range(4 * RH):
                n, h = u // RH, u % RH
                if u + 1 < 4 * RH:
                    decayed(u + 1)
                dve.wait_ge(S("rcp"), u + 1)
                v.bn_stats(hstats[:, h, :], R[:, n, P * h:P * h + P]).then_inc(S("rbs"), 1)
                dve.wait_ge(S("rbs"), u + 1)
                v.bn_aggr(hmv[:, u, :], hstats[:, h, :])
                dve.wait_ge(S("rkv"), u + 1)
                kv = bank(6 + u % 2, 0, P)
                if n == 0:
                    v.tensor_copy(state_p[:, h, :], kv).then_inc(S("rst"), 1)
                else:
                    v.scalar_tensor_tensor(state_p[:, h, :], state_p[:, h, :], g_chunk[h], kv, ALU.mult, ALU.add) \
                        .then_inc(S("rst"), 1)
            for h in range(RH):
                b = h % 2
                if h >= 2:
                    dve.wait_ge(S("rr"), 24 + h - 1)
                v.tensor_tensor(qds[:, b, :], qT[:, h, SEQ:TOK], C("qdecay_s")[:, NS * h:NS * h + NS], ALU.mult)
                dve.wait_ge(S("rsc"), 24 + h + 1)
                v.tensor_tensor(scs[0:NS, b, :], bank(b, 0, NS, rows=(0, NS)),
                                C("decay_s", NS)[:, NS * h:NS * h + NS], ALU.mult)
                if h:
                    dve.wait_ge(S("rkv"), 24 + h)
                v.tensor_tensor(vbd[0:NS].rearrange("p (b e) -> p b e", b=DB),
                                bc(V[0:NS, ST, P * h:P * h + P].unsqueeze(1), [NS, DB, P]),
                                bc(C("kdecay_s", NS)[:, DB * h:DB * h + DB].unsqueeze(2), [NS, DB, P]), ALU.mult) \
                    .then_inc(S("rsm"), 1)
                dve.wait_ge(S("rkv"), 24 + h + 1)
                v.scalar_tensor_tensor(st_s[:, b, :], st_s[:, b, :], g_step[h], ps[:, 3072:4096], ALU.mult, ALU.add) \
                    .then_inc(S("rst"), 1)
            dve.wait_ge(S("srow"), 1)
            for h in range(RH):
                link(v.bn_stats(hstats[0:NS, h, :], R[0:NS, ST, P * h:P * h + P]))
                ins = v.bn_aggr(hmv[0:NS, 24 + h, :], hstats[0:NS, h, :])
            ins.then_inc(S("hmv"), 1)
            dve.wait_ge(S("hsd"), 1)
            dve.wait_ge(S("rcp"), 24)
            link(v.reciprocal(hrs, hrs))
            for i in range(NT):
                n = ROWS[i]
                for h in range(RH):
                    r = R[0:n, i, P * h:P * h + P]
                    q = RH * i + h
                    ins = v.tensor_scalar(r, r, hmv[0:n, q, 0:1], hrs[0:n, q:q + 1], ALU.subtract, ALU.mult)
                link(ins)
                v.tensor_tensor(R[0:n, i], R[0:n, i], G[0:n, i], ALU.mult).then_inc(S("gated"), 1)
            mem_prompt(0)
            mem_sample(0)
            attention_to_routes(0)
            experts(0)
            combine(0)

            dve.wait_ge(S("tm_ev"), 45)
            link(v.tensor_tensor(fz, fz, bc(bf_b.unsqueeze(1), [P, NT, FH]), ALU.add))
            link(v.tensor_scalar(fe, fz, -1.0, None, ALU.mult))
            v.tensor_tensor(fe, fe, fz, ALU.max).then_inc(S("f_step"), 1)
            dve.wait_ge(S("f_step"), 2)
            v.tensor_scalar(fe, fe, 1.0, None, ALU.add).then_inc(S("f_step"), 1)
            dve.wait_ge(S("f_step"), 4)
            v.scalar_tensor_tensor(logf, fz, 0.0, fe, ALU.min, ALU.subtract).then_inc(S("logf"), 1)
            dve.wait_ge(S("cum"), 1)
            v.tensor_copy(cq[:, 0:ST, :], bank(4, 0, FH * ST).rearrange("p (i h) -> p i h", i=ST))
            link(v.tensor_copy(cq[0:NS, ST, :], bank(4, FH * ST, FH * NT, rows=(0, NS))))
            v.tensor_scalar(negc[:, 0:ST, :], cq[:, 0:ST, :], -1.0, None, ALU.mult)
            v.tensor_scalar(negc[0:NS, ST, :], cq[0:NS, ST, :], -1.0, None, ALU.mult)
            for hh in range(4):
                v.tensor_copy(cqs[NS * hh:NS * hh + NS, :], cq[0:NS, ST, hh::4])
            v.tensor_copy(ckp.rearrange("p g c -> p (g c)"), bank(5, 0, PG * DB * FH)).then_inc(S("cum_ev"), 1)

            def prompt_top(h):
                rows = fpr[h % 2]
                dve.wait_ge(S("fnb_cp"), h + 1)
                if h >= 2:
                    dve.wait_ge(S("fp_t"), 3 * (h - 1))
                for n, tiles in enumerate(((1,), (0, 2), (3,))):
                    dve.wait_ge(S("fp_l"), 3 * h + n + 1)
                    for i in tiles:
                        w = P * (i + 1)
                        b, o = LOGIT_AT[i]
                        last = v.scalar_tensor_tensor(rows[:, i, 0:w], bank(b, o, o + w), cq[:, i, h:h + 1],
                                                      fnb[:, h % 2, 0:w], ALU.add, ALU.add)
                    last.then_inc(S("fp_s"), 1)
                dve.wait_ge(S("fp_s"), 3 * h + 3)
                link(v.tensor_tensor(fdiag[h % 2], fdiag[h % 2], bc(C("causal").unsqueeze(1), [P, ST, P]), ALU.add))
                for i in range(ST):
                    last = v.tensor_reduce(mx2[:, h % 2, i:i + 1], rows[:, i, 0:P * (i + 1)], AX.X, ALU.max)
                link(last)
                v.tensor_scalar(nmx2[:, h % 2, :], mx2[:, h % 2, :], -1.0, None, ALU.mult).then_inc(S("fp_m"), 1)

            def prompt_result(h):
                dve.wait_ge(S("fp_e"), 4 * h + 4)
                link(v.reciprocal(rsum2[:, h % 2, :], esum2[:, h % 2, :]))
                dve.wait_ge(S("fox_p"), h + 1)
                v.tensor_tensor(o_rows[:, :, FD * h:FD * h + FD], bank(7, 0, ST * FD).rearrange("p (i d) -> p i d", i=ST),
                                bc(rsum2[:, h % 2, :].unsqueeze(2), [P, ST, FD]), ALU.mult).then_inc(S("fp_ev"), 1)

            dve.wait_ge(S("fm_ev"), 10)
            link(v.memset(qbd, 0.0))
            for r in range(2):
                f = slice(64 * r, 64 * r + 64)
                last = v.tensor_copy(qbd[f, :, r, :], qT[f, :, SEQ:TOK])
            last.then_inc(S("qbd"), 1)
            dve.wait_ge(S("kv_out"), 64)
            for s in range(FH + 2):
                if s < FH:
                    prompt_top(s)
                if s >= 2:
                    prompt_result(s - 2)
            for n in range(DB * PG):
                dve.wait_ge(S("fk_tr"), n + 1)
                if n >= 2:
                    dve.wait_ge(S("fs_l"), n - 1)
                v.tensor_copy(fkT[n % 2][:, 4:6, :], bank(3 + 4 * (n % 2), 0, 2 * P).rearrange("p (h t) -> p h t", h=2)) \
                    .then_inc(S("fk_cp2"), 1)
            dve.wait_ge(S("fs_new"), 1)
            for g in range(PG):
                v.tensor_tensor(
                    fl_t[:, g].rearrange("p h (b t) -> p h b t", t=DS),
                    bank(g, 0, FH * NS).rearrange("p (h b t) -> p h b t", h=FH, t=DS),
                    bc(ckp[:, g, :].rearrange("p (b h) -> p h b", h=FH).unsqueeze(3), [P, FH, DB, DS]),
                    ALU.subtract).then_inc(S("fs_lt"), 1)
            for hh in range(4):
                rr = (NS * hh, NS * hh + NS)
                ins = v.tensor_tensor(fl_r[rr[0]:rr[1], :, PG * PAGE:],
                                      bank(4 + hh % 2, 0, 3 * NS, rows=rr).rearrange("p (r t) -> p r t", r=3),
                                      bc(C("causal_s")[rr[0]:rr[1]].unsqueeze(1), [NS, 3, NS]), ALU.add)
            link(ins)
            v.tensor_tensor(fl_r[:, :, PG * PAGE:], fl_r[:, :, PG * PAGE:], bc(cqs.unsqueeze(2), [P, 3, NS]), ALU.add)
            for r in range(3):
                dve.wait_ge(S("fs_r"), r + 1)
                ins = v.tensor_scalar(fl_r[:, r, 0:PG * PAGE], bank((6, 7, 2)[r], 0, PG * PAGE), cqs[:, r:r + 1],
                                      None, ALU.add)
            link(ins)
            link(v.tensor_reduce(mx[:, 0:3], fl_r, AX.X, ALU.max))
            v.tensor_scalar(nmx[:, 0:3], mx[:, 0:3], -1.0, None, ALU.mult).then_inc(S("fs_m"), 1)
            dve.wait_ge(S("fs_e"), 1)
            link(v.reciprocal(rsum[:, 0:3], esum[:, 0:3]))
            v.tensor_tensor(fl_r, fl_r, bc(rsum[:, 0:3].unsqueeze(2), [P, 3, FLW]), ALU.mult).then_inc(S("fs_n"), 1)
            mem_prompt(1)
            mem_sample(1)
            attention_to_routes(1)
            experts(1)
            combine(1)


_INS = ['x_prompt', 'x_sample', 'mem_prompt', 'state_ret', 'cache_fox_k', 'cache_fox_v', 'cache_fox_logf',
        'cache_mem_k', 'cache_mem_v', 'page_table', 'w_in_a', 'w_in_b', 'w_kv_shared', 'b_forget', 'w_o', 'w_mem_kv',
        'ln1_g', 'ln1_b', 'ln2_g', 'ln2_b', 'w_group', 'b_group', 'w_route', 'b_route', 'w_up', 'w_down']
_OUTS = [(1, SEQ, D), (DB, DS, D), (1, 1, RH, RD, RD), (1, DB, RH, RD, RD), (1, SEQ, FH, FD), (1, SEQ, FH, FD),
         (1, SEQ, FH), (DB, DS, FH, FD), (DB, DS, FH, FD), (DB, DS, FH), (LAYERS, 1, ML, MH, MD),
         (LAYERS, 1, ML, MH, MD)]


def kernel(**inputs):
    import concourse.bacc as _bacc
    from concourse.bass_utils import run_bass_kernel_spmd as _run

    nc = _bacc.Bacc("TRN2", target_bir_lowering=False, num_devices=1)
    consts, rope = shape_constants()
    given = [(n, np.ascontiguousarray(inputs[n])) for n in _INS] + [("consts", consts), ("rope", rope)]
    arrays, args = {}, []
    for name, a in given:
        arrays[f"in_{name}_dram"] = a
        args.append(nc.dram_tensor(f"in_{name}_dram", a.shape, mybir.dt.from_np(a.dtype), kind="ExternalInput").ap())
    outs = [nc.dram_tensor(f"out_{i}_dram", s, F32, kind="ExternalOutput").ap() for i, s in enumerate(_OUTS)]
    build(nc, *args, outs)
    r = _run(nc, [arrays], core_ids=[0])
    return tuple(r.results[0][f"out_{i}_dram"] for i in range(len(_OUTS)))
```

```python
from contextlib import ExitStack

import numpy as np

import concourse.bass as bass
from concourse import mybir

F32 = mybir.dt.float32
F32R = mybir.dt.float32r
I32 = mybir.dt.int32
U32 = mybir.dt.uint32
ALU = mybir.AluOpType
ACT = mybir.ActivationFunctionType
AX = mybir.AxisListType

P = 128
D = 1024
KD = D // P
SEQ, DB, DS = 512, 8, 4
NS = DB * DS
NT = SEQ // P + 1
ST = NT - 1
ROWS = [P] * ST + [NS]
TOK = SEQ + NS
LAYERS = 2
RH, RD = 6, 128
RW = RH * RD
FH, FD = 12, 64
FW = FH * FD
MH, MD, ML = 4, 64, 256
MW = MH * MD
PG, PAGE = 2, 128
NG, EG = 4, 8
NE = NG * EG
DE = 256
ALPHA = float(np.float32((2 * LAYERS) ** 0.25))
LN_EPS, HN_EPS = 1e-5, 1e-6
SLOTS = 64
PAIRS = NE // 2
MORE = 16
STEPS = [SLOTS + P * k for k in range(4)]
NEG = -1.0e30

CONST = {}
CW = 0
for _name, _w in (("ident", P), ("tri", P), ("strict", P), ("ones", P), ("iota", P), 
                  ("decay", RH * P), ("qdecay", RH * P), ("kdecay", RH), ("decay_s", RH * NS), ("qdecay_s", RH * NS),
                  ("kdecay_s", RH * DB), ("causal", P), ("causal_s", NS), ("tri_s", NS), ("batch_s", 60),
                  ("token", 2 * NT), ("valid", NT), ("steps", 4), ("mem_head", 2 * MH), ("block_s", DB * NS),
                  ("fox_head", FH)):
    CONST[_name] = (CW, CW + _w)
    CW += _w


def shape_constants():
    f = np.float32
    c = np.zeros((P, CW), f)

    def put(name, a):
        lo, hi = CONST[name]
        a = np.asarray(a, f)
        c[:a.shape[0], lo:hi] = a.reshape(a.shape[0], hi - lo)

    i = np.arange(P)
    t = np.arange(NS)
    lg = np.log(f(1.0) - f(2.0) ** (f(-5.0) - np.arange(RH, dtype=f))).astype(f)

    def power(h, n):
        return np.exp((lg[h] * np.asarray(n, f)).astype(f)).astype(f)

    put("ident", np.eye(P))
    put("tri", i[:, None] <= i[None, :])
    put("strict", i[:, None] < i[None, :])
    put("ones", np.ones((P, P)))
    put("iota", np.tile(i, (P, 1)))
    diff = i[None, :] - i[:, None]
    put("decay", np.stack([np.where(diff >= 0, power(h, np.maximum(diff, 0)), 0) for h in range(RH)], 1))
    put("qdecay", np.stack([np.tile(power(h, i + 1), (P, 1)) for h in range(RH)], 1))
    put("kdecay", np.stack([power(h, P - 1 - i) for h in range(RH)], 1))
    same = (t[:, None] // DS) == (t[None, :] // DS)
    ds = t[None, :] - t[:, None]
    put("decay_s", np.stack([np.where(same & (ds >= 0), power(h, np.maximum(ds, 0)), 0) for h in range(RH)], 1))
    put("qdecay_s", np.stack([np.tile(power(h, t % DS + 1), (P, 1)) for h in range(RH)], 1))
    put("kdecay_s", np.stack([np.where((t[:, None] // DS) == np.arange(DB)[None, :],
                                       power(h, DS - 1 - t % DS)[:, None], 0) for h in range(RH)], 1))
    put("causal", np.where(i[None, :] <= i[:, None], 0, NEG))
    put("causal_s", np.where(same & (ds <= 0), 0, NEG))
    put("tri_s", same & (ds >= 0))
    put("fox_head", (i % 64)[:, None] // DS == np.arange(FH)[None, :])
    put("block_s", np.tile(((t[None, :] // DS) == np.arange(DB)[:, None])[None], (P, 1, 1)))
    b = np.zeros((P, 60), f)
    b[:, 28:32] = 1
    put("batch_s", b)
    valid = i[:, None] < np.array(ROWS)[None, :]
    put("token", np.tile((i[:, None] + P * np.arange(NT)[None, :]) * valid, (1, 2)))
    put("valid", valid)
    r = i % 32
    put("mem_head", np.tile((r[:, None] // DS == np.arange(MH)[None, :]) & (r[:, None] < MH * DS), (1, 2)))
    put("steps", np.tile(np.array(STEPS), (P, 1)))
    pos = np.concatenate([np.arange(SEQ), PG * PAGE + t % DS]).astype(f)
    half = RD // 2
    inv = (f(10000.0) ** (-np.arange(half, dtype=f) / f(half))).astype(f)
    ang = (inv[:, None] * pos[None, :]).astype(f)
    cos, sin = np.cos(ang).astype(f), np.sin(ang).astype(f)
    ks = f(RD ** -0.5)
    cs, sn = np.concatenate([cos, cos]), np.concatenate([sin, -sin])
    rope = np.concatenate([cs, sn, cs * ks, sn * ks], axis=1).astype(f)
    return c, rope


def build(nc, x_prompt, x_sample, mem_prompt, state_ret, cache_fox_k, cache_fox_v, cache_fox_logf, cache_mem_k,
          cache_mem_v, page_table, w_in_a, w_in_b, w_kv_shared, b_forget, w_o, w_mem_kv, ln1_g, ln1_b, ln2_g, ln2_b,
          w_group, b_group, w_route, b_route, w_up, w_down, consts, rope, outs):
    (y_prompt, y_sample, ret_prompt, ret_sample, fox_k_p, fox_v_p, fox_f_p, fox_k_s, fox_v_s, fox_f_s,
     mem_k_p, mem_v_p) = outs
    ctx = ExitStack()
    sems = {}

    def S(name):
        if name not in sems:
            sems[name] = ctx.enter_context(nc.semaphore(name))
        return sems[name]

    with ctx:
        where = {}

        def sb(name, w, dt=F32):
            t = ctx.enter_context(nc.sbuf_tensor(name, [P, w], dt))
            where[name] = nc.sbuf_base - 4 * w
            return t

        def rounded(name, w):
            return nc.alloc_sbuf_tensor_at(name + "_r", [P, w], F32R, offset=where[name])

        x_rows_t, x_cols_t, mix_t = sb("x_rows", NT * D), sb("x_cols", KD * TOK), sb("mix_cols", KD * TOK)
        const_t = sb("const", CW)
        big = sb("expert_weights", 4 * 3072)
        ring = sb("weight_ring", 3 * 3072)
        work = sb("work", 2 * NT * RW)
        mem_kv_t, mem_kt_t = sb("mem_kv", 2 * 2 * 512), sb("mem_kt", 2 * 2 * ML)
        ln_t = sb("ln_gb", 2 * D)
        small = sb("small", 1100)
        queries_t = sb("mem_queries", 2 * (DB + 1) * MH * DS)
        ints = sb("ints", 200, I32)
        index_t = sb("max_index", 10 * 8, U32)
        big_r, work_r = rounded("expert_weights", 4 * 3072), rounded("work", 2 * NT * RW)
        ring_r, mix_lo = rounded("weight_ring", 3 * 3072), rounded("mix_cols", KD * TOK)
        x_cols_r = rounded("x_cols", KD * TOK)
        ps = ctx.enter_context(nc.psum_tensor("ps", [P, 8 * 512], F32))
        xs = [nc.dram_tensor(f"stream_rows{l}", [TOK, D], F32, kind="Internal").ap() for l in range(LAYERS)]
        ys_all = nc.dram_tensor("expert_rows", [(PAIRS + MORE) * P, D], F32, kind="Internal").ap()
        ys = [ys_all, ys_all]

        def view(t, at, *shape, rows=(0, P)):
            n = int(np.prod(shape))
            v = t[rows[0]:rows[1], at:at + n]
            if len(shape) == 2:
                v = v.rearrange("p (a b) -> p a b", a=shape[0])
            elif len(shape) == 3:
                v = v.rearrange("p (a b c) -> p a b c", a=shape[0], b=shape[1])
            return v

        def C(name, rows=P):
            lo, hi = CONST[name]
            return const_t[0:rows, lo:hi]

        def bank(b, lo=0, hi=512, rows=(0, P)):
            return ps[rows[0]:rows[1], b * 512 + lo:b * 512 + hi]

        X = view(x_rows_t, 0, NT, D)
        XT = view(x_cols_t, 0, KD, TOK)
        MX = view(mix_t, 0, KD, TOK)
        XT_r, XT_lo = view(mix_lo, 0, KD, TOK), view(x_cols_r, 0, KD, TOK)
        ident = C("ident")
        memkv = view(mem_kv_t, 0, 2, 2, 512)
        memkt = view(mem_kt_t, 0, 2, 2, ML)
        qT = view(big, 0, 6, TOK)
        kT = view(big, 6 * TOK, 6, TOK)
        V = view(big, 12 * TOK, NT, RW)
        free0 = 12 * TOK + NT * RW
        state_p = view(big, free0, RH, P)
        scm = [view(x_cols_t, 0, RH, P), view(big, free0 + RW, RH, P)]
        kd = [view(x_cols_t, RW, RH, P), view(x_cols_t, 3 * RW, RH, P)]
        qd = [view(x_cols_t, 2 * RW, RH, P), view(x_cols_t, 4 * RW, RH, P)]
        kds = view(big, free0 + 2 * RW, 2, P)
        qds = view(big, free0 + 2 * RW + 256, 2, NS)
        scs = view(big, free0 + 2 * RW + 320, 2, NS)
        vbd = [view(x_cols_t, 0, DB * P), view(x_cols_t, DB * P, DB * P)]
        qbs = view(x_cols_t, 5 * RW, 2, DB, NS)
        zeros = view(big, free0, D)
        assert free0 + 1920 <= 4 * 3072
        R = view(work, 0, NT, RW)
        G = view(work, NT * RW, NT, RW)
        rope_v = view(work, 0, 4, TOK)
        mem_rows = view(work, NT * RW, 2, D)
        ropeA = view(work, 4 * TOK, TOK)
        ropeB = view(work, 5 * TOK, TOK)
        memT = view(big, 12 * TOK, KD, ML)
        st_s = view(mix_t, 0, 3, DB * P)
        at = [0]

        def sm(*shape):
            v = view(small, at[0], *shape)
            at[0] += int(np.prod(shape))
            assert at[0] <= 900
            return v

        stats, mv, rstd = sm(NT, 12), sm(NT, 2), sm(NT)
        hstats, hmv, hrs = sm(RH, 6), sm(NT * RH, 2), sm(NT * RH)
        mx, nmx, esum, rsum = sm(4), sm(4), sm(4), sm(4)
        mx2, nmx2, esum2, rsum2 = sm(2, 4), sm(2, 4), sm(2, 4), sm(2, 4)
        logf = sm(NT, FH)
        cq, negc = sm(NT, FH), sm(NT, FH)
        fz, fe = sm(NT, FH), sm(NT, FH)
        past_f = sm(PG, DB * FH)
        bf_b = sm(FH)
        biasr = sm(NG + NE)
        eps_ln, eps_hn = sm(1), sm(1)
        wslot = sm(PAIRS + MORE)
        pages = ints[:, 0:16]
        slot_tok = ints[:, 16:16 + 32]
        pos_i = ints[:, 48:58]
        lists = ints[:, 64:64 + 17]
        idx_now = ints[:, 96:97]
        ib = [ints[:, 100 + 10 * k:110 + 10 * k] for k in range(3)]

        def cols(w, lo, hi):
            return w[:, lo:hi].rearrange("(k p) n -> p k n", p=P)

        mem_chunks = [cols(w_mem_kv[l], 256 * kv, 256 * kv + 256) for l in range(LAYERS) for kv in range(2)]

        def mem_chunk_view(n):
            return view(big, 2048 * (n % 3), KD, 256)

        chunks = []
        for n in range(4):
            chunks.append((cols(w_in_a[0], 384 * n, 384 * n + 384), ("rope_mm", 3 * n + 3)))
        for n in range(4):
            chunks.append((cols(w_in_a[0], 1536 + 384 * n, 1920 + 384 * n), ("tm_mm", 5 * n + 5)))
        chunks.append((cols(w_in_a[0], 3072, 3328), ("fm_mm", 2)))
        for n in range(4):
            chunks.append((cols(w_kv_shared, 384 * n, 384 * n + 384), ("tm_mm", 25 + 5 * n)))
        chunks.append((cols(w_kv_shared, 1536, 1548), ("tm_mm", 45)))
        chunks.append((cols(w_in_b[0], 0, 384), ("fm_mm", 5)))
        chunks.append((cols(w_in_b[0], 384, 768), ("fm_mm", 8)))
        chunks.append((cols(w_in_b[0], 768, 1024), ("fm_mm", 10)))
        CH_A, CH_S, CH_B, CH_END = 0, 9, 14, 17
        FM0 = 512 - TOK // 2

        def w_raw(m, t=None):
            return view(ring if t is None else t, 3072 * (m % 2), KD, chunks[m][0].shape[-1])

        def w_lo(m):
            return w_raw(m, ring_r)

        def w_r(m):
            w = chunks[m][0].shape[-1]
            if m == 10:
                return view(big_r, 6 * TOK, KD, w)
            if (m % 2 == 0) == (m < CH_S):
                return view(ring_r, 6144, KD, w)
            return view(work_r, 3840 if m < 4 else 0, KD, w)

        def chunk_split(eng, m):
            eng.wait_ge(S("w_lo"), 2 * m + 2)

        wo_v = view(ring, 0, KD, D)
        wo_r, wo_lo = view(big_r, 0, KD, D), view(ring_r, 0, KD, D)
        mix_r = [view(big_r, KD * D + KD * P * k, KD, P) for k in range(2)]
        MX_lo = view(mix_lo, 0, KD, TOK)
        wr = view(ring, KD * D, KD, NG + NE)

        WU = [view(big, 0, KD, 512), view(big, 4096, KD, 512), view(ring, 0, KD, 512), view(ring, 4096, KD, 512)]
        WD = [view(big, 8192, 2, D), view(big, 8192 + 2048, 2, D), view(mix_t, 0, 2, D), view(mix_t, 2048, 2, D)]
        xg, yb = view(work, 0, D), view(work, D, D)
        xgT = view(work, 2 * D, KD, P)
        sg = view(work, 3 * D, 2, P)
        hid = view(work, 3 * D + 256, 2, 2, SLOTS)
        sgx = view(work, 3 * D + 512, 2, P)
        hidx = view(work, 3 * D + 768, 2, P)
        yg = [view(work, 0, 2, D), view(big, 0, 2, D)]
        RB = 0
        rl = view(work, RB, NT, 40)
        gm = view(work, 200, NT, 8)
        em = view(work, 240, NT, 8)
        esel = view(work, 280, NT, 8)
        gf = view(work, 320, NT)
        gexp = view(work, 325, NT, NG)
        gw = view(work, 345, NT)
        ohg = view(work, 350, NT, NG)
        ef = view(work, 370, 2, NT)
        wj = view(work, 380, 2, NT)
        tmpw = view(work, 390, NT)
        s10, b10, p10 = [view(work, 400 + 10 * k, 10) for k in range(3)]
        oh = view(work, 450, 10, NE)
        oh_t = view(work, 770, 10, NE)
        cnt = view(work, 1090, NT + 1, NE)
        sums = [view(work, 1284 + 48 * k, 48) for k in range(2)]
        further = view(work, 1380, NE)
        place = view(work, 1412, NT, NE)
        before = view(work, 1572, MORE, NE)
        a1 = view(work, 2530, 10, P)
        bb = view(work, 3810, 10, 2 * NE)
        esw = view(work, 6976, NT * NG * EG)
        nxc = view(work, 7136, NE * 4)
        lf = view(work, 7264, 17)
        bt = view(work, 7296, 10, NE)
        gi = index_t[:, :]

        mvc = view(work, 0, DB, 2 * MW)
        mkc = view(x_cols_t, 0, DB, 2, MW)
        qmb = view(queries_t, 0, 2, (DB + 1) * MH * DS)
        mpr = view(work, 4096, 2, MH, ML)
        mprT = view(work, 6144, 2 * MH, P)
        mkcT = view(work, 4096, 2, 2, ML)
        mexp = view(work, 5120, 2, ML)
        mp_s = view(work, 5632, 4, P)
        mhead = view(work, 6144, 2 * MH, MD)
        mres = view(work, 6656, 2, 2, MD)
        k_rows = view(work, NT * RW, NT, FW)
        fpr = [view(work, 4 * SEQ * k, ST, SEQ) for k in range(2)]
        fdiag = [view(work, 4 * SEQ * k, ST, SEQ + P)[:, :, 0:P] for k in range(2)]
        fprT = view(work, 8 * SEQ, 2, 10 * P)
        fnb = view(work, 8 * SEQ + 20 * P, 2, SEQ)
        PT_AT = {3: 0, 2: 4 * P, 0: 7 * P, 1: 8 * P}
        LOGIT_AT = {1: (0, 0), 0: (1, 0), 2: (1, P), 3: (2, 0)}
        o_rows = view(x_cols_t, 0, ST, FW)
        pages_at = [view(ring, FW * n, FW) for n in range(12)] + [view(big, free0 + FW * n, FW) for n in range(2)] \
            + [view(x_cols_t, ST * FW, FW)]
        fkc = pages_at + [view(mix_t, 0, FW)]
        fvc = pages_at + [view(work, FW, FW)]
        QR, GR, FLW = FH * DS, DB // 2, PG * PAGE + NS
        qbd = view(mix_t, FW, 6, DB, QR)
        cq_rows = view(x_cols_t, (ST + 1) * FW, DB, 64)
        negp_rows = view(ln_t, 0, PG, DB, QR)
        negc_rows = view(ln_t, PG * DB * QR, QR)
        own_row = view(ln_t, (PG * DB + 1) * QR, DB, QR)
        fkT = [view(work, 3072, 6, P), view(work, 3840, 6, P)]
        fl_r = view(work, 4608, GR, FLW)
        fs_p = view(work, 5760, GR, PG + 1, P)
        fhead = view(work, 2 * FW, FH, FD)
        fres = view(work, 3 * FW, GR, 2, FD)
        mqT = MX[:, 6:8]
        negp = view(small, 900, PG, DB * FH)

        block = ctx.enter_context(nc.Block())

        @block.sync
        def _(sp):
            def mem_chunk(n):
                sp.dma_start(mem_chunk_view(n), mem_chunks[n]).then_inc(S(f"mkv_w{n % 3}"), 16)

            lo, hi = CONST["ident"]
            sp.dma_start(const_t[:, lo:hi], consts[:, lo:hi]).then_inc(S("mem_in"), 16)
            sp.dma_start(mem_rows, mem_prompt[0].rearrange("(t p) d -> p t d", p=P)).then_inc(S("mem_in"), 16)
            mem_chunk(0)
            mem_chunk(1)
            sp.dma_start(X[:, 0:ST, :], x_prompt[0].rearrange("(t p) d -> p t d", p=P)).then_inc(S("x_in"), 16)
            sp.dma_start(X[0:NS, ST, :], x_sample.rearrange("b t d -> (b t) d")).then_inc(S("x_in"), 16)
            sp.dma_start(view(work, 0, 4 * TOK), rope).then_inc(S("tables"), 16)
            sp.dma_start(const_t[:, hi:], consts[:, hi:]).then_inc(S("tables"), 16)
            sp.dma_start(bf_b, b_forget.rearrange("(a h) -> a h", a=1).partition_broadcast(P)).then_inc(S("tables"), 16)
            sp.dma_start(pages[0:1, :], page_table.rearrange("b g -> (b g)").rearrange("(a n) -> a n", a=1)) \
                .then_inc(S("tables"), 16)

            def chunk(m):
                if m >= 2:
                    sp.wait_ge(S(chunks[m - 2][1][0]), chunks[m - 2][1][1])
                sp.dma_start(w_raw(m), chunks[m][0]).then_inc(S(f"w_in{m % 2}"), 16)

            def ln_params(p):
                if p:
                    sp.wait_ge(S("x_ready"), NT * p)
                g, b = ((ln1_g, ln1_b), (ln2_g, ln2_b))[p % 2]
                sp.dma_start(ln_t[:, 0:D], g[p // 2:p // 2 + 1, :].partition_broadcast(P)).then_inc(S("ln_in"), 16)
                sp.dma_start(ln_t[:, D:2 * D], b[p // 2:p // 2 + 1, :].partition_broadcast(P)).then_inc(S("ln_in"), 16)

            def output_weights(l):
                sp.wait_ge(S("fm_mm"), 2 if l == 0 else 10)
                if l:
                    sp.wait_ge(S("tok_done"), 2)
                for half in range(2):
                    sp.dma_start(wo_v[:, :, 512 * half:512 * half + 512], cols(w_o[l], 512 * half, 512 * half + 512)) \
                        .then_inc(S("wo_in"), 16)
                s = S("route_in")
                sp.dma_start(wr[:, :, 0:NG], w_group[l].rearrange("(k p) g -> p k g", p=P)).then_inc(s, 16)
                for g in range(NG):
                    sp.dma_start(wr[:, :, NG + EG * g:NG + EG * g + EG],
                                 w_route[l, g].rearrange("(k p) e -> p k e", p=P)).then_inc(s, 16)
                sp.dma_start(biasr[:, 0:NG], b_group[l:l + 1, :].partition_broadcast(P)).then_inc(s, 16)
                sp.dma_start(biasr[:, NG:], b_route[l:l + 1].rearrange("a g e -> a (g e)").partition_broadcast(P)) \
                    .then_inc(s, 16)

            def mem_keys(l):
                if l == 0:
                    sp.wait_ge(S("rkv"), 2 * ST + RH)
                else:
                    sp.wait_ge(S("tok_done"), 2)
                for b in range(DB):
                    sp.dma_start(mkc[:, b], cache_mem_k[l, b].rearrange("(t p) h d -> p t (h d)", p=P)) \
                        .then_inc(S("mk_in"), 16)

            def mem_values(l):
                sp.wait_ge(S("tok_done"), l + 1)
                for b in range(DB):
                    sp.dma_start(mvc[:, b], cache_mem_v[l, b].rearrange("(t p) h d -> p t (h d)", p=P)) \
                        .then_inc(S("mv_in"), 16)

            def expert(l, e, b):
                sp.dma_start(WU[b], w_up[l].rearrange("g e (k p) f -> p (g e) k f", p=P)[:, bass.ds(e, 1)]
                             .rearrange("p a k f -> p (a k) f")).then_inc(S(f"exp_in{b}"), 16)
                sp.dma_start(WD[b], w_down[l].rearrange("g e (k p) f -> p (g e) k f", p=P)[:, bass.ds(e, 1)]
                             .rearrange("p a k f -> p (a k) f")).then_inc(S(f"exp_in{b}"), 16)

            def experts(l):
                sp.wait_ge(S("wo_mm"), 10 * (l + 1))
                for b in range(2):
                    expert(l, b, b)
                sp.wait_ge(S("rt_mm"), NT * (l + 1))
                for b in range(2, 4):
                    expert(l, b, b)
                ln_params(2 * l + 1)
                with sp.Fori(1, NE // 4) as r:
                    for b in range(4):
                        sp.wait_ge(S("down_done"), r * 4 + (NE * l + b - 3))
                        expert(l, r * 4 + b, b)
                sp.wait_ge(S("lists"), l + 1)
                more = sp.value_load(lists[0:1, 16:17], min_val=0, max_val=MORE)
                with sp.If(more > 0):
                    with sp.Fori(0, more) as x:
                        sp.wait_ge(S(f"more_step{l}"), x * 9 + 1)
                        e = sp.value_load(lists[0:1, bass.ds(x, 1)], min_val=0, max_val=NE - 1)
                        sp.dma_start(WU[0], w_up[l].rearrange("g e (k p) f -> p (g e) k f", p=P)
                                     [:, bass.ds(e, 1)].rearrange("p a k f -> p (a k) f")) \
                            .then_inc(S(f"more_w{l}"), 16)
                        sp.dma_start(WD[0], w_down[l].rearrange("g e (k p) f -> p (g e) k f", p=P)
                                     [:, bass.ds(e, 1)].rearrange("p a k f -> p (a k) f")) \
                            .then_inc(S(f"more_w{l}"), 16)
                sp.wait_ge(S("down_done"), NE * (l + 1))

            chunk(0)
            mem_chunk(2)
            sp.wait_ge(S("mkv_mm"), 2)
            mem_chunk(3)
            for m in range(1, CH_S):
                chunk(m)
            ln_params(0)
            sp.wait_ge(S("fm_mm"), 2)
            for h in range(RH):
                if h >= 3:
                    sp.wait_ge(S(f"st_out{h % 3}"), 16 * (h // 3))
                sp.dma_start(st_s[:, h % 3].rearrange("p (b e) -> p b e", b=DB),
                             state_ret[0, :, h].rearrange("b d e -> d b e")).then_inc(S(f"st_in{h % 3}"), 16)
            mem_keys(0)
            output_weights(0)
            mem_values(0)
            experts(0)
            sp.wait_ge(S("yg_in0"), 32)
            for n in range(CH_S, CH_END):
                chunk(n)
            sp.wait_ge(S("tables"), 64)
            sp.wait_ge(S("fm_mm"), 10)
            sp.wait_ge(S("x_ready"), 2 * NT)
            for n in range(DB * PG):
                pg = sp.value_load(pages[0:1, n:n + 1], min_val=0, max_val=cache_fox_k.shape[0] - 1)
                sp.dma_start(fkc[n], cache_fox_k.rearrange("n s h d -> s n (h d)")[:, bass.ds(pg, 1)]
                             .rearrange("s a f -> s (a f)")).then_inc(S("fk_in"), 16)
            for n in range(DB * PG):
                sp.wait_ge(S("fk_tr"), n + 1)
                pg = sp.value_load(pages[0:1, n:n + 1], min_val=0, max_val=cache_fox_k.shape[0] - 1)
                sp.dma_start(fvc[n], cache_fox_v.rearrange("n s h d -> s n (h d)")[:, bass.ds(pg, 1)]
                             .rearrange("s a f -> s (a f)")).then_inc(S("fv_in"), 16)
            sp.wait_ge(S("fs_l"), DB * PG)
            ln_params(2)
            mem_keys(1)
            output_weights(1)
            mem_values(1)
            experts(1)
            for i in range(ST):
                sp.wait_ge(S("x_ready"), 3 * NT + i + 1)
                sp.dma_start(y_prompt[0, P * i:P * i + P], X[:, i]).then_inc(S("x_out"), 16)
            sp.wait_ge(S("x_ready"), 4 * NT)
            sp.dma_start(y_sample.rearrange("b t d -> (b t) d"), X[0:NS, ST]).then_inc(S("x_out"), 16)

        @block.gpsimd
        def _(pool):
            def dispatch(l):
                for i in range(NT):
                    pool.wait_ge(S("x_ready"), NT * 2 * l + i + 1)
                    pool.dma_start(xs[l][P * i:P * i + ROWS[i]], X[0:ROWS[i], i]).then_inc(S("xs_out"), 16)
                pool.wait_ge(S("slots"), l + 1)
                pool.wait_ge(S("xs_out"), 80 * (l + 1))
                with pool.Fori(0, PAIRS + 1) as i:
                    b = l * (PAIRS + 1)
                    pool.wait_ge(S("xg_free"), i + (b + 1))
                    nc.gpsimd.tensor_copy(idx_now, slot_tok[:, bass.ds(i, 1)]).then_inc(S("idx"), 1)
                    pool.wait_ge(S("idx"), i + (b + 1))
                    pool.sem_inc(S("gathers"), 1)
                    pool.indirect_dma_start(xg, None, xs[l], bass.IndirectOffsetOnAxis(idx_now, 0)) \
                        .then_inc(S("xg_in"), 16)
                    pool.wait_ge(S("xg_in"), i * 16 + (16 * b + 16))
                more = pool.value_load(lists[0:1, 16:17], min_val=0, max_val=MORE)
                with pool.If(more > 0):
                    with pool.Fori(0, more) as x:
                        pool.wait_ge(S(f"more_step{l}"), x * 9 + 1)
                        nc.gpsimd.tensor_copy(idx_now, slot_tok[:, bass.ds(x + PAIRS, 1)]) \
                            .then_inc(S(f"more_step{l}"), 1)
                        pool.wait_ge(S(f"more_step{l}"), x * 9 + 2)
                        pool.sem_inc(S("gathers"), 1)
                        pool.indirect_dma_start(xg, None, xs[l], bass.IndirectOffsetOnAxis(idx_now, 0)) \
                            .then_inc(S(f"more_x{l}"), 16)
                        pool.wait_ge(S(f"more_step{l}"), x * 9 + 9)
                        pool.dma_start(ys[l].rearrange("(b p) d -> p b d", p=P)[:, bass.ds(x + PAIRS, 1)]
                                       .rearrange("p a d -> p (a d)"), yb).then_inc(S(f"more_out{l}"), 16)
                        pool.wait_ge(S(f"more_out{l}"), x * 16 + 16)
                        pool.sem_inc(S(f"more_step{l}"), 1)
                pool.wait_ge(S("y_out"), 16 * PAIRS * (l + 1) + 16)
                for i in range(NT + 1):
                    if i < NT:
                        n = ROWS[i]
                        if i >= 2:
                            pool.wait_ge(S("yg_used"), NT * l + i - 1)
                        for j in range(2):
                            pool.indirect_dma_start(yg[i % 2][0:n, j], None, ys[l],
                                                    bass.IndirectOffsetOnAxis(pos_i[0:n, NT * j + i:NT * j + i + 1],
                                                                              0)).then_inc(S(f"yg_in{i % 2}"), 16)
                    if i:
                        q = i - 1
                        pool.wait_ge(S(f"yg_in{q % 2}"), 32 * ((3 if q % 2 == 0 else 2) * l + q // 2 + 1))
                        y = yg[q % 2][0:ROWS[q]]
                        nc.gpsimd.tensor_tensor(y[:, 0], y[:, 0], y[:, 1], ALU.add).then_inc(S("yg_sum"), 1)

            nc.gpsimd.memset(zeros, 0.0).then_inc(S("pool_zero"), 1)
            pool.wait_ge(S("pool_zero"), 1)
            pool.wait_ge(S("rope_mm"), 1)
            for b in range(MORE):
                pool.dma_start(ys_all[(PAIRS + b) * P:(PAIRS + b + 1) * P], zeros).then_inc(S("zero_out"), 16)
            pool.wait_ge(S("mkv_ev"), 8)
            for l in range(LAYERS):
                for out, lo in ((mem_k_p, 0), (mem_v_p, MW)):
                    pool.dma_start(out[l, 0].rearrange("(t p) h d -> p t (h d)", p=P), memkv[:, l, :, lo:lo + MW]) \
                        .then_inc(S("mp_out"), 16)
            pool.wait_ge(S("rst"), 2 * ST)
            pool.dma_start(ret_prompt[0, 0].rearrange("h d e -> d h e"), state_p).then_inc(S("rs_out"), 16)
            for h in range(RH):
                pool.wait_ge(S("rst"), 2 * ST + h + 1)
                pool.dma_start(ret_sample[0, :, h].rearrange("b d e -> d b e"),
                               st_s[:, h % 3].rearrange("p (b e) -> p b e", b=DB)).then_inc(S(f"st_out{h % 3}"), 16)
            dispatch(0)
            pool.wait_ge(S("tables"), 64)
            for n in range(DB * PG):
                pg = pool.value_load(pages[0:1, n:n + 1], min_val=0, max_val=cache_fox_k.shape[0] - 1)
                pool.dma_start(past_f[:, n % PG, FH * (n // PG):FH * (n // PG) + FH],
                               cache_fox_logf.rearrange("n s h -> s n h")[:, bass.ds(pg, 1)]
                               .rearrange("s a h -> s (a h)")).then_inc(S("pf_in"), 16)
            pool.wait_ge(S("tm_ev"), 40)
            pool.dma_start(fox_k_p[0].rearrange("(t p) h d -> p t (h d)", p=P), k_rows[:, 0:ST]) \
                .then_inc(S("kv_out"), 16)
            pool.dma_start(fox_k_s.rearrange("b t h d -> (b t) (h d)"), k_rows[0:NS, ST]).then_inc(S("kv_out"), 16)
            pool.dma_start(fox_v_p[0].rearrange("(t p) h d -> p t (h d)", p=P), V[:, 0:ST]).then_inc(S("kv_out"), 16)
            pool.dma_start(fox_v_s.rearrange("b t h d -> (b t) (h d)"), V[0:NS, ST]).then_inc(S("kv_out"), 16)
            pool.wait_ge(S("logf"), 1)
            pool.dma_start(fox_f_p[0].rearrange("(t p) h -> p t h", p=P), logf[:, 0:ST]).then_inc(S("f_out"), 16)
            pool.dma_start(fox_f_s.rearrange("b t h -> (b t) h"), logf[0:NS, ST]).then_inc(S("f_out"), 16)
            pool.wait_ge(S("fm_ev"), 10)
            pool.wait_ge(S("cum_ev"), 1)
            nc.gpsimd.memset(cq_rows[0:NS], 0.0).then_inc(S("pool_zero"), 1)
            nc.gpsimd.memset(qbd, 0.0).then_inc(S("pool_zero"), 1)
            pool.wait_ge(S("pool_zero"), 3)
            for h in range(FH):
                f = slice(64 * (h % 2), 64 * (h % 2) + 64)
                nc.gpsimd.tensor_copy(qbd[f, h // 2, :, DS * h:DS * h + DS],
                                      qT[f, h // 2, SEQ:TOK].rearrange("p (b t) -> p b t", b=DB)).then_inc(S("qbd"), 1)
            def by_row(a, *shape):
                return a.broadcast_to(list(shape))

            token = ident[0:NS, 0:NS].rearrange("p (b t) -> p b t", b=DB).unsqueeze(2)
            nc.gpsimd.tensor_tensor(cq_rows[0:NS, :, 0:QR].rearrange("p b (h t) -> p b h t", t=DS),
                                    by_row(cq[0:NS, ST, :].unsqueeze(1).unsqueeze(3), NS, DB, FH, DS),
                                    by_row(token, NS, DB, FH, DS), ALU.mult).then_inc(S("qbd"), 1)
            nc.gpsimd.tensor_copy(own_row[0:NS].rearrange("p b (h t) -> p b h t", t=DS),
                                  by_row(token, NS, DB, FH, DS)).then_inc(S("qbd"), 1)
            nc.gpsimd.tensor_copy(negc_rows[0:NS].rearrange("p (h t) -> p h t", t=DS),
                                  by_row(negc[0:NS, ST, :].unsqueeze(2), NS, FH, DS)).then_inc(S("qbd"), 1)
            pool.wait_ge(S("qbd"), FH + 3)
            nc.gpsimd.tensor_copy(negp_rows.rearrange("p g b (h t) -> p (g b h) t", t=DS),
                                  by_row(negp.rearrange("p g c -> p (g c)").unsqueeze(2), P, PG * DB * FH, DS)) \
                .then_inc(S("qbd"), 1)
            dispatch(1)
            pool.wait_ge(S("x_out"), 16 * NT)
            pool.wait_ge(S("f_out"), 32)
            pool.wait_ge(S("kv_out"), 64)
            pool.wait_ge(S("mp_out"), 64)
            pool.wait_ge(S("rs_out"), 16)
            for k in range(3):
                pool.wait_ge(S(f"st_out{k}"), 32)

        @block.tensor
        def _(pe):
            mm, tr = nc.tensor.matmul, nc.tensor.transpose

            def cols_of(p, i):
                n = ROWS[i]
                if p:
                    pe.wait_ge(S("x_ready"), NT * (p - 1) + i + 1)
                for half in range(2):
                    j = 10 * p + 2 * i + half
                    if j >= 2:
                        pe.wait_ge(S("xt_cp"), j - 1)
                    for k in range(4):
                        kk = 4 * half + k
                        last = tr(bank(j % 2, n * k, n * k + n), X[0:n, i, kk * P:kk * P + P], ident[0:n, 0:n])
                    last.then_inc(S("xt_mm"), 1)

            def split_product(o, a_r, a_lo, b_r, b_lo, k):
                mm(o, a_r, b_r, start=(k == 0), stop=False)
                mm(o, a_r, b_lo, start=False, stop=False)
                return mm(o, a_lo, b_r, start=False, stop=(k == KD - 1))

            def feature_major(n, m, lo):
                b, f = 2 * (n % 2), slice(lo, lo + P)
                for o, t in ((bank(b, FM0), slice(0, TOK // 2)), (bank(b + 1, 0, TOK // 2), slice(TOK // 2, TOK))):
                    for k in range(KD):
                        last = split_product(o, w_r(m)[:, k, f], w_lo(m)[:, k, f], XT_r[:, k, t], XT_lo[:, k, t], k)
                return last

            def token_major(n, m, i):
                t = slice(P * i, P * i + ROWS[i])
                o = bank(4 + n % 4, 0, chunks[m][0].shape[-1], rows=(0, ROWS[i]))
                for k in range(KD):
                    last = split_product(o, XT_r[:, k, t], XT_lo[:, k, t], w_r(m)[:, k, :], w_lo(m)[:, k, :], k)
                return last

            def mem_prompt_attention(l):
                n0 = ST * l

                def logits(i):
                    if n0 + i >= 2:
                        pe.wait_ge(S("mp_e"), n0 + i - 1)
                    for h in range(MH):
                        f = slice(64 * (h % 2), 64 * (h % 2) + 64)
                        o = ML * (h // 2)
                        last = mm(bank(2 * (i % 2) + h % 2, o, o + ML), mqT[f, h // 2, P * i:P * i + P],
                                  memkt[f, l, h // 2, :], start=True, stop=True)
                    last.then_inc(S("mp_l"), 1)

                def turn(i):
                    pe.wait_ge(S("mp_n"), n0 + i + 1)
                    for r in range(2):
                        if n0 + i:
                            pe.wait_ge(S(("mp_c", "mp_c2")[r]), n0 + i)
                        for q in range(2):
                            for m in range(2):
                                o = P * (2 * q + m)
                                last = tr(bank(4 + r, o, o + P), mpr[:, i % 2, 2 * r + q, P * m:P * m + P], ident)
                        last.then_inc(S("mp_t"), 1)

                def values(i):
                    pe.wait_ge(S("mp_c"), n0 + i + 1)
                    pe.wait_ge(S("mp_c2"), n0 + i + 1)
                    if n0 + i:
                        pe.wait_ge(S("mp_ev"), n0 + i)
                    for h in range(MH):
                        q = 2 * (h % 2) + h // 2
                        o = bank(6, P * (h // 2), P * (h // 2) + P, rows=(64 * (h % 2), 64 * (h % 2) + 64))
                        for m in range(2):
                            last = mm(o, memkv[:, l, m, MW + MD * h:MW + MD * h + MD], mprT[:, 2 * q + m, :],
                                      start=(m == 0), stop=(m == 1))
                    last.then_inc(S("mp_o"), 1)

                for s in range(ST + 2):
                    if s < ST:
                        logits(s)
                    if 1 <= s <= ST:
                        turn(s - 1)
                    if s >= 2:
                        values(s - 2)

            def mem_sample_attention(l):
                n0 = DB * l

                def turn(b):
                    if n0 + b >= 2:
                        pe.wait_ge(S("mk_cp"), n0 + b - 1)
                    for a in range(2):
                        for m in range(2):
                            o = P * (2 * a + m)
                            last = tr(bank(2 + b % 2, o, o + P), mkc[:, b, m, P * a:P * a + P], ident)
                    last.then_inc(S("mk_tr"), 1)

                pe.wait_ge(S("mk_in"), 16 * DB * (l + 1))
                pe.wait_ge(S("qmb"), l + 1)
                turn(0)
                for b in range(DB):
                    if b + 1 < DB:
                        turn(b + 1)
                    pe.wait_ge(S("mk_cp"), n0 + b + 1)
                    rr = (32 * (b % 4), 32 * (b % 4) + 32)
                    for a in range(2):
                        last = mm(bank(b // 4, 0, ML, rows=rr), qmb[:, a, 16 * b:16 * b + 32], mkcT[:, b % 2, a, :],
                                  start=(a == 0), stop=(a == 1), skip_group_check=True)
                    last.then_inc(S("ms_l"), 1)
                pe.wait_ge(S("ms_e"), l + 1)
                for g in range(2):
                    for m in range(2):
                        o = P * (2 * g + m)
                        last = tr(bank(2, o, o + P), mexp[:, g, P * m:P * m + P], ident)
                last.then_inc(S("ms_t"), 1)
                pe.wait_ge(S("ms_c"), l + 1)
                pe.wait_ge(S("mv_in"), 16 * DB * (l + 1))
                for b in range(DB):
                    g = b // 4
                    rr = (32 * (b % 4), 32 * (b % 4) + 32)
                    for m in range(2):
                        last = mm(bank(3, MW * g, MW * g + MW, rows=rr), mp_s[:, 2 * g + m, rr[0]:rr[1]],
                                  mvc[:, b, MW * m:MW * m + MW], start=(m == 0), stop=(m == 1),
                                  skip_group_check=True)
                last.then_inc(S("ms_o"), 1)

            def mem_sample_columns(l):
                pe.wait_ge(S("ms_n"), l + 1)
                for g in range(2):
                    last = tr(bank(2, P * g, P * g + P), mres[:, g].rearrange("p r d -> p (r d)"), ident)
                last.then_inc(S("ms_r"), 1)

            def router_tile(l, i):
                n, j = ROWS[i], NT * l + i
                pe.wait_ge(S("xt_cp"), 10 * (2 * l + 1) + 2 * i + 2)
                if j >= 2:
                    pe.wait_ge(S("rt_ev"), j - 1)
                for k in range(KD):
                    last = mm(bank(2 + j % 2, 0, NG + NE, rows=(0, n)), XT[:, k, P * i:P * i + n], wr[:, k, :],
                              start=(k == 0), stop=(k == KD - 1))
                last.then_inc(S("rt_mm"), 1)

            def project_tile(l, i):
                n = ROWS[i]
                pe.wait_ge(S("mix_lo"), NT * l + i + 1)
                for half in range(2):
                    j = 10 * l + 2 * i + half
                    if j >= 4:
                        pe.wait_ge(S("wo_ev"), j - 3)
                    c = slice(512 * half, 512 * half + 512)
                    for k in range(KD):
                        last = split_product(bank(4 + j % 4, rows=(0, n)), mix_r[i % 2][:, k, 0:n],
                                             MX_lo[:, k, P * i:P * i + n], wo_r[:, k, c], wo_lo[:, k, c], k)
                    last.then_inc(S("wo_mm"), 1)

            def project_and_route(l):
                pe.wait_ge(S("wo_lo"), KD * (l + 1))
                pe.wait_ge(S("mp_ev"), ST * (l + 1))
                project_tile(l, 0)
                mem_sample_columns(l)
                pe.wait_ge(S("route_in"), 16 * 7 * (l + 1))
                for i in range(NT + 1):
                    if 1 <= i < NT:
                        project_tile(l, i)
                    if i:
                        cols_of(2 * l + 1, i - 1)
                        router_tile(l, i - 1)
                pe.wait_ge(S("onehot"), l + 1)
                pe.wait_ge(S("wo_ev"), 10 * (l + 1))
                mm(bank(4, 0, NE * (NT + 1)), C("strict"), cnt.rearrange("p i e -> p (i e)"), start=True, stop=False)
                for q in range(1, NT + 1):
                    last = mm(bank(4, NE * q, NE * (NT + 1)), C("ones"),
                              cnt[:, 0:NT + 1 - q, :].rearrange("p i e -> p (i e)"), start=False, stop=(q == NT))
                last.then_inc(S("rank_mm"), 1)
                pe.wait_ge(S("places"), l + 1)
                for n in range(10):
                    last = mm(bank(5, 0, 64), a1[:, n, :], bb[:, n, :], start=(n == 0), stop=(n == 9))
                last.then_inc(S("slot_mm"), 1)

            def turn_rows():
                for half in range(2):
                    for k in range(4):
                        kk = 4 * half + k
                        last = tr(bank(2 + half, P * k, P * k + P), xg[:, kk * P:kk * P + P], ident)
                return last

            def experts(l):
                s = l * PAIRS
                g = l * (PAIRS + 1)
                if l == 0:
                    pe.sem_inc(S("xg_free"), 1)
                pe.wait_ge(S("slots"), l + 1)
                pe.wait_ge(S("xg_in"), 16 * (g + 1))
                turn_rows().then_inc(S("xg_free"), 1)
                with pe.Fori(0, PAIRS // 2) as r:
                    for q in range(2):
                        pe.wait_ge(S("xgt"), r * 2 + (g + q + 1))
                        for j in range(2):
                            b = 2 * q + j
                            pe.wait_ge(S(f"exp_in{b}"), r * 32 + (16 * s + 32))
                            for f in range(4):
                                for k in range(KD):
                                    last = mm(bank(j, SLOTS * f, SLOTS * f + SLOTS), WU[b][:, k, P * f:P * f + P],
                                              xgT[:, k, SLOTS * j:SLOTS * j + SLOTS], start=(k == 0),
                                              stop=(k == KD - 1))
                            last.then_inc(S("up_done"), 1)
                        pe.wait_ge(S("xg_in"), r * 32 + (16 * (g + q) + 32))
                        turn_rows().then_inc(S("xg_free"), 1)
                        pe.wait_ge(S("y_ev"), r * 2 + (s + q + 1))
                        for j in range(2):
                            b = 2 * q + j
                            pe.wait_ge(S("hid"), r * 4 + (2 * (s + q) + j + 1))
                            for half in range(2):
                                for f in range(2):
                                    last = mm(bank(4 + half, rows=(SLOTS * j, SLOTS * j + SLOTS)), hid[:, j, f, :],
                                              WD[b][:, f, 512 * half:512 * half + 512], start=(f == 0),
                                              stop=(f == 1))
                            last.then_inc(S("down_done"), 1)
                more = pe.value_load(lists[0:1, 16:17], min_val=0, max_val=MORE)
                pe.wait_ge(S("xgt"), g + PAIRS + 1)
                pe.wait_ge(S("y_ev"), s + PAIRS + 1)
                pe.sem_inc(S(f"more_step{l}"), 1)
                with pe.If(more > 0):
                    with pe.Fori(0, more) as x:
                        pe.wait_ge(S(f"more_step{l}"), x * 9 + 2)
                        pe.wait_ge(S(f"more_x{l}"), x * 16 + 16)
                        turn_rows().then_inc(S(f"more_step{l}"), 1)
                        pe.wait_ge(S(f"more_step{l}"), x * 9 + 4)
                        pe.wait_ge(S(f"more_w{l}"), x * 32 + 32)
                        for f in range(4):
                            for k in range(KD):
                                last = mm(bank(0, P * f, P * f + P), WU[0][:, k, P * f:P * f + P], xgT[:, k, :],
                                          start=(k == 0), stop=(k == KD - 1))
                        last.then_inc(S(f"more_step{l}"), 1)
                        pe.wait_ge(S(f"more_step{l}"), x * 9 + 7)
                        for half in range(2):
                            for f in range(2):
                                last = mm(bank(4 + half), hidx[:, f, :], WD[0][:, f, 512 * half:512 * half + 512],
                                          start=(f == 0), stop=(f == 1))
                        last.then_inc(S(f"more_step{l}"), 1)

            pe.wait_ge(S("mem_in"), 32)
            for m in range(2):
                for half in range(2):
                    j = 2 * m + half
                    if j >= 2:
                        pe.wait_ge(S("mt_cp"), j - 1)
                    for k in range(4):
                        kk = 4 * half + k
                        last = tr(bank(2 + j % 2, P * k, P * k + P), mem_rows[:, m, kk * P:kk * P + P], ident)
                    last.then_inc(S("mt_mm"), 1)
            pe.wait_ge(S("mt_cp"), 4)
            for l in range(LAYERS):
                for kv in range(2):
                    n = 2 * l + kv
                    pe.wait_ge(S(f"mkv_w{n % 3}"), 16 * (n // 3 + 1))
                    for m in range(2):
                        j = 4 * l + 2 * kv + m
                        if j >= 4:
                            pe.wait_ge(S("mkv_ev"), j - 3)
                        for k in range(KD):
                            last = mm(bank(4 + j % 4, 0, 256), memT[:, k, P * m:P * m + P],
                                      mem_chunk_view(n)[:, k, :], start=(k == 0), stop=(k == KD - 1))
                        last.then_inc(S("mkv_mm"), 1)
                pe.wait_ge(S("mkv_ev"), 4 * l + 2)
                for hp in range(2):
                    for m in range(2):
                        o = P * (2 * hp + m)
                        last = tr(bank(2 + l, o, o + P), memkv[:, l, m, P * hp:P * hp + P], ident)
                last.then_inc(S("mkt_mm"), 1)
                if l == 0:
                    pe.wait_ge(S("x_in"), 32)
                    for i in range(NT):
                        cols_of(0, i)
            pe.wait_ge(S("xt_cp"), 10)
            for h in range(2 * RH):
                m = CH_A + h // 3
                if h % 3 == 0:
                    chunk_split(pe, m)
                if h >= 2:
                    pe.wait_ge(S("rope_ev"), h - 1)
                elif h == 1:
                    pe.wait_ge(S("mkt_ev"), 2)
                feature_major(h, m, P * (h % 3)).then_inc(S("rope_mm"), 1)
            pe.wait_ge(S("mkv_ev"), 8)
            for j in range(20):
                m = CH_A + 4 + j // 5
                if j % 5 == 0:
                    chunk_split(pe, m)
                if j >= 4:
                    pe.wait_ge(S("tm_ev"), j - 3)
                token_major(j, m, j % 5).then_inc(S("tm_mm"), 1)
            pe.wait_ge(S("rope_ev"), 12)
            chunk_split(pe, CH_A + 8)
            for n in range(2):
                feature_major(n, CH_A + 8, P * n).then_inc(S("fm_mm"), 1)

            def front(n):
                for j in range(2):
                    if n:
                        pe.wait_ge(S("rsm"), 2 * (n - 1) + j + 1)
                    for h in range(3 * j, 3 * j + 3):
                        o = P * (h % 3)
                        last = mm(bank(j, o, o + P), kT[:, h, P * n:P * n + P], qT[:, h, P * n:P * n + P],
                                  start=True, stop=True)
                    last.then_inc(S("rsc"), 1)
                for j in range(2):
                    if n:
                        pe.wait_ge(S("rkd"), 2 * (n - 1) + j + 1)
                    for h in range(3 * j, 3 * j + 3):
                        o = P * (h % 3)
                        last = tr(bank(2 + j, o, o + P), kT[:, h, P * n:P * n + P], ident)
                    last.then_inc(S("rkt"), 1)

            def back(n):
                for j in range(2):
                    u = 2 * n + j
                    pe.wait_ge(S("rsm"), u + 1)
                    if n:
                        pe.wait_ge(S("rcp"), u - 1)
                        pe.wait_ge(S("rst"), u - 1)
                    for h in range(3 * j, 3 * j + 3):
                        o = bank(4 + j, P * (h % 3), P * (h % 3) + P)
                        last = mm(o, scm[n % 2][:, h, :], V[:, n, P * h:P * h + P], start=True, stop=(n == 0))
                        if n:
                            last = mm(o, qd[n % 2][:, h, :], state_p[:, h, :], start=False, stop=True)
                    last.then_inc(S("rr"), 1)
                    pe.wait_ge(S("rkd"), u + 1)
                    for h in range(3 * j, 3 * j + 3):
                        o = P * (h % 3)
                        last = mm(bank(6 + j, o, o + P), kd[n % 2][:, h, :], V[:, n, P * h:P * h + P], start=True,
                                  stop=True)
                    last.then_inc(S("rkv"), 1)

            pe.wait_ge(S("fm_ev"), 2)
            front(0)
            pe.wait_ge(S("tm_ev"), 20)
            for n in range(1, ST):
                front(n)
                back(n - 1)

            def sample_front(h):
                if h >= 2:
                    pe.wait_ge(S("rsm"), 2 * ST + h - 1)
                    pe.wait_ge(S("rkd"), 2 * ST + h - 1)
                mm(bank(h % 2, 0, NS, rows=(0, NS)), kT[:, h, SEQ:TOK], qT[:, h, SEQ:TOK], start=True,
                   stop=True).then_inc(S("rsc"), 1)
                tr(bank(2 + h % 2, 0, P, rows=(0, NS)), kT[:, h, SEQ:TOK], ident).then_inc(S("rkt"), 1)

            def sample_back(h):
                b = h % 2
                pe.wait_ge(S("rsm"), 2 * ST + h + 1)
                if h >= 2:
                    pe.wait_ge(S("rcp"), 2 * ST + h - 1)
                o = bank(4 + b, 0, P, rows=(0, NS))
                mm(o, scs[0:NS, b, :], V[0:NS, ST, P * h:P * h + P], start=True, stop=False)
                pe.wait_ge(S(f"st_in{h % 3}"), 16 * (h // 3 + 1))
                for q in range(DB):
                    last = mm(o, qbs[:, b, q, :], st_s[:, h % 3, P * q:P * q + P], start=False, stop=(q == DB - 1))
                last.then_inc(S("rr"), 1)
                pe.wait_ge(S("rkd"), 2 * ST + h + 1)
                pe.wait_ge(S("rst"), 2 * ST + h)
                for q in range(2):
                    last = mm(bank(6 + q), kds[0:NS, b, :], vbd[b][0:NS, 512 * q:512 * q + 512], start=True,
                              stop=True)
                last.then_inc(S("rkv"), 1)

            pe.wait_ge(S("rsm"), 2 * ST)
            pe.wait_ge(S("rkd"), 2 * ST)
            sample_front(0)
            sample_front(1)
            back(ST - 1)
            pe.wait_ge(S("rcp"), 2 * ST)
            for h in range(RH):
                if 2 <= h + 1 < RH:
                    sample_front(h + 1)
                sample_back(h)
            pe.wait_ge(S("rsm"), 2 * ST + RH)
            pe.wait_ge(S("rkd"), 2 * ST + RH)
            for i in range(NT):
                n = ROWS[i]
                pe.wait_ge(S("gated"), i + 1)
                if i >= 2:
                    pe.wait_ge(S("tk_cp"), i - 1)
                for h in range(RH):
                    o = 1024 * (i % 2) + n * h
                    last = tr(ps[:, o:o + n], R[0:n, i, P * h:P * h + P], ident[0:n, 0:n])
                last.then_inc(S("tk_mm"), 1)
            pe.wait_ge(S("tk_cp"), NT)
            pe.wait_ge(S("rst"), 2 * ST + RH)
            pe.wait_ge(S("rcp"), 2 * ST + RH)
            pe.sem_inc(S("tok_done"), 1)
            mem_prompt_attention(0)
            mem_sample_attention(0)
            project_and_route(0)
            experts(0)

            for j in range(20, 45):
                m = CH_S + (j - 20) // 5
                if j % 5 == 0:
                    chunk_split(pe, m)
                if j == 20:
                    cols_of(2, 0)
                if j < 24:
                    cols_of(2, j - 19)
                if j < 25:
                    pe.wait_ge(S("xt_cp"), 20 + 2 * (j - 20) + 2)
                if j >= 24:
                    pe.wait_ge(S("tm_ev"), j - 3)
                token_major(j, m, j % 5).then_inc(S("tm_mm"), 1)
            for i in range(NT):
                n = ROWS[i]
                pe.wait_ge(S("tm_ev"), 30)
                if i >= 2:
                    pe.wait_ge(S("tk_cp"), NT + i - 1)
                for h in range(6):
                    o = 1024 * (i % 2) + n * h
                    last = tr(ps[:, o:o + n], k_rows[0:n, i, P * h:P * h + P], ident[0:n, 0:n])
                last.then_inc(S("tk_mm"), 1)
            pe.wait_ge(S("tk_cp"), NT + NT)
            for n in range(2, 10):
                m = CH_B + (n - 2) // 3
                if (n - 2) % 3 == 0:
                    chunk_split(pe, m)
                if n >= 4:
                    pe.wait_ge(S("fm_ev"), n - 1)
                feature_major(n, m, P * ((n - 2) % 3)).then_inc(S("fm_mm"), 1)
            pe.wait_ge(S("logf"), 1)
            pe.wait_ge(S("tm_ev"), 45)
            pe.wait_ge(S("pf_in"), 16 * DB * PG)
            for i in range(ST):
                for q in range(i + 1):
                    mm(bank(4, FH * i, FH * i + FH), C("tri") if q == i else C("ones"), logf[:, q, :],
                       start=(q == 0), stop=(q == i))
            o = bank(4, FH * ST, FH * NT, rows=(0, NS))
            mm(o, C("tri_s", NS), logf[0:NS, ST, :], start=True, stop=False)
            for b in range(DB):
                for g in range(PG):
                    last = mm(o, C("batch_s")[:, 28 - DS * b:60 - DS * b], past_f[:, g, FH * b:FH * b + FH],
                              start=False, stop=(b == DB - 1 and g == PG - 1))
            mm(bank(5, 0, DB * FH), C("tri"), past_f[:, 0, :], start=True, stop=True)
            mm(bank(5, DB * FH, 2 * DB * FH), C("ones"), past_f[:, 0, :], start=True, stop=False)
            mm(bank(5, DB * FH, 2 * DB * FH), C("tri"), past_f[:, 1, :], start=False, stop=True) \
                .then_inc(S("cum"), 1)
            pe.wait_ge(S("cum_ev"), 1)
            pe.wait_ge(S("fm_ev"), 10)

            def minus_c(h):
                if h:
                    pe.wait_ge(S("fnb_cp"), h)
                for q in range(ST):
                    last = mm(bank(3, P * q, P * q + P), negc[:, q, h:h + 1].broadcast_to([P, P]), ident,
                              start=True, stop=True)
                last.then_inc(S("fnb"), 1)

            def fox_logits(h):
                f = slice(64 * (h % 2), 64 * (h % 2) + 64)
                for n, tiles in enumerate(((1,), (0, 2), (3,))):
                    if h:
                        pe.wait_ge(S("fp_s"), 3 * h - 2 + n)
                    for i in tiles:
                        b, o = LOGIT_AT[i]
                        last = mm(bank(b, o, o + P * (i + 1)), qT[f, h // 2, P * i:P * i + P],
                                  kT[f, h // 2, 0:P * (i + 1)], start=True, stop=True)
                    last.then_inc(S("fp_l"), 1)

            def fox_turn(h):
                for n, tiles in enumerate(((3,), (2, 0), (1,))):
                    pe.wait_ge(S("fp_e"), 4 * h + (1, 3, 4)[n])
                    if h:
                        pe.wait_ge(S("fp_c"), 3 * h - 2 + n)
                    for i in tiles:
                        for q in range(i + 1):
                            o = 4 * SEQ + PT_AT[i] + P * q
                            last = tr(ps[:, o:o + P], fpr[h % 2][:, i, P * q:P * q + P], ident)
                    last.then_inc(S("fp_t"), 1)

            def fox_values(h):
                pe.wait_ge(S("fp_c"), 3 * h + 3)
                if h:
                    pe.wait_ge(S("fp_ev"), h)
                for i in range(ST):
                    for q in range(i + 1):
                        o = PT_AT[i] + P * q
                        last = mm(bank(7, FD * i, FD * i + FD), fprT[:, h % 2, o:o + P],
                                  V[:, q, FD * h:FD * h + FD], start=(q == 0), stop=(q == i))
                last.then_inc(S("fox_p"), 1)

            minus_c(0)
            for s in range(FH + 2):
                if s < FH:
                    fox_logits(s)
                if 1 <= s <= FH:
                    fox_turn(s - 1)
                if s >= 2:
                    fox_values(s - 2)
                if s + 1 < FH:
                    minus_c(s + 1)
            pe.wait_ge(S("fp_ev"), FH)
            def turn_page(n):
                if n >= 2:
                    pe.wait_ge(S("fk_cp"), n - 1)
                    pe.wait_ge(S("fk_cp2"), n - 1)
                for h in range(6):
                    o = 2048 + 1024 * (n % 2) + P * h
                    last = tr(ps[:, o:o + P], fkc[n][:, P * h:P * h + P], ident)
                last.then_inc(S("fk_tr"), 1)

            pe.wait_ge(S("fk_in"), 16 * DB * PG)
            pe.wait_ge(S("qbd"), FH + 4)
            turn_page(0)
            for n in range(DB * PG):
                b, g = n // PG, n % PG
                r0 = 64 * (b % 2)
                if n + 1 < DB * PG:
                    turn_page(n + 1)
                if g == 0:
                    mm(bank(b // 2, 0, FLW, rows=(r0, r0 + 64)), cq_rows[0:NS, b, :],
                       C("ones", NS)[:, 0:1].broadcast_to([NS, FLW]), start=True, stop=False, skip_group_check=True)
                    o = bank(b // 2, PG * PAGE, FLW, rows=(r0, r0 + QR))
                    for h in range(6):
                        mm(o, qbd[:, h, b, :], kT[:, h, SEQ:TOK], start=False, stop=False, skip_group_check=True)
                    mm(o, negc_rows[0:NS], ident[0:NS, 0:NS], start=False, stop=False, skip_group_check=True)
                    mm(o, own_row[0:NS, b, :], C("causal_s", NS), start=False, stop=True, skip_group_check=True)
                pe.wait_ge(S("fk_cp"), n + 1)
                pe.wait_ge(S("fk_cp2"), n + 1)
                o = bank(b // 2, PAGE * g, PAGE * g + PAGE, rows=(r0, r0 + QR))
                for h in range(6):
                    last = mm(o, qbd[:, h, b, :], fkT[n % 2][:, h, :], start=False, stop=False,
                              skip_group_check=True)
                mm(o, negp_rows[:, g, b, :], ident, start=False, stop=True,
                   skip_group_check=True).then_inc(S("fs_l"), 1)
            for i in range(ST):
                if i >= 2:
                    pe.wait_ge(S("tk_cp"), 2 * NT + i - 1)
                else:
                    pe.wait_ge(S("fk_cp"), DB * PG)
                    pe.wait_ge(S("fk_cp2"), DB * PG)
                for h in range(6):
                    o = 2048 + 1024 * (i % 2) + P * h
                    last = tr(ps[:, o:o + P], o_rows[:, i, P * h:P * h + P], ident)
                last.then_inc(S("tk_mm"), 1)
            pe.wait_ge(S("tk_cp"), 2 * NT + ST)
            pe.wait_ge(S("fs_e"), 1)
            for q in range(GR):
                for g in range(PG):
                    tr(bank(4 + q, PAGE * g, PAGE * g + PAGE), fl_r[:, q, PAGE * g:PAGE * g + PAGE], ident)
                tr(bank(4 + q, PG * PAGE, PG * PAGE + P, rows=(0, NS)), fl_r[:, q, PG * PAGE:], ident) \
                    .then_inc(S("fs_t"), 1)
            pe.wait_ge(S("fv_in"), 16 * DB * PG)
            for q in range(GR):
                pe.wait_ge(S(("fs_c", "fs_c2")[q % 2]), q // 2 + 1)
                if q >= 2:
                    pe.wait_ge(S("fs_h"), q - 1)
                for c0, c1, bk in ((0, 512, 2 * (q % 2)), (512, FW, 2 * (q % 2) + 1)):
                    mm(bank(bk, 0, c1 - c0), fs_p[0:NS, q, PG, :], V[0:NS, ST, c0:c1], start=True, stop=False,
                       skip_group_check=True)
                    for b in (2 * q, 2 * q + 1):
                        r0 = 64 * (b % 2)
                        for g in range(PG):
                            last = mm(bank(bk, 0, c1 - c0, rows=(r0, r0 + QR)), fs_p[:, q, g, r0:r0 + QR],
                                      fvc[PG * b + g][:, c0:c1], start=False, stop=(g == PG - 1),
                                      skip_group_check=True)
                last.then_inc(S("fs_pv"), 1)
            for q in range(GR):
                pe.wait_ge(S("fs_n"), q + 1)
                last = tr(bank(4, P * q, P * q + P), fres[:, q].rearrange("p r d -> p (r d)"), ident)
            last.then_inc(S("fs_o"), 1)
            pe.wait_ge(S("fs_ev"), 1)
            pe.sem_inc(S("tok_done"), 1)
            mem_prompt_attention(1)
            mem_sample_attention(1)
            project_and_route(1)
            experts(1)

        @block.scalar
        def _(act):
            af = nc.scalar.activation

            def copy_cols(p, i):
                n = ROWS[i]
                for half in range(2):
                    j = 2 * i + half
                    act.wait_ge(S("xt_mm"), 10 * p + j + 1)
                    af(XT[:, 4 * half:4 * half + 4, P * i:P * i + n],
                       bank(j % 2, 0, 4 * n).rearrange("p (k n) -> p k n", k=4), ACT.Copy).then_inc(S("xt_cp"), 1)

            def deviation(p, i):
                act.wait_ge(S("ln_st"), NT * p + i + 1)
                af(rstd[:, i:i + 1], mv[:, i, 1:2], ACT.Sqrt, bias=eps_ln[:, 0:1]).then_inc(S("ln_sd"), 1)

            def cols_rounded(p, i):
                n = ROWS[i]
                for half in range(2):
                    j = 2 * i + half
                    act.wait_ge(S("xt_mm"), 10 * p + j + 1)
                    af(XT_r[:, 4 * half:4 * half + 4, P * i:P * i + n],
                       bank(j % 2, 0, 4 * n).rearrange("p (k n) -> p k n", k=4), ACT.Copy).then_inc(S("xt_r"), 1)

            def round_chunk(m):
                act.wait_ge(S(f"w_in{m % 2}"), 16 * (m // 2 + 1))
                before = {1: ("mt_mm", 4), 5: ("rope_ev", 12), CH_S: ("fm_mm", 2), 12: ("yg_used", NT)}.get(m)
                if before:
                    act.wait_ge(S(before[0]), before[1])
                if m >= 2 and m != CH_S:
                    act.wait_ge(S(chunks[m - 2][1][0]), chunks[m - 2][1][1])
                for half in range(2):
                    k = slice(4 * half, 4 * half + 4)
                    af(w_r(m)[:, k, :], w_raw(m)[:, k, :], ACT.Copy).then_inc(S("w_r"), 1)

            def output_weights_ready(l):
                act.wait_ge(S("wo_in"), 32 * (l + 1))
                act.wait_ge(S("tok_done"), l + 1)
                act.wait_ge(S("rs_out"), 16)
                if l:
                    act.wait_ge(S("kv_out"), 64)

            def round_weights(k0, k1):
                for k in range(k0, k1):
                    af(wo_r[:, k, :], wo_v[:, k, :], ACT.Copy).then_inc(S("wo_r"), 1)

            def mix_rounded(l, i):
                if i >= 2:
                    act.wait_ge(S("wo_mm"), 10 * l + 2 * (i - 1))
                af(mix_r[i % 2][:, :, 0:ROWS[i]], MX[:, :, P * i:P * i + ROWS[i]], ACT.Copy) \
                    .then_inc(S("mix_r"), 1)

            def norm_and_columns(p, columns=True):
                if columns:
                    act.wait_ge(S("ms_ev"), p // 2 + 1)
                for i in range(NT + 1):
                    if i < NT:
                        if columns and i + 2 < NT:
                            mix_rounded(p // 2, i + 2)
                        deviation(p, i)
                    if i and columns:
                        copy_cols(p + 1, i - 1)

            def mem_prompt(l):
                n0 = ST * l
                for s in range(ST + 2):
                    if s < ST:
                        act.wait_ge(S("mp_m"), n0 + s + 1)
                        if n0 + s >= 2:
                            act.wait_ge(S("mp_t"), 2 * (n0 + s - 1))
                        for q in range(MH):
                            last = af(mpr[:, s % 2, q, :], bank(2 * (s % 2) + q // 2, ML * (q % 2), ML * (q % 2) + ML),
                                      ACT.Exp, bias=nmx2[:, s % 2, q:q + 1], accum_out=esum2[:, s % 2, q:q + 1])
                        last.then_inc(S("mp_e"), 1)
                    if 1 <= s <= ST:
                        i = s - 1
                        act.wait_ge(S("mp_t"), 2 * (n0 + i) + 1)
                        if n0 + i:
                            act.wait_ge(S("mp_o"), n0 + i)
                        af(mprT[:, 0:4, :], bank(4).rearrange("p (n t) -> p n t", n=4), ACT.Copy) \
                            .then_inc(S("mp_c"), 1)
                    if s >= 2:
                        i = s - 2
                        act.wait_ge(S("mp_o"), n0 + i + 1)
                        af(MX[:, 6:8, P * i:P * i + P], bank(6, 0, 2 * P).rearrange("p (a t) -> p a t", a=2),
                           ACT.Copy).then_inc(S("mp_ev"), 1)
                    if s == 3:
                        output_weights_ready(l)
                    if s >= 3:
                        round_weights(*((0, 2), (2, 5), (5, 8))[s - 3])

            def mem_sample(l):
                for b in range(DB):
                    n = DB * l + b
                    act.wait_ge(S("mk_tr"), n + 1)
                    if n >= 2:
                        act.wait_ge(S("ms_l"), n - 1)
                    af(mkcT[:, b % 2], bank(2 + b % 2).rearrange("p (a t) -> p a t", a=2), ACT.Copy) \
                        .then_inc(S("mk_cp"), 1)
                act.wait_ge(S("ms_m"), l + 1)
                for g in range(2):
                    last = af(mexp[:, g, :], bank(g, 0, ML), ACT.Exp, bias=nmx[:, g:g + 1],
                              accum_out=esum[:, g:g + 1])
                last.then_inc(S("ms_e"), 1)
                act.wait_ge(S("ms_t"), l + 1)
                af(mp_s, bank(2).rearrange("p (n t) -> p n t", n=4), ACT.Copy).then_inc(S("ms_c"), 1)
                act.wait_ge(S("mp_ev"), ST * (l + 1))
                mix_rounded(l, 0)
                mix_rounded(l, 1)
                act.wait_ge(S("ms_r"), l + 1)
                for g in range(2):
                    for r in range(2):
                        rr = (64 * r, 64 * r + 64)
                        src = bank(2, P * g, P * g + P, rows=rr).rearrange("p (b a c) -> p a b c", b=4, a=4)
                        src = src[:, 0:2, :, DS * r:DS * r + DS]
                        last = af(MX[rr[0]:rr[1], 6:8, SEQ + 16 * g:SEQ + 16 * g + 16]
                                  .rearrange("p a (b t) -> p a b t", t=DS), src, ACT.Copy)
                last.then_inc(S("ms_ev"), 1)

            def routing(l):
                act.wait_ge(S("r_step"), 4 * l + 1)
                af(gexp, gexp, ACT.Exp).then_inc(S("r_step"), 1)
                act.wait_ge(S("r_step"), 4 * l + 3)
                af(tmpw, tmpw, ACT.Exp).then_inc(S("r_step"), 1)

            def turn_copy(sem):
                for half in range(2):
                    last = af(xgT[:, 4 * half:4 * half + 4, :],
                              bank(2 + half).rearrange("p (k n) -> p k n", k=4), ACT.Copy)
                last.then_inc(sem, 1)

            def experts(l):
                s, g = l * PAIRS, l * (PAIRS + 1)
                if l == 0:
                    act.sem_inc(S("y_ev"), 1)
                    act.sem_inc(S("y_out"), 16)
                act.wait_ge(S("xg_free"), g + 2)
                turn_copy(S("xgt"))
                with act.Fori(0, PAIRS) as i:
                    for j in range(2):
                        act.wait_ge(S("up_done"), i * 2 + (2 * s + j + 1))
                        af(sg[:, j, :], bank(j, 0, 2 * SLOTS), ACT.Silu).then_inc(S("gate"), 1)
                    act.wait_ge(S("xg_free"), i + (g + 3))
                    turn_copy(S("xgt"))
                    act.wait_ge(S("y_out"), i * 16 + (16 * s + 16))
                    act.wait_ge(S("down_done"), i * 2 + (2 * s + 2))
                    for half in range(2):
                        last = af(yb[:, 512 * half:512 * half + 512], bank(4 + half), ACT.Copy,
                                  scale=wslot[:, bass.ds(i, 1)])
                    last.then_inc(S("y_ev"), 1)
                    act.wait_ge(S("y_ev"), i + (s + 2))
                    act.dma_start(ys[l].rearrange("(b p) d -> p b d", p=P)[:, bass.ds(i, 1)]
                                  .rearrange("p a d -> p (a d)"), yb).then_inc(S("y_out"), 16)
                act.wait_ge(S("y_out"), 16 * (s + PAIRS) + 16)
                more = act.value_load(lists[0:1, 16:17], min_val=0, max_val=MORE)
                with act.If(more > 0):
                    with act.Fori(0, more) as x:
                        act.wait_ge(S(f"more_step{l}"), x * 9 + 3)
                        turn_copy(S(f"more_step{l}"))
                        act.wait_ge(S(f"more_step{l}"), x * 9 + 5)
                        af(sgx, bank(0, 0, 2 * P).rearrange("p (f n) -> p f n", f=2), ACT.Silu) \
                            .then_inc(S(f"more_step{l}"), 1)
                        act.wait_ge(S(f"more_step{l}"), x * 9 + 8)
                        for half in range(2):
                            last = af(yb[:, 512 * half:512 * half + 512], bank(4 + half), ACT.Copy,
                                      scale=wslot[:, bass.ds(x + PAIRS, 1)])
                        last.then_inc(S(f"more_step{l}"), 1)

            for j in range(4):
                act.wait_ge(S("mt_mm"), j + 1)
                af(memT[:, 4 * (j % 2):4 * (j % 2) + 4, P * (j // 2):P * (j // 2) + P],
                   bank(2 + j % 2).rearrange("p (k n) -> p k n", k=4), ACT.Copy).then_inc(S("mt_cp"), 1)
            for l in range(LAYERS):
                for j in range(4):
                    act.wait_ge(S("mkv_mm"), 4 * l + j + 1)
                    af(memkv[:, l, j % 2, MW * (j // 2):MW * (j // 2) + MW], bank(4 + j, 0, 256), ACT.Copy) \
                        .then_inc(S("mkv_ev"), 1)
                act.wait_ge(S("mkt_mm"), l + 1)
                af(memkt[:, l], bank(2 + l).rearrange("p (a t) -> p a t", a=2), ACT.Copy).then_inc(S("mkt_ev"), 1)
                if l == 0:
                    for i in range(NT):
                        cols_rounded(0, i)
                round_chunk(l)
            for m in range(2, 5):
                round_chunk(m)
            for j in range(20):
                n, i = ROWS[j % 5], j % 5
                act.wait_ge(S("tm_mm"), j + 1)
                c = 384 * ((j // 5) % 2)
                if j < 10:
                    af(V[0:n, i, c:c + 384], bank(4 + j % 4, 0, 384, rows=(0, n)), ACT.Copy).then_inc(S("tm_ev"), 1)
                else:
                    af(G[0:n, i, c:c + 384], bank(4 + j % 4, 0, 384, rows=(0, n)), ACT.Silu).then_inc(S("tm_ev"), 1)
                if j % 5 == 1:
                    round_chunk(5 + j // 5)

            def queries(n, dst, scale):
                act.wait_ge(S("fm_mm"), n + 1)
                o = 1024 * (n % 2) + FM0
                af(dst, ps[:, o:o + TOK], ACT.Copy, scale=scale).then_inc(S("fm_ev"), 1)

            act.wait_ge(S("fm_mm"), 2)
            for n in range(2):
                queries(n, mqT[:, n, :], MD ** -0.5)

            def decayed_keys(n):
                for j in range(2):
                    act.wait_ge(S("rkt"), 2 * n + j + 1)
                    if n >= 2:
                        act.wait_ge(S("rkv"), 2 * (n - 2) + j + 1)
                    for h in range(3 * j, 3 * j + 3):
                        o = P * (h % 3)
                        last = af(kd[n % 2][:, h, :], bank(2 + j, o, o + P), ACT.Copy, scale=C("kdecay")[:, h:h + 1])
                    last.then_inc(S("rkd"), 1)

            act.wait_ge(S("rope_ev"), 12)
            decayed_keys(0)
            for n in range(ST):
                if n + 1 < ST:
                    decayed_keys(n + 1)
                for j in range(2):
                    act.wait_ge(S("rr"), 2 * n + j + 1)
                    af(R[:, n, 384 * j:384 * j + 384], bank(4 + j, 0, 384), ACT.Copy).then_inc(S("rcp"), 1)

            def sample_keys(h):
                act.wait_ge(S("rkt"), 2 * ST + h + 1)
                if h >= 2:
                    act.wait_ge(S("rkv"), 2 * ST + h - 1)
                af(kds[0:NS, h % 2, :], bank(2 + h % 2, 0, P, rows=(0, NS)), ACT.Copy).then_inc(S("rkd"), 1)

            sample_keys(0)
            for h in range(RH):
                if h + 1 < RH:
                    sample_keys(h + 1)
                act.wait_ge(S("rr"), 2 * ST + h + 1)
                af(R[0:NS, ST, P * h:P * h + P], bank(4 + h % 2, 0, P, rows=(0, NS)), ACT.Copy) \
                    .then_inc(S("rcp"), 1)
            act.wait_ge(S("head_sd"), 1)
            af(hrs, hmv[:, :, 1], ACT.Sqrt, bias=eps_hn[:, 0:1]).then_inc(S("head_sd"), 1)
            for k in range(3):
                act.wait_ge(S(f"st_out{k}"), 32)
            for i in range(NT):
                n = ROWS[i]
                act.wait_ge(S("tk_mm"), i + 1)
                o = 1024 * (i % 2)
                af(MX[:, 0:6, P * i:P * i + n], ps[:, o:o + 6 * n].rearrange("p (h n) -> p h n", h=6), ACT.Copy) \
                    .then_inc(S("tk_cp"), 1)
            mem_prompt(0)
            mem_sample(0)
            norm_and_columns(0)
            routing(0)
            experts(0)

            deviation(1, 0)
            round_chunk(CH_S)
            cols_rounded(2, 0)
            deviation(1, 1)
            for j in range(20, 45):
                n, i = ROWS[j % 5], j % 5
                if j < 24:
                    cols_rounded(2, i + 1)
                    if i + 2 < NT:
                        deviation(1, i + 2)
                act.wait_ge(S("tm_mm"), j + 1)
                c = 384 * ((j // 5) % 2)
                if j < 40:
                    dst = (k_rows if j < 30 else V)[0:n, i, c:c + 384]
                    af(dst, bank(4 + j % 4, 0, 384, rows=(0, n)), ACT.Copy).then_inc(S("tm_ev"), 1)
                else:
                    af(fz[0:n, i, :], bank(4 + j % 4, 0, FH, rows=(0, n)), ACT.Copy).then_inc(S("tm_ev"), 1)
                if j in (22, 26, 31, 36, 41):
                    round_chunk(CH_S + 1 + (j - 20) // 5)
            for i in range(NT):
                n = ROWS[i]
                act.wait_ge(S("tk_mm"), NT + i + 1)
                o = 1024 * (i % 2)
                af(kT[:, :, P * i:P * i + n], ps[:, o:o + 6 * n].rearrange("p (h n) -> p h n", h=6), ACT.Copy) \
                    .then_inc(S("tk_cp"), 1)
            for n in range(2, 10):
                if n == 8:
                    act.wait_ge(S("fm_mm"), 10)
                queries(n, qT[:, n - 2, :] if n < 8 else mqT[:, n - 8, :], FD ** -0.5)
                if n in (2, 5):
                    round_chunk(CH_B + 1 + (n - 2) // 3)
            act.wait_ge(S("f_step"), 1)
            af(fe, fe, ACT.Exp, scale=-1.0).then_inc(S("f_step"), 1)
            act.wait_ge(S("f_step"), 3)
            af(fe, fe, ACT.Ln).then_inc(S("f_step"), 1)

            def keys_sum(h):
                act.wait_ge(S("fnb"), h + 1)
                if h >= 2:
                    act.wait_ge(S("fp_s"), 3 * (h - 1))
                af(fnb[:, h % 2, :], bank(3), ACT.Copy).then_inc(S("fnb_cp"), 1)

            act.wait_ge(S("x_ready"), 2 * NT)
            act.wait_ge(S("kv_out"), 64)
            keys_sum(0)
            keys_sum(1)
            for h in range(FH):
                act.wait_ge(S("fp_m"), h + 1)
                if h >= 2:
                    act.wait_ge(S("fp_ev"), h - 1)
                for i in (3, 2, 0, 1):
                    row = fpr[h % 2][:, i, 0:P * (i + 1)]
                    af(row, row, ACT.Exp, bias=nmx2[:, h % 2, i:i + 1],
                       accum_out=esum2[:, h % 2, i:i + 1]).then_inc(S("fp_e"), 1)
                for n in range(3):
                    act.wait_ge(S("fp_t"), 3 * h + n + 1)
                    if n == 0 and h >= 2:
                        act.wait_ge(S("fox_p"), h - 1)
                    w = 4 * P if n < 2 else 2 * P
                    af(fprT[:, h % 2, 4 * P * n:4 * P * n + w], bank(4 + n, 0, w), ACT.Copy).then_inc(S("fp_c"), 1)
                if h + 2 < FH:
                    keys_sum(h + 2)
            for n in range(DB * PG):
                act.wait_ge(S("fk_tr"), n + 1)
                if n >= 2:
                    act.wait_ge(S("fs_l"), n - 1)
                af(fkT[n % 2][:, 0:4, :], bank(4 + 2 * (n % 2)).rearrange("p (h t) -> p h t", h=4), ACT.Copy) \
                    .then_inc(S("fk_cp"), 1)
            for i in range(ST):
                act.wait_ge(S("tk_mm"), 2 * NT + i + 1)
                o = 2048 + 1024 * (i % 2)
                af(MX[:, 0:6, P * i:P * i + P], ps[:, o:o + 6 * P].rearrange("p (h n) -> p h n", h=6), ACT.Copy) \
                    .then_inc(S("tk_cp"), 1)
            act.wait_ge(S("fs_m"), 1)
            for q in range(GR):
                last = af(fl_r[:, q, :], bank(q, 0, FLW), ACT.Exp, bias=nmx[:, q:q + 1], accum_out=esum[:, q:q + 1])
            last.then_inc(S("fs_e"), 1)

            def rows_turned(q):
                af(fs_p[:, q, 0:PG, :], bank(4 + q, 0, PG * P).rearrange("p (g t) -> p g t", g=PG), ACT.Copy)
                return af(fs_p[0:NS, q, PG, :], bank(4 + q, PG * P, PG * P + P, rows=(0, NS)), ACT.Copy)

            for q in (0, 2):
                act.wait_ge(S("fs_t"), q + 1)
                rows_turned(q).then_inc(S("fs_c"), 1)
            act.wait_ge(S("fs_o"), 1)
            for q in range(GR):
                for r in range(2):
                    rr = (64 * r, 64 * r + 64)
                    src = bank(4, P * q, P * q + P, rows=rr).rearrange("p (b a c) -> p a b c", b=2, a=8)
                    last = af(MX[rr[0]:rr[1], 0:6, SEQ + 2 * DS * q:SEQ + 2 * DS * q + 2 * DS]
                              .rearrange("p a (b t) -> p a b t", t=DS), src[:, 0:6, :, DS * r:DS * r + DS], ACT.Copy)
            last.then_inc(S("fs_ev"), 1)
            mem_prompt(1)
            mem_sample(1)
            norm_and_columns(2)
            routing(1)
            experts(1)
            norm_and_columns(3, columns=False)

        @block.vector
        def _(dve):
            v = nc.vector
            count = [0]

            def link(ins):
                count[0] += 1
                ins.then_inc(S("dve_c"), 1)
                dve.wait_ge(S("dve_c"), count[0])

            def bc(ap, shape):
                return ap.broadcast_to(shape)

            def mem_queries(l):
                dve.wait_ge(S("fm_ev"), 2 if l == 0 else 10)
                if l:
                    dve.wait_ge(S("ms_l"), DB)
                link(v.memset(qmb, 0.0))
                for h in range(MH):
                    f = slice(64 * (h % 2), 64 * (h % 2) + 64)
                    last = v.tensor_copy(qmb[f, h // 2, 0:16 * DB].rearrange("p (b c) -> p b c", b=DB)
                                         [:, :, DS * h:DS * h + DS],
                                         mqT[f, h // 2, SEQ:TOK].rearrange("p (b t) -> p b t", b=DB))
                last.then_inc(S("qmb"), 1)

            def mem_prompt(l):
                n0 = ST * l

                def top(i):
                    dve.wait_ge(S("mp_l"), n0 + i + 1)
                    link(v.tensor_reduce(mx2[:, i % 2, :], ps[:, 1024 * (i % 2):1024 * (i % 2) + MH * ML]
                                         .rearrange("p (q t) -> p q t", q=MH), AX.X, ALU.max))
                    v.tensor_scalar(nmx2[:, i % 2, :], mx2[:, i % 2, :], -1.0, None, ALU.mult).then_inc(S("mp_m"), 1)

                def copy(i):
                    dve.wait_ge(S("mp_t"), 2 * (n0 + i) + 2)
                    if n0 + i:
                        dve.wait_ge(S("mp_o"), n0 + i)
                    v.tensor_copy(mprT[:, 4:8, :], bank(5).rearrange("p (n t) -> p n t", n=4)) \
                        .then_inc(S("mp_c2"), 1)

                def scale(i):
                    dve.wait_ge(S("mp_e"), n0 + i + 1)
                    link(v.reciprocal(rsum2[:, i % 2, :], esum2[:, i % 2, :]))
                    v.tensor_tensor(mpr[:, i % 2], mpr[:, i % 2], bc(rsum2[:, i % 2, :].unsqueeze(2), [P, MH, ML]),
                                    ALU.mult).then_inc(S("mp_n"), 1)

                for s in range(ST + 2):
                    if s < ST:
                        top(s)
                    if 1 <= s <= ST:
                        scale(s - 1)
                        copy(s - 1)
                    if s >= 4:
                        weights_remainder(l, *((0, 2), (2, 5))[s - 4])

            def mem_sample(l):
                dve.wait_ge(S("ms_l"), DB * (l + 1))
                link(v.tensor_reduce(mx[:, 0:2], ps[:, 0:1024].rearrange("p (g t) -> p g t", g=2)[:, :, 0:ML],
                                     AX.X, ALU.max))
                v.tensor_scalar(nmx[:, 0:2], mx[:, 0:2], -1.0, None, ALU.mult).then_inc(S("ms_m"), 1)
                dve.wait_ge(S("ms_e"), l + 1)
                link(v.reciprocal(rsum[:, 0:2], esum[:, 0:2]))
                mix_remainder(l, 0)
                mix_remainder(l, 1)
                dve.wait_ge(S("ms_o"), l + 1)
                link(v.tensor_tensor(mhead, bank(3).rearrange("p (n d) -> p n d", d=MD),
                                     bc(C("mem_head").unsqueeze(2), [P, 2 * MH, MD]), ALU.mult))
                for g in range(2):
                    last = v.tensor_reduce(mres[:, g, 0, :], mhead[:, MH * g:MH * g + MH].rearrange("p h d -> p d h"),
                                           AX.X, ALU.add)
                link(last)
                link(v.tensor_tensor(mres[:, :, 1, :], mres[:, :, 0, :], bc(rsum[:, 0:2].unsqueeze(2), [P, 2, MD]),
                                     ALU.mult))
                v.tensor_copy(mres[:, :, 0, :], mres[:, :, 1, :]).then_inc(S("ms_n"), 1)

            def cols_remainder(p, i):
                n = ROWS[i]
                for half in range(2):
                    j = 2 * i + half
                    dve.wait_ge(S("xt_r"), 10 * (p // 2) + j + 1)
                    c = (slice(0, P), slice(4 * half, 4 * half + 4), slice(P * i, P * i + n))
                    v.tensor_tensor(XT_lo[c], bank(j % 2, 0, 4 * n).rearrange("p (k n) -> p k n", k=4), XT_r[c],
                                    ALU.subtract).then_inc(S("xt_cp"), 1)

            def split_chunk(m):
                for half in range(2):
                    dve.wait_ge(S("w_r"), 2 * m + half + 1)
                    k = slice(4 * half, 4 * half + 4)
                    v.tensor_tensor(w_lo(m)[:, k, :], w_raw(m)[:, k, :], w_r(m)[:, k, :], ALU.subtract) \
                        .then_inc(S("w_lo"), 1)

            def weights_remainder(l, k0, k1):
                for k in range(k0, k1):
                    dve.wait_ge(S("wo_r"), KD * l + k + 1)
                    v.tensor_tensor(wo_lo[:, k, :], wo_v[:, k, :], wo_r[:, k, :], ALU.subtract).then_inc(S("wo_lo"), 1)

            def mix_remainder(l, i):
                dve.wait_ge(S("mix_r"), NT * l + i + 1)
                c = slice(P * i, P * i + ROWS[i])
                v.tensor_tensor(MX_lo[:, :, c], MX[:, :, c], mix_r[i % 2][:, :, 0:ROWS[i]], ALU.subtract).then_inc(S("mix_lo"), 1)

            def norm_tile(p, i):
                n = ROWS[i]
                if i == 0:
                    dve.wait_ge(S("ln_in"), 32 * (p + 1))
                for half in range(2):
                    ins = v.bn_stats(stats[0:n, i, 6 * half:6 * half + 6], X[0:n, i, 512 * half:512 * half + 512])
                link(ins)
                v.bn_aggr(mv[0:n, i, :], stats[0:n, i, :]).then_inc(S("ln_st"), 1)
                dve.wait_ge(S("ln_st"), NT * p + i + 1)
                link(v.scalar_tensor_tensor(X[0:n, i], X[0:n, i], mv[0:n, i, 0:1], ln_t[0:n, 0:D], ALU.subtract,
                                            ALU.mult))
                dve.wait_ge(S("ln_sd"), NT * p + i + 1)
                link(v.reciprocal(rstd[:, i:i + 1], rstd[:, i:i + 1]))
                v.scalar_tensor_tensor(X[0:n, i], X[0:n, i], rstd[0:n, i:i + 1], ln_t[0:n, D:], ALU.mult,
                                       ALU.add).then_inc(S("x_ready"), 1)

            def residual_tile(l, i):
                n = ROWS[i]
                for half in range(2):
                    j = 10 * l + 2 * i + half
                    dve.wait_ge(S("wo_mm"), j + 1)
                    xc = X[0:n, i, 512 * half:512 * half + 512]
                    v.scalar_tensor_tensor(xc, xc, ALPHA, bank(4 + j % 4, rows=(0, n)), ALU.mult,
                                           ALU.add).then_inc(S("wo_ev"), 1)
                dve.wait_ge(S("wo_ev"), 10 * l + 2 * i + 2)

            iota = C("iota")
            giv = gi.rearrange("p (i q) -> p i q", q=8)
            e4 = esw.rearrange("p (i g e) -> p i g e", i=NT, g=NG)

            def route_tile(l, i):
                n = ROWS[i]
                if i == 0:
                    v.memset(rl, 0.0)
                    v.memset(cnt, 0.0)
                    for k in range(2):
                        link(v.memset(sums[k], 0.0))
                    link(v.memset(rl[:, :, 4:8], NEG))
                b = bank(2 + (NT * l + i) % 2, 0, NG + NE, rows=(0, n))
                dve.wait_ge(S("rt_mm"), NT * l + i + 1)
                v.tensor_tensor(rl[0:n, i, 0:NG], b[:, 0:NG], biasr[0:n, 0:NG], ALU.add)
                v.tensor_tensor(rl[0:n, i, 8:], b[:, NG:], biasr[0:n, NG:], ALU.add).then_inc(S("rt_ev"), 1)
                dve.wait_ge(S("rt_ev"), NT * l + i + 1)
                link(v.max(gm[:, i, :], rl[:, i, 0:8]))
                link(v.max_index(gi[:, 8 * i:8 * i + 8], gm[:, i, :], rl[:, i, 0:8]))
                link(v.tensor_copy(gf[:, i:i + 1], giv[:, i, 0:1]))
                link(v.tensor_tensor(ohg[:, i, :], iota[:, 0:NG], bc(gf[:, i:i + 1], [P, NG]), ALU.is_equal))
                link(v.tensor_tensor(e4[:, i], rl[:, i, 8:].rearrange("p (g e) -> p g e", g=NG),
                                     bc(ohg[:, i, :].unsqueeze(2), [P, NG, EG]), ALU.mult))
                link(v.tensor_reduce(esel[:, i, :], e4[:, i].rearrange("p g e -> p e g"), AX.X, ALU.add))
                link(v.max(em[:, i, :], esel[:, i, :]))
                link(v.max_index(gi[:, 40 + 8 * i:48 + 8 * i], em[:, i, :], esel[:, i, :]))

            def attention_to_routes(l):
                for i in range(NT + 1):
                    if i < NT:
                        residual_tile(l, i)
                        if i + 2 < NT:
                            mix_remainder(l, i + 2)
                        norm_tile(2 * l, i)
                    if i:
                        route_tile(l, i - 1)
                routing(l)

            def routing(l):
                for j in range(2):
                    last = v.tensor_copy(ef[:, j, :], giv[:, NT:2 * NT, j])
                link(last)
                for j in range(2):
                    last = v.scalar_tensor_tensor(ef[:, j, :], gf, float(EG), ef[:, j, :], ALU.mult, ALU.add)
                link(last)
                link(v.scalar_tensor_tensor(ef, ef, 1.0, bc(C("valid").unsqueeze(1), [P, 2, NT]), ALU.add, ALU.mult))
                oh4 = oh.rearrange("p (j i) e -> p j i e", j=2)
                link(v.tensor_tensor(oh, bc(iota[:, 1:NE + 1].unsqueeze(1), [P, 10, NE]),
                                     bc(ef.rearrange("p j i -> p (j i)").unsqueeze(2), [P, 10, NE]), ALU.is_equal))
                v.tensor_tensor(cnt[:, 0:NT], oh4[:, 0], oh4[:, 1], ALU.add).then_inc(S("onehot"), 1)
                v.tensor_tensor(gexp, rl[:, :, 0:NG], bc(gm[:, :, 0:1], [P, NT, NG]), ALU.subtract) \
                    .then_inc(S("r_step"), 1)
                dve.wait_ge(S("r_step"), 4 * l + 2)
                link(v.tensor_reduce(gw, gexp, AX.X, ALU.add))
                link(v.reciprocal(gw, gw))
                v.tensor_tensor(tmpw, em[:, :, 1], em[:, :, 0], ALU.subtract).then_inc(S("r_step"), 1)
                dve.wait_ge(S("r_step"), 4 * l + 4)
                link(v.tensor_scalar(wj[:, 0, :], tmpw, 1.0, None, ALU.add))
                link(v.reciprocal(wj[:, 0, :], wj[:, 0, :]))
                link(v.tensor_tensor(wj[:, 0, :], wj[:, 0, :], gw, ALU.mult))
                link(v.tensor_tensor(wj[:, 1, :], wj[:, 0, :], tmpw, ALU.mult))
                link(v.tensor_tensor(wj, wj, bc(C("valid").unsqueeze(1), [P, 2, NT]), ALU.mult))
                dve.wait_ge(S("rank_mm"), l + 1)
                rank = bank(4, 0, NE * (NT + 1)).rearrange("p (i e) -> p i e", e=NE)
                n4 = nxc.rearrange("p (e k) -> p e k", k=4)
                link(v.tensor_tensor(n4, bc(rank[:, NT, :].unsqueeze(2), [P, NE, 4]),
                                     bc(C("steps").unsqueeze(1), [P, NE, 4]), ALU.is_gt))
                link(v.tensor_reduce(sums[0][:, 16:], n4, AX.X, ALU.add))
                for k in range(5):
                    a, b = sums[k % 2], sums[(k + 1) % 2]
                    link(v.tensor_tensor(b[:, 16:], a[:, 16:], a[:, 16 - 2 ** k:48 - 2 ** k], ALU.add))
                total = sums[1]
                link(v.tensor_scalar(further, total[:, 15:47], float(P), float(PAIRS * P - SLOTS), ALU.mult, ALU.add))
                link(v.scalar_tensor_tensor(further, iota[:, 0:NE], -float(SLOTS), further, ALU.mult, ALU.add))
                link(v.scalar_tensor_tensor(place, rank[:, 0:NT], float(SLOTS), bc(further.unsqueeze(1), [P, NT, NE]),
                                            ALU.is_ge, ALU.mult))
                link(v.tensor_tensor(place, place, rank[:, 0:NT], ALU.add))
                link(v.scalar_tensor_tensor(place, bc(iota[:, 0:NE].unsqueeze(1), [P, NT, NE]), float(SLOTS), place,
                                            ALU.mult, ALU.add))
                th4 = oh_t.rearrange("p (j i) e -> p j i e", j=2)
                for j in range(2):
                    last = v.tensor_tensor(th4[:, j], oh4[:, j], place, ALU.mult)
                link(last)
                link(v.tensor_reduce(p10, oh_t, AX.X, ALU.add))
                link(v.tensor_copy(pos_i, p10))
                v.tensor_scalar(ib[0], pos_i, P - 1, None, ALU.bitwise_and)
                link(v.tensor_scalar(ib[1], pos_i, 7, None, ALU.logical_shift_right))
                v.tensor_copy(s10, ib[0])
                link(v.tensor_copy(b10, ib[1]))
                v.tensor_tensor(a1, bc(iota.unsqueeze(1), [P, 10, P]), bc(s10.unsqueeze(2), [P, 10, P]), ALU.is_equal)
                link(v.tensor_tensor(bt, bc(iota[:, 0:NE].unsqueeze(1), [P, 10, NE]),
                                     bc(b10.unsqueeze(2), [P, 10, NE]), ALU.is_equal))
                v.tensor_tensor(bb[:, :, 0:NE], bt, bc(C("token").unsqueeze(2), [P, 10, NE]), ALU.mult)
                v.tensor_tensor(bb[:, :, NE:], bt, bc(wj.rearrange("p j i -> p (j i)").unsqueeze(2), [P, 10, NE]),
                                ALU.mult).then_inc(S("places"), 1)
                link(v.tensor_tensor(before, bc(total[:, 16:].unsqueeze(1), [P, MORE, NE]),
                                     bc(iota[:, 0:MORE].unsqueeze(2), [P, MORE, NE]), ALU.is_le))
                link(v.tensor_reduce(lf[:, 0:MORE], before, AX.X, ALU.add))
                link(v.tensor_scalar(lf[:, 0:MORE], lf[:, 0:MORE], float(NE - 1), None, ALU.min))
                link(v.tensor_copy(lf[:, MORE:], total[:, 47:48]))
                v.tensor_copy(lists, lf).then_inc(S("lists"), 1)
                dve.wait_ge(S("slot_mm"), l + 1)
                link(v.tensor_copy(wslot, bank(5, NE, 2 * NE)))
                dve.wait_ge(S("lists"), l + 1)
                v.tensor_copy(slot_tok, bank(5, 0, NE)).then_inc(S("slots"), 1)

            def experts(l):
                s = l * PAIRS
                with dve.Fori(0, PAIRS) as i:
                    for j in range(2):
                        dve.wait_ge(S("gate"), i * 2 + (2 * s + j + 1))
                        v.tensor_tensor(hid[:, j].rearrange("p f n -> p (f n)"), bank(j, 2 * SLOTS, 4 * SLOTS),
                                        sg[:, j, :], ALU.mult).then_inc(S("hid"), 1)
                more = dve.value_load(lists[0:1, 16:17], min_val=0, max_val=MORE)
                with dve.If(more > 0):
                    with dve.Fori(0, more) as x:
                        dve.wait_ge(S(f"more_step{l}"), x * 9 + 6)
                        v.tensor_tensor(hidx.rearrange("p f n -> p (f n)"), bank(0, 2 * P, 4 * P),
                                        sgx.rearrange("p f n -> p (f n)"), ALU.mult).then_inc(S(f"more_step{l}"), 1)

            def combine(l):
                for i in range(NT):
                    if l == 0 and i >= 2:
                        cols_remainder(2, i - 2)
                    n = ROWS[i]
                    dve.wait_ge(S("yg_sum"), NT * l + i + 1)
                    v.scalar_tensor_tensor(X[0:n, i], X[0:n, i], ALPHA, yg[i % 2][0:n, 0], ALU.mult, ALU.add) \
                        .then_inc(S("yg_used"), 1)
                    dve.wait_ge(S("yg_used"), NT * l + i + 1)
                    norm_tile(2 * l + 1, i)
                    if l == 0 and i in (0, 4):
                        split_chunk(CH_S + i // 4)

            v.memset(eps_ln, LN_EPS)
            v.memset(eps_hn, HN_EPS)
            v.memset(hmv, 1.0)
            v.memset(mv, 1.0)
            v.memset(hrs, 1.0)
            v.memset(ints[:, 16:], 0)
            link(v.memset(fz, 0.0))
            for i in range(NT):
                cols_remainder(0, i)
            dve.wait_ge(S("tables"), 64)
            split_chunk(0)
            split_chunk(1)
            for h in range(2 * RH):
                t = 2 * (h // RH)
                src = ps[:, 1024 * (h % 2) + FM0:1024 * (h % 2) + FM0 + TOK]
                dve.wait_ge(S("rope_mm"), h + 1)
                v.tensor_tensor(ropeA, src, rope_v[:, t, :], ALU.mult)
                v.tensor_tensor(ropeB[0:64], src[64:128], rope_v[64:128, t + 1, :], ALU.mult)
                link(v.tensor_tensor(ropeB[64:128], src[0:64], rope_v[0:64, t + 1, :], ALU.mult))
                ins = v.tensor_tensor((qT if h < RH else kT)[:, h % RH, :], ropeA, ropeB, ALU.add)
                ins.then_inc(S("rope_ev"), 1)
                dve.wait_ge(S("rope_ev"), h + 1)
                if h in (3, 6, 9):
                    split_chunk(1 + h // 3)
            for m in range(5, CH_S):
                split_chunk(m)
            lg = np.log(np.float32(1) - np.float32(2) ** (np.float32(-5) - np.arange(RH, dtype=np.float32)))
            g_chunk = [float(x) for x in np.exp(lg.astype(np.float32) * np.float32(P))]
            g_step = [float(x) for x in np.exp(lg.astype(np.float32) * np.float32(DS))]

            def decayed(n):
                if n >= 2:
                    dve.wait_ge(S("rr"), 2 * (n - 1))
                if n:
                    v.tensor_tensor(qd[n % 2], qT[:, :, P * n:P * n + P],
                                    C("qdecay").rearrange("p (h t) -> p h t", h=RH), ALU.mult)
                for j in range(2):
                    dve.wait_ge(S("rsc"), 2 * n + j + 1)
                    v.tensor_tensor(scm[n % 2][:, 3 * j:3 * j + 3].rearrange("p h t -> p (h t)"), bank(j, 0, 384),
                                    C("decay")[:, 384 * j:384 * j + 384], ALU.mult).then_inc(S("rsm"), 1)

            def norm_and_gate(n, rows, heads, count):
                dve.wait_ge(S("rcp"), count)
                for h in heads:
                    last = v.bn_stats(hstats[0:rows, h, :], R[0:rows, n, P * h:P * h + P])
                link(last)
                for h in heads:
                    last = v.bn_aggr(hmv[0:rows, RH * n + h, :], hstats[0:rows, h, :])
                link(last)
                for h in heads:
                    r = R[0:rows, n, P * h:P * h + P]
                    last = v.scalar_tensor_tensor(r, r, hmv[0:rows, RH * n + h, 0:1], G[0:rows, n, P * h:P * h + P],
                                                  ALU.subtract, ALU.mult)
                return last

            def state_update(n):
                for j in range(2):
                    dve.wait_ge(S("rkv"), 2 * n + j + 1)
                    if n == 0:
                        v.tensor_copy(state_p[:, 3 * j:3 * j + 3].rearrange("p h e -> p (h e)"),
                                      bank(6 + j, 0, 384)).then_inc(S("rst"), 1)
                        continue
                    for h in range(3 * j, 3 * j + 3):
                        last = v.scalar_tensor_tensor(state_p[:, h, :], state_p[:, h, :], g_chunk[h],
                                                      bank(6 + j, P * (h % 3), P * (h % 3) + P), ALU.mult, ALU.add)
                    last.then_inc(S("rst"), 1)

            def sample_parts(h):
                b = h % 2
                if h >= 2:
                    dve.wait_ge(S("rr"), 2 * ST + h - 1)
                link(v.tensor_tensor(qds[:, b, :], qT[:, h, SEQ:TOK], C("qdecay_s")[:, NS * h:NS * h + NS], ALU.mult))
                v.tensor_tensor(qbs[:, b], bc(qds[:, b, :].unsqueeze(1), [P, DB, NS]),
                                C("block_s").rearrange("p (b t) -> p b t", b=DB), ALU.mult)
                dve.wait_ge(S("rsc"), 2 * ST + h + 1)
                v.tensor_tensor(scs[0:NS, b, :], bank(b, 0, NS, rows=(0, NS)),
                                C("decay_s", NS)[:, NS * h:NS * h + NS], ALU.mult)
                if h >= 2:
                    dve.wait_ge(S("rkv"), 2 * ST + h - 1)
                v.tensor_tensor(vbd[b][0:NS].rearrange("p (b e) -> p b e", b=DB),
                                bc(V[0:NS, ST, P * h:P * h + P].unsqueeze(1), [NS, DB, P]),
                                bc(C("kdecay_s", NS)[:, DB * h:DB * h + DB].unsqueeze(2), [NS, DB, P]), ALU.mult) \
                    .then_inc(S("rsm"), 1)

            dve.wait_ge(S("zero_out"), 16 * MORE)
            decayed(0)
            for n in range(ST):
                if n + 1 < ST:
                    decayed(n + 1)
                else:
                    sample_parts(0)
                    sample_parts(1)
                state_update(n)
                link(norm_and_gate(n, P, range(RH), 2 * n + 2))
            for h in range(RH):
                if 2 <= h + 1 < RH:
                    sample_parts(h + 1)
                dve.wait_ge(S("rkv"), 2 * ST + h + 1)
                v.scalar_tensor_tensor(st_s[:, h % 3, :], st_s[:, h % 3, :], g_step[h], ps[:, 3072:4096], ALU.mult,
                                       ALU.add).then_inc(S("rst"), 1)
            norm_and_gate(ST, NS, range(RH), 2 * ST + RH).then_inc(S("head_sd"), 1)
            dve.wait_ge(S("head_sd"), 2)
            link(v.reciprocal(hrs, hrs))
            for i in range(NT):
                n = ROWS[i]
                r = R[0:n, i].rearrange("p (h e) -> p h e", h=RH)
                v.tensor_tensor(r, r, bc(hrs[0:n, RH * i:RH * i + RH].unsqueeze(2), [n, RH, P]), ALU.mult) \
                    .then_inc(S("gated"), 1)
            mem_queries(0)
            mem_prompt(0)
            weights_remainder(0, 5, KD)
            mem_sample(0)
            attention_to_routes(0)
            experts(0)
            combine(0)

            cols_remainder(2, ST - 1)
            cols_remainder(2, ST)
            for m in range(CH_S + 2, CH_END):
                split_chunk(m)
            dve.wait_ge(S("tm_ev"), 45)
            link(v.tensor_tensor(fz, fz, bc(bf_b.unsqueeze(1), [P, NT, FH]), ALU.add))
            link(v.tensor_scalar(fe, fz, -1.0, None, ALU.mult))
            v.tensor_tensor(fe, fe, fz, ALU.max).then_inc(S("f_step"), 1)
            dve.wait_ge(S("f_step"), 2)
            v.tensor_scalar(fe, fe, 1.0, None, ALU.add).then_inc(S("f_step"), 1)
            dve.wait_ge(S("f_step"), 4)
            v.scalar_tensor_tensor(logf, fz, 0.0, fe, ALU.min, ALU.subtract).then_inc(S("logf"), 1)
            dve.wait_ge(S("cum"), 1)
            v.tensor_copy(cq[:, 0:ST, :], bank(4, 0, FH * ST).rearrange("p (i h) -> p i h", i=ST))
            link(v.tensor_copy(cq[0:NS, ST, :], bank(4, FH * ST, FH * NT, rows=(0, NS))))
            v.tensor_scalar(negc[:, 0:ST, :], cq[:, 0:ST, :], -1.0, None, ALU.mult)
            v.tensor_scalar(negc[0:NS, ST, :], cq[0:NS, ST, :], -1.0, None, ALU.mult)
            v.tensor_scalar(negp.rearrange("p g c -> p (g c)"), bank(5, 0, PG * DB * FH), -1.0, None, ALU.mult) \
                .then_inc(S("cum_ev"), 1)

            def prompt_top(h):
                rows = fpr[h % 2]
                dve.wait_ge(S("fnb_cp"), h + 1)
                if h >= 2:
                    dve.wait_ge(S("fp_t"), 3 * (h - 1))
                for n, tiles in enumerate(((1,), (0, 2), (3,))):
                    dve.wait_ge(S("fp_l"), 3 * h + n + 1)
                    for i in tiles:
                        w = P * (i + 1)
                        b, o = LOGIT_AT[i]
                        last = v.scalar_tensor_tensor(rows[:, i, 0:w], bank(b, o, o + w), cq[:, i, h:h + 1],
                                                      fnb[:, h % 2, 0:w], ALU.add, ALU.add)
                    last.then_inc(S("fp_s"), 1)
                dve.wait_ge(S("fp_s"), 3 * h + 3)
                link(v.tensor_tensor(fdiag[h % 2], fdiag[h % 2], bc(C("causal").unsqueeze(1), [P, ST, P]), ALU.add))
                for i in range(ST):
                    last = v.tensor_reduce(mx2[:, h % 2, i:i + 1], rows[:, i, 0:P * (i + 1)], AX.X, ALU.max)
                link(last)
                v.tensor_scalar(nmx2[:, h % 2, :], mx2[:, h % 2, :], -1.0, None, ALU.mult).then_inc(S("fp_m"), 1)

            def prompt_result(h):
                dve.wait_ge(S("fp_e"), 4 * h + 4)
                link(v.reciprocal(rsum2[:, h % 2, :], esum2[:, h % 2, :]))
                dve.wait_ge(S("fox_p"), h + 1)
                v.tensor_tensor(o_rows[:, :, FD * h:FD * h + FD], bank(7, 0, ST * FD).rearrange("p (i d) -> p i d", i=ST),
                                bc(rsum2[:, h % 2, :].unsqueeze(2), [P, ST, FD]), ALU.mult).then_inc(S("fp_ev"), 1)

            dve.wait_ge(S("kv_out"), 64)
            for s in range(FH + 2):
                if s < FH:
                    prompt_top(s)
                if s >= 2:
                    prompt_result(s - 2)
            for n in range(DB * PG):
                dve.wait_ge(S("fk_tr"), n + 1)
                if n >= 2:
                    dve.wait_ge(S("fs_l"), n - 1)
                v.tensor_copy(fkT[n % 2][:, 4:6, :], bank(5 + 2 * (n % 2), 0, 2 * P).rearrange("p (h t) -> p h t", h=2)) \
                    .then_inc(S("fk_cp2"), 1)
            dve.wait_ge(S("fs_l"), DB * PG)
            link(v.tensor_reduce(mx[:, 0:GR], ps[:, 0:512 * GR].rearrange("p (q t) -> p q t", q=GR)[:, :, 0:FLW], AX.X,
                                 ALU.max))
            v.tensor_scalar(nmx[:, 0:GR], mx[:, 0:GR], -1.0, None, ALU.mult).then_inc(S("fs_m"), 1)
            dve.wait_ge(S("fs_e"), 1)
            link(v.reciprocal(rsum[:, 0:GR], esum[:, 0:GR]))
            for q in (1, 3):
                dve.wait_ge(S("fs_t"), q + 1)
                v.tensor_copy(fs_p[:, q, 0:PG, :], bank(4 + q, 0, PG * P).rearrange("p (g t) -> p g t", g=PG))
                v.tensor_copy(fs_p[0:NS, q, PG, :], bank(4 + q, PG * P, PG * P + P, rows=(0, NS))) \
                    .then_inc(S("fs_c2"), 1)
            for q in range(GR):
                dve.wait_ge(S("fs_pv"), q + 1)
                o = 1024 * (q % 2)
                v.tensor_tensor(fhead, ps[:, o:o + FW].rearrange("p (h d) -> p h d", h=FH),
                                bc(C("fox_head").unsqueeze(2), [P, FH, FD]), ALU.mult).then_inc(S("fs_h"), 1)
                dve.wait_ge(S("fs_h"), q + 1)
                link(v.tensor_reduce(fres[:, q, 0, :], fhead.rearrange("p h d -> p d h"), AX.X, ALU.add))
                link(v.tensor_scalar(fres[:, q, 1, :], fres[:, q, 0, :], rsum[:, q:q + 1], None, ALU.mult))
                v.tensor_copy(fres[:, q, 0, :], fres[:, q, 1, :]).then_inc(S("fs_n"), 1)
                dve.wait_ge(S("fs_n"), q + 1)
            mem_queries(1)
            mem_prompt(1)
            weights_remainder(1, 5, KD)
            mem_sample(1)
            attention_to_routes(1)
            experts(1)
            combine(1)


_INS = ['x_prompt', 'x_sample', 'mem_prompt', 'state_ret', 'cache_fox_k', 'cache_fox_v', 'cache_fox_logf',
        'cache_mem_k', 'cache_mem_v', 'page_table', 'w_in_a', 'w_in_b', 'w_kv_shared', 'b_forget', 'w_o', 'w_mem_kv',
        'ln1_g', 'ln1_b', 'ln2_g', 'ln2_b', 'w_group', 'b_group', 'w_route', 'b_route', 'w_up', 'w_down']
_OUTS = [(1, SEQ, D), (DB, DS, D), (1, 1, RH, RD, RD), (1, DB, RH, RD, RD), (1, SEQ, FH, FD), (1, SEQ, FH, FD),
         (1, SEQ, FH), (DB, DS, FH, FD), (DB, DS, FH, FD), (DB, DS, FH), (LAYERS, 1, ML, MH, MD),
         (LAYERS, 1, ML, MH, MD)]


def kernel(**inputs):
    import concourse.bacc as _bacc
    from concourse.bass_utils import run_bass_kernel_spmd as _run

    nc = _bacc.Bacc("TRN2", target_bir_lowering=False, num_devices=1)
    consts, rope = shape_constants()
    given = [(n, np.ascontiguousarray(inputs[n])) for n in _INS] + [("consts", consts), ("rope", rope)]
    arrays, args = {}, []
    for name, a in given:
        arrays[f"in_{name}_dram"] = a
        args.append(nc.dram_tensor(f"in_{name}_dram", a.shape, mybir.dt.from_np(a.dtype), kind="ExternalInput").ap())
    outs = [nc.dram_tensor(f"out_{i}_dram", s, F32, kind="ExternalOutput").ap() for i, s in enumerate(_OUTS)]
    build(nc, *args, outs)
    r = _run(nc, [arrays], core_ids=[0])
    return tuple(r.results[0][f"out_{i}_dram"] for i in range(len(_OUTS)))
```
